# Optimizing a Trainium2 kernel written in Bass

```python
import jax, jax.numpy as jnp
from jax import lax
import numpy as np

D_MODEL = 1024
BATCH = 1
SEQ = 2048
DEPTH = 1
DEC_BATCH = 8
DEC_SEQ = 8
PAST_LEN = 16384
PAGE_SIZE = 128

D_MIX = D_MODEL
D_POOL = D_MIX // 2
D_LRU = D_MIX - D_POOL
POOL_WINDOWS = (2, 4, 8, 16)
N_POOL_GROUPS = len(POOL_WINDOWS)
POOL_GROUP = D_POOL // N_POOL_GROUPS
POOL_BUF = max(POOL_WINDOWS) - 1
N_LRU_HEADS = 8
LRU_HEAD = D_LRU // N_LRU_HEADS
CONV_W = 4
LRU_C = 8.0
D_IN = D_POOL + 2 * D_LRU
N_EXPERT_GROUPS = 4
EXPERTS_PER_GROUP = 4
N_EXPERTS = N_EXPERT_GROUPS * EXPERTS_PER_GROUP
TOP_K = 2
D_EXPERT = D_MODEL // 4
ALPHA = (2.0 * DEPTH) ** 0.25
BETA = (8.0 * DEPTH) ** -0.25
LN_EPS = 1e-5

kernel_name = 'hymba_pool_rglru_hmoe_deepnorm_step'

def _layer_norm(x, g, b):
    x32 = x.astype(jnp.float32)
    mu = jnp.mean(x32, -1, keepdims=True)
    var = jnp.mean(jnp.square(x32 - mu), -1, keepdims=True)
    y = (x32 - mu) * lax.rsqrt(var + LN_EPS) * g.astype(jnp.float32) + b.astype(jnp.float32)
    return y.astype(x.dtype)

def _pool_mixer(p, buf, n_prev, w_pool, pool_scale):
    bsz, t_len, _ = p.shape
    z = jnp.concatenate([buf.astype(p.dtype), p], axis=1)
    z32 = z.astype(jnp.float32)
    cs = jnp.concatenate([jnp.zeros_like(z32[:, :1]), jnp.cumsum(z32, axis=1)], axis=1)
    pos = jnp.arange(t_len, dtype=jnp.float32)
    pooled = []
    for g, w in enumerate(POOL_WINDOWS):
        ch = slice(g * POOL_GROUP, (g + 1) * POOL_GROUP)
        hi = cs[:, POOL_BUF + 1:POOL_BUF + 1 + t_len, ch]
        lo = cs[:, POOL_BUF + 1 - w:POOL_BUF + 1 - w + t_len, ch]
        cnt = jnp.minimum(jnp.float32(w), pos + jnp.float32(1 + n_prev))
        pooled.append((hi - lo) / cnt[None, :, None])
    d = jnp.concatenate(pooled, -1) - p.astype(jnp.float32)
    d = d.astype(p.dtype).reshape(bsz, t_len, N_POOL_GROUPS, POOL_GROUP)
    y = jnp.einsum('btgc,gcd->btgd', d, w_pool).reshape(bsz, t_len, D_POOL) * pool_scale
    return y, z[:, -POOL_BUF:]

def _causal_conv(xr, buf, w_conv, b_conv):
    t_len = xr.shape[1]
    z = jnp.concatenate([buf.astype(xr.dtype), xr], axis=1)
    y = b_conv + z[:, 0:t_len] * w_conv[0]
    for k in range(1, CONV_W):
        y = y + z[:, k:k + t_len] * w_conv[k]
    return y, z[:, -(CONV_W - 1):]

def _lin_combine(left, right):
    a_l, b_l = left
    a_r, b_r = right
    return a_l * a_r, a_r * b_l + b_r

def _rg_lru(xc, h0, w_a, b_a, w_x, b_x, lam):
    bsz, t_len, _ = xc.shape
    xh = xc.reshape(bsz, t_len, N_LRU_HEADS, LRU_HEAD)
    r = jax.nn.sigmoid((jnp.einsum('bthi,hij->bthj', xh, w_a).reshape(bsz, t_len, D_LRU) + b_a).astype(jnp.float32))
    i = jax.nn.sigmoid((jnp.einsum('bthi,hij->bthj', xh, w_x).reshape(bsz, t_len, D_LRU) + b_x).astype(jnp.float32))
    log_a = -LRU_C * r * jax.nn.softplus(-lam.astype(jnp.float32))
    a = jnp.exp(log_a)
    mult = jnp.sqrt(jnp.maximum(-jnp.expm1(2.0 * log_a), 0.0))
    b = mult * i * xc.astype(jnp.float32)
    a_cum, h_zero = lax.associative_scan(_lin_combine, (a, b), axis=1)
    h = a_cum * h0.astype(jnp.float32)[:, None, :] + h_zero
    return h.astype(xc.dtype), h[:, -1].astype(h0.dtype)

def _hier_moe(u, w_group, b_group, w_route, b_route, w_gate, w_up, w_down):
    shp = u.shape
    un = u.reshape(-1, D_MODEL)
    n_tok = un.shape[0]
    g_logits = (un @ w_group + b_group).astype(jnp.float32)
    p_group = jax.nn.softmax(g_logits, axis=-1)
    g_sel = jnp.argmax(g_logits, axis=-1)
    e_logits = (un @ w_route + b_route).astype(jnp.float32).reshape(n_tok, N_EXPERT_GROUPS, EXPERTS_PER_GROUP)
    e_sel = jnp.take_along_axis(e_logits, g_sel[:, None, None], axis=1)[:, 0]
    top_v, top_i = lax.top_k(e_sel, TOP_K)
    top_w = jax.nn.softmax(top_v, axis=-1) * jnp.take_along_axis(p_group, g_sel[:, None], axis=1)
    w_in_group = jnp.einsum('nk,nke->ne', top_w, jax.nn.one_hot(top_i, EXPERTS_PER_GROUP, dtype=jnp.float32))
    comb = (jax.nn.one_hot(g_sel, N_EXPERT_GROUPS, dtype=jnp.float32)[:, :, None] * w_in_group[:, None, :])
    comb = comb.reshape(n_tok, N_EXPERTS).astype(u.dtype)
    hg = jnp.einsum('nd,edf->nef', un, w_gate)
    hu = jnp.einsum('nd,edf->nef', un, w_up)
    h = jax.nn.silu(hg) * hu * comb[:, :, None]
    y = jnp.einsum('nef,efd->nd', h, w_down)
    return y.reshape(shp)

def _layer(x, c, pool_buf, n_prev, conv_buf, h0,
           w_ada, b_ada, w_in, w_pool, pool_scale, w_conv, b_conv, w_a, b_a, w_x, b_x, lam,
           w_out, ln1_g, ln1_b, w_group, b_group, w_route, b_route, w_gate, w_up, w_down, ln2_g, ln2_b):
    mod = c @ w_ada + b_ada
    sh1, sc1, g1, sh2, sc2, g2 = jnp.split(mod, 6, axis=-1)
    u = x * (1.0 + sc1[:, None]) + sh1[:, None]
    proj = u @ w_in
    p = proj[..., :D_POOL]
    xr = proj[..., D_POOL:D_POOL + D_LRU]
    gr = proj[..., D_POOL + D_LRU:]
    y_pool, new_pool = _pool_mixer(p, pool_buf, n_prev, w_pool, pool_scale)
    xc, new_conv = _causal_conv(xr, conv_buf, w_conv, b_conv)
    h_seq, h_last = _rg_lru(xc, h0, w_a, b_a, w_x, b_x, lam)
    y_lru = h_seq * jax.nn.gelu(gr)
    mix = jnp.concatenate([y_pool, y_lru], axis=-1) @ w_out
    x = _layer_norm(ALPHA * x + (1.0 + g1[:, None]) * mix, ln1_g, ln1_b)
    u2 = x * (1.0 + sc2[:, None]) + sh2[:, None]
    y_moe = _hier_moe(u2, w_group, b_group, w_route, b_route, w_gate, w_up, w_down)
    x = _layer_norm(ALPHA * x + (1.0 + g2[:, None]) * y_moe, ln2_g, ln2_b)
    return x, new_pool, new_conv, h_last

def setup_inputs(seed: int = 0) -> dict:
    key = jax.random.key(seed)
    ks = jax.random.split(key, 32)

    def nrm(k, shape, scale):
        return jax.random.normal(k, shape, jnp.float32) * scale

    a0 = jax.random.uniform(ks[19], (DEPTH, D_LRU), jnp.float32, 0.9, 0.999)
    return {
        'x_prompt': nrm(ks[0], (BATCH, SEQ, D_MODEL), 1.0),
        'x_sample': nrm(ks[1], (DEC_BATCH, DEC_SEQ, D_MODEL), 1.0),
        'c_prompt': nrm(ks[2], (BATCH, D_MODEL), 1.0),
        'c_sample': nrm(ks[3], (DEC_BATCH, D_MODEL), 1.0),
        'state_pool': nrm(ks[4], (DEPTH, DEC_BATCH, POOL_BUF, D_POOL), 1.0),
        'state_conv': nrm(ks[5], (DEPTH, DEC_BATCH, CONV_W - 1, D_LRU), 1.0),
        'state_lru': nrm(ks[6], (DEPTH, DEC_BATCH, D_LRU), 0.5),
        'w_ada': nrm(ks[7], (DEPTH, D_MODEL, 6 * D_MODEL), 0.1 * D_MODEL ** -0.5),
        'b_ada': nrm(ks[8], (DEPTH, 6 * D_MODEL), 0.01),
        'w_in': nrm(ks[9], (DEPTH, D_MODEL, D_IN), D_MODEL ** -0.5),
        'w_pool': nrm(ks[10], (DEPTH, N_POOL_GROUPS, POOL_GROUP, POOL_GROUP), POOL_GROUP ** -0.5),
        'pool_scale': 1.0 + nrm(ks[11], (DEPTH, D_POOL), 0.1),
        'w_conv': nrm(ks[12], (DEPTH, CONV_W, D_LRU), CONV_W ** -0.5),
        'b_conv': nrm(ks[13], (DEPTH, D_LRU), 0.01),
        'w_a': nrm(ks[14], (DEPTH, N_LRU_HEADS, LRU_HEAD, LRU_HEAD), LRU_HEAD ** -0.5),
        'b_a': nrm(ks[15], (DEPTH, D_LRU), 0.01),
        'w_x': nrm(ks[16], (DEPTH, N_LRU_HEADS, LRU_HEAD, LRU_HEAD), LRU_HEAD ** -0.5),
        'b_x': nrm(ks[17], (DEPTH, D_LRU), 0.01),
        'lru_lambda': jnp.log(a0) - jnp.log1p(-a0),
        'w_out': nrm(ks[18], (DEPTH, D_MIX, D_MODEL), BETA * D_MIX ** -0.5),
        'ln1_g': 1.0 + nrm(ks[20], (DEPTH, D_MODEL), 0.01),
        'ln1_b': nrm(ks[21], (DEPTH, D_MODEL), 0.01),
        'w_group': nrm(ks[22], (DEPTH, D_MODEL, N_EXPERT_GROUPS), D_MODEL ** -0.5),
        'b_group': nrm(ks[23], (DEPTH, N_EXPERT_GROUPS), 0.01),
        'w_route': nrm(ks[24], (DEPTH, D_MODEL, N_EXPERTS), D_MODEL ** -0.5),
        'b_route': nrm(ks[25], (DEPTH, N_EXPERTS), 0.01),
        'w_gate': nrm(ks[26], (DEPTH, N_EXPERTS, D_MODEL, D_EXPERT), D_MODEL ** -0.5),
        'w_up': nrm(ks[27], (DEPTH, N_EXPERTS, D_MODEL, D_EXPERT), D_MODEL ** -0.5),
        'w_down': nrm(ks[28], (DEPTH, N_EXPERTS, D_EXPERT, D_MODEL), BETA * D_EXPERT ** -0.5),
        'ln2_g': 1.0 + nrm(ks[29], (DEPTH, D_MODEL), 0.01),
        'ln2_b': nrm(ks[30], (DEPTH, D_MODEL), 0.01),
    }

def reference(x_prompt, x_sample, c_prompt, c_sample, state_pool, state_conv, state_lru,
              w_ada, b_ada, w_in, w_pool, pool_scale, w_conv, b_conv, w_a, b_a, w_x, b_x, lru_lambda,
              w_out, ln1_g, ln1_b, w_group, b_group, w_route, b_route, w_gate, w_up, w_down, ln2_g, ln2_b):
    n_prev_sample = min(PAST_LEN, POOL_BUF)
    bp = x_prompt.shape[0]
    xp, xs = x_prompt, x_sample
    pool_p, conv_p, lru_p, pool_s, conv_s, lru_s = [], [], [], [], [], []
    for l in range(DEPTH):
        wl = (w_ada[l], b_ada[l], w_in[l], w_pool[l], pool_scale[l], w_conv[l], b_conv[l],
              w_a[l], b_a[l], w_x[l], b_x[l], lru_lambda[l], w_out[l], ln1_g[l], ln1_b[l],
              w_group[l], b_group[l], w_route[l], b_route[l], w_gate[l], w_up[l], w_down[l],
              ln2_g[l], ln2_b[l])
        zero_pool = jnp.zeros((bp, POOL_BUF, D_POOL), x_prompt.dtype)
        zero_conv = jnp.zeros((bp, CONV_W - 1, D_LRU), x_prompt.dtype)
        zero_h = jnp.zeros((bp, D_LRU), state_lru.dtype)
        xp, npl, ncv, nh = _layer(xp, c_prompt, zero_pool, 0, zero_conv, zero_h, *wl)
        pool_p.append(npl); conv_p.append(ncv); lru_p.append(nh)
        xs, npl, ncv, nh = _layer(xs, c_sample, state_pool[l], n_prev_sample, state_conv[l], state_lru[l], *wl)
        pool_s.append(npl); conv_s.append(ncv); lru_s.append(nh)
    return (xp, xs, jnp.stack(pool_p), jnp.stack(conv_p), jnp.stack(lru_p),
            jnp.stack(pool_s), jnp.stack(conv_s), jnp.stack(lru_s))


_drawn_inputs = setup_inputs


def setup_inputs(seed=0):
    import zlib

    import numpy as np

    out = dict(_drawn_inputs(seed))
    spreads = {}
    factors = {'b_a': 8.0,
     'b_x': 8.0,
     'ln1_g': 4.364,
     'ln1_b': 3.05,
     'b_group': 8.0,
     'b_route': 8.0,
     'ln2_g': 5.854,
     'ln2_b': 5.537}
    for name, (base, spread) in spreads.items():
        noise = np.random.default_rng([zlib.crc32(name.encode()), seed]).standard_normal(out[name].shape)
        drawn = base * np.exp(spread * noise) if base else spread * noise
        out[name] = __import__('jax').numpy.asarray(drawn.astype(out[name].dtype))
    for name, factor in factors.items():
        out[name] = (out[name] * factor).astype(out[name].dtype)
    return out
```

```python
from contextlib import ExitStack

import concourse.bass as bass
from concourse import mybir

P = 128
D = 1024
KD = D // P
SEQ, DEC_B, DEC_T = 2048, 8, 8
NS = DEC_B * DEC_T
NTOK = SEQ + NS
C = 512
NCH = SEQ // C
TPC = C // P
NT = SEQ // P + 1
DH = 512
NG = DH // P
PB, CB = 15, 3
WINDOWS = (2, 4, 8, 16)
NM = DEC_B + 1
NE, NGR, EPG, F = 16, 4, 4, 256
NR = NGR + NE
SLOTS = (2 * NTOK + NE * P - 1) // P
ALPHA = 2.0 ** 0.25
LN_EPS = 1e-5
LRU_C = 8.0
BIG = 3.0e38

ALU = mybir.AluOpType
ACT = mybir.ActivationFunctionType
F32 = mybir.dt.float32
BF16 = mybir.dt.bfloat16
I32 = mybir.dt.int32
AX = mybir.AxisListType.X
ds = bass.ds

SH1, SC1, G1, SH2, SC2, G2 = (n * D for n in range(6))
V_BCONV, V_BA, V_BX, V_LAM, V_PSCALE, V_WCONV = 0, 1, 2, 3, 4, 5
NV = 9


class Order:

    def __init__(self, eng, sem):
        self.eng, self.sem, self.base, self.n = eng, sem, 0, 0

    def did(self, ins):
        ins.then_inc(self.sem, 1)
        self.n += 1

    def wait(self):
        self.eng.wait_ge(self.sem, self.base + self.n)

    def step(self, ins):
        self.did(ins)
        self.wait()

    def enter(self, i, first, per):
        self.entry, self.per, self.first = self.base + self.n, per, first
        self.base, self.n = self.entry + (i - first) * per, 0

    def leave(self, trips):
        assert self.n == self.per, f"the loop's body counts {self.n}"
        self.base, self.n = self.entry + trips * self.per, 0


def build(nc, A):
    with ExitStack() as ctx:
        def sb(name, shape, dt=F32):
            return ctx.enter_context(nc.sbuf_tensor(name, shape, dt))

        def sem(name):
            return ctx.enter_context(nc.semaphore(name))

        bank = [ctx.enter_context(nc.psum_tensor(f"bank{n}", [P, 512], F32)) for n in range(8)]

        mod_d = nc.dram_tensor("mod_d", [NM, 6 * D], F32).ap()
        yT_d = nc.dram_tensor("yT_d", [NT, P, KD, P], F32).ap()
        x1_d = nc.dram_tensor("x1_d", [NTOK, D], F32).ap()
        u2_d = nc.dram_tensor("u2_d", [NTOK, D], F32).ap()
        ys_d = nc.dram_tensor("ys_d", [P * SLOTS, D], F32).ap()

        arena = sb("arena", [P, 50200])

        def at(off, *shape):
            n = 1
            for s in shape:
                n *= s
            v = arena[:, off:off + n]
            if len(shape) == 2:
                v = v.rearrange("p (a b) -> p a b", b=shape[1])
            if len(shape) == 3:
                v = v.rearrange("p (a b c) -> p a b c", b=shape[1], c=shape[2])
            return v

        w_in = at(0, KD, 3 * DH)
        xin = at(12288, TPC, D)
        uT = at(16384, KD, C)
        p_buf = at(20480, NG, PB + C)
        xr_buf = at(22592, NG, CB + C)
        xc = at(24656, NG, C)
        gel = at(26704, NG, C)
        tT = at(28752, NG, C)
        tI = at(30800, NG, C)
        tS = at(32848, NG, C)
        q_t, a_t, b_t, h_t = at(34896, C), at(35408, C), at(35920, C), at(36432, C)
        wsum = [at(36944, PB + C), at(37472, PB + C)]
        dif = at(38000, 2, C)
        yT = at(39024, KD, C)
        wa, wx, wp = at(43120, NG, P), at(43632, NG, P), at(44144, NG, P)
        xs = at(44656, D)
        uTs = at(45680, KD, NS)
        p_s = arena[:, 46192:46192 + NG * DEC_B * (PB + DEC_T)].rearrange(
            "p (g s t) -> p g s t", g=NG, s=DEC_B)
        xr_s = arena[:, 46928:46928 + NG * DEC_B * (CB + DEC_T)].rearrange("p (g s t) -> p g s t", g=NG, s=DEC_B)
        prj_s = at(47280, 2 * NG, NS)
        row_a, row_b, row_c, row_v = at(48304, DH), at(48816, DH), at(49328, DH), at(47792, DH)
        row_d, row_e = at(38000, DH), at(38512, DH)
        w_ada = [at(20480 + n * 4096, KD, 512) for n in range(3)]
        mod = at(32768, 6 * D)
        c_rows = at(39024, D)
        w_out = at(12288, KD, D)
        yTt = [at(n * 1024, KD, P) for n in range(2)]
        xres = [at(2048 + n * 1024, D) for n in range(2)]
        z = [at(4096 + n * 1024, D) for n in range(2)]
        x1 = [at(6144 + n * 1024, D) for n in range(2)]
        u2 = [at(8192 + n * 1024, D) for n in range(2)]
        u2T = at(10240, KD, P)
        w_rt = at(11264, KD, NR)
        b_rt = at(11424, NR)
        row_tiles = at(20480, 5, D)
        row_tiles_s = at(25600, 3, D)
        logits = at(49840, NT, NR)
        w_gu = [at(28752 + n * 6144, KD, 2 * F) for n in range(2)]
        w_gu2 = arena[:, 28752:28752 + 2 * 6144].rearrange("p (b n) -> p b n", b=2)
        w_dn = [at(28752 + n * 6144 + 4096, F // P, D) for n in range(2)]
        xg = [at(n * 1024, D) for n in range(2)]
        xT = at(2048, KD, P)
        hid, sil, hT = at(3072, F), at(3328, F), at(3584, F // P, P)
        y_sb = [at(4096 + n * 1024, D) for n in range(2)]
        ya = [at(6144 + n * 1024, D) for n in range(2)]
        yb = [at(8192 + n * 1024, D) for n in range(2)]
        xo = [at(12288 + n * 1024, D) for n in range(2)]
        oo = [at(14336 + n * 1024, D) for n in range(2)]
        fin_tiles = at(20480, 3, D)
        fin_tile_s = at(23552, D)
        rt = [at(41040 + n * 272, NT, NE) for n in range(9)]
        rt_f = [arena[:, 43500 + n * 68:43500 + (n + 1) * 68].rearrange("p (t e) -> p t e", t=NT) for n in range(10)]
        r17 = [at(44300 + n * NT, NT) for n in range(16)]
        big_t = arena[:, 44600:44600 + NE * NT].rearrange("p (a b) -> p a b", a=NE)
        lt_prod = at(44900, NE, NE)
        slot_ge = at(45200, SLOTS, NE)
        hot_a = [arena[:, 46000 + n * 64:46064 + n * 64].bitcast(BF16) for n in range(2)]
        hot_b = [arena[:, 46200 + n * SLOTS:46200 + (n + 1) * SLOTS].bitcast(BF16) for n in range(2)]
        e16 = [at(46400 + n * NE, NE) for n in range(6)]

        ident = sb("ident", [P, P])
        tri = sb("tri", [P, P])
        ones = sb("ones", [P, P])
        cT = sb("cT", [P, KD, NM])
        modT = sb("modT", [P, 2 * KD, NM])
        vecT = sb("vecT", [P, NG, NV])
        sp_t = sb("sp_t", [P, 5, NG])
        sp2 = sb("sp2", [P, NG])
        half_b = sb("half_b", [P, NG, 2])
        inv_cnt = sb("inv_cnt", [P, NG, 16])
        fix = sb("fix", [P, 16])
        h_last = sb("h_last", [P, NG])
        h0_s = sb("h0_s", [P, NG, DEC_B])
        st6 = [sb(f"st6_{n}", [P, 2, 6]) for n in range(2)]
        mv = [sb(f"mv{n}", [P, 2]) for n in range(2)]
        sd = [sb(f"sd{n}", [P, 1]) for n in range(2)]
        rs = [sb(f"rs{n}", [P, 2]) for n in range(2)]
        prio = sb("prio", [P, EPG])
        lt16 = sb("lt16", [P, NE, NE])
        iota17 = sb("iota17", [P, NT])
        iota_s = sb("iota_s", [P, SLOTS])
        iota_r = sb("iota_r", [P, P])
        part_i = sb("part_i", [P, 1])
        valid = sb("valid", [P, NT])
        wgt = sb("wgt", [P, 2, NT])
        pos_i = sb("pos_i", [P, 2, NT], I32)
        pos_a = sb("pos_a", [P, 2, NT], I32)
        pos_b = sb("pos_b", [P, 2, NT], I32)
        pos_f = sb("pos_f", [P, 4, NT])
        tok_i = sb("tok_i", [P, SLOTS], I32)
        slot_e = sb("slot_e", [P, SLOTS])
        slot_ei = sb("slot_ei", [P, 2, SLOTS], I32)
        end_i = sb("end_i", [P, NE], I32)
        tok_now = [sb(f"tok_now{n}", [P, 1], I32) for n in range(2)]
        pos_now = [sb(f"pos_now{n}", [P, 2], I32) for n in range(2)]
        spare = sb("spare", [1, 2])
        hP = sb("hP", [NG, P])

        S = {n: sem(n) for n in """consts small_in c_in vec_in ba_in gates_in gates_zero wpool_in st_in x_loaded xs_loaded w_in_in
            ada0 ada1 ada2 cT_mm cT_ok ada_mm ada_ok mod_ok modT_mm modT_ok vec_mm vec_ok st_mm xsT_mm mod_stored
            dve_order act_order pool_order xT_ready uT_ready uTs_ready proj_ready proj_evac xc_ready xr_free p_free
            gates_mm gates_evac T_ready T_guard S_ready d_ready pool_mm pool_evac ylru_ready y_stored prj_copied
            out_mm out_evac out_stored w_out_in tiles_in tiles_s_in rt_in yTt0 yTt1 xres0 xres1 mix_ready mix_used
            var_ready sd_ready z_scaled z_norm u2_ready x1_ready x1_st0 x1_st1 u2_st0 u2_st1 u2T_mm u2T_ok rt_mm rt_ok
            m_ready cnt_mm w_exp w_expd hot_ready hot_used idx_mm idx_ready w_exp_in xg0 xg1 xgT_mm xT_act xT_dve
            gu_mm sil_ok hid_ok hT_mm hT_ok dn_mm y_act y_dve ys0 ys1 fin_in fin_s_in ya0 ya1 yb0 yb1 xo0 xo1
            ya_scaled fvar_ready fsd_ready fz_ok fnorm fg_ok fo_ok os0 os1""".split()}

        block = ctx.enter_context(nc.Block())
        xp_d = A["x_prompt"].rearrange("b (c t p) d -> c p (b t) d", t=TPC, p=P)
        xpt_d = A["x_prompt"].rearrange("b (t p) d -> (b t) p d", p=P)
        xs_d = A["x_sample"].rearrange("b t d -> (b t) d")
        ada_d = A["w_ada"][0].rearrange("(k p) (g n) -> g p k n", p=P, n=512)
        yt_p, yt_s = A["out_0"].rearrange("b (t p) d -> (b t) p d", p=P), A["out_1"].rearrange("b t d -> (b t) d")
        gate_d = A["w_gate"][0].rearrange("e (k p) f -> e p k f", p=P)
        up_d = A["w_up"][0].rearrange("e (k p) f -> e p k f", p=P)
        down_d = A["w_down"][0].rearrange("e (k p) n -> e p k n", p=P)
        x1_t = x1_d[0:SEQ, :].rearrange("(t p) d -> t p d", p=P)
        u2_t = u2_d[0:SEQ, :].rearrange("(t p) d -> t p d", p=P)
        ys_t = ys_d.rearrange("(p s) d -> s p d", s=SLOTS)

        def all_parts(row, n=P):
            return row.rearrange("(a d) -> a d", a=1).broadcast_to([n, row.shape[0]])

        @block.sync
        def _(sp):
            sp.dma_start(c_rows[0:1, :], A["c_prompt"]).then_inc(S["c_in"], 16)
            sp.dma_start(c_rows[1:NM, :], A["c_sample"]).then_inc(S["c_in"], 16)
            for n in range(3):
                sp.dma_start(w_ada[n], ada_d[n]).then_inc(S[f"ada{n}"], 16)
            sp.dma_start(mod[0:NM, :], all_parts(A["b_ada"][0], NM)).then_inc(S["ba_in"], 16)
            for r, name in enumerate(("b_conv", "b_a", "b_x", "lru_lambda", "pool_scale")):
                sp.dma_start(row_v[r:r + 1, :], A[name]).then_inc(S["vec_in"], 16)
            sp.dma_start(row_v[V_WCONV:NV, :], A["w_conv"][0]).then_inc(S["vec_in"], 16)
            sp.dma_start(row_a[0:DEC_B * PB, :], A["state_pool"][0].rearrange("b t c -> (b t) c")).then_inc(S["st_in"], 16)
            sp.dma_start(row_b[0:DEC_B * CB, :], A["state_conv"][0].rearrange("b t c -> (b t) c")).then_inc(S["st_in"], 16)
            sp.dma_start(row_c[0:DEC_B, :], A["state_lru"][0]).then_inc(S["st_in"], 16)
            sp.dma_start(xs[0:NS, :], xs_d).then_inc(S["xs_loaded"], 16)
            with sp.Fori(1, 4) as j:
                for n in range(3):
                    sp.wait_ge(S["ada_mm"], 3 * j + n - 2)
                    sp.dma_start(w_ada[n], ada_d[ds(3 * j + n, 1)].rearrange("a p k n -> p (a k) n")).then_inc(S[f"ada{n}"], 16)
            sp.dma_start(xin, xp_d[0]).then_inc(S["x_loaded"], 16)
            sp.dma_start(w_in, A["w_in"][0].rearrange("(k p) n -> p k n", p=P)).then_inc(S["w_in_in"], 16)
            sp.wait_ge(S["gates_zero"], 1)
            for w, name in ((wa, "w_a"), (wx, "w_x")):
                heads = A[name][0].rearrange("(j q) i o -> q i j o", q=2)
                for q in range(2):
                    sp.dma_start(w[64 * q:64 * q + 64, :, 64 * q:64 * q + 64], heads[q]).then_inc(S["gates_in"], 16)
            sp.dma_start(wp, A["w_pool"][0].rearrange("g i o -> i g o")).then_inc(S["wpool_in"], 16)
            sp.dma_start(A["out_5"][0][:, 0:PB - DEC_T, :], A["state_pool"][0][:, DEC_T:PB, :]).then_inc(S["out_stored"], 16)
            sp.wait_ge(S["mod_ok"], 1)
            sp.dma_start(mod_d[:, 2 * D:6 * D], mod[0:NM, 2 * D:6 * D]).then_inc(S["mod_stored"], 16)

            def load_x(i):
                sp.wait_ge(S["xT_ready"], 8 * i)
                sp.dma_start(xin, xp_d[ds(i, 1)].rearrange("a p t d -> p (a t) d")).then_inc(S["x_loaded"], 16)

            def store_y(i):
                sp.wait_ge(S["pool_evac"], NG * i + NG)
                sp.wait_ge(S["ylru_ready"], NG * i + NG)
                for t in range(TPC):
                    sp.dma_start(yT_d[ds(TPC * i + t, 1)].rearrange("a p k n -> p (a k) n"),
                                 yT[:, :, t * P:(t + 1) * P]).then_inc(S["y_stored"], 16)

            load_x(1)
            with sp.Fori(0, NCH - 2) as i:
                store_y(i)
                load_x(i + 2)
            store_y(NCH - 2)
            sp.wait_ge(S["proj_ready"], 12 * NCH)
            sp.dma_start(w_out, A["w_out"][0].rearrange("(k p) n -> p k n", p=P)).then_inc(S["w_out_in"], 16)
            store_y(NCH - 1)
            sp.wait_ge(S["pool_evac"], NG * NCH + NG)
            sp.wait_ge(S["ylru_ready"], NG * NCH + NG)
            sp.dma_start(yT_d[NT - 1][:, :, 0:NS], yT[:, :, 0:NS]).then_inc(S["y_stored"], 16)
            sp.wait_ge(S["out_evac"], 6)
            sp.dma_start(A["out_2"][0, 0], row_v[0:PB, :]).then_inc(S["out_stored"], 16)
            sp.dma_start(A["out_3"][0, 0], row_d[0:CB, :]).then_inc(S["out_stored"], 16)
            sp.dma_start(A["out_4"].rearrange("a b (g c) -> (a b g) c", c=P), hP[:, :]).then_inc(S["out_stored"], 16)
            for s in range(DEC_B):
                sp.dma_start(A["out_5"][0, s, PB - DEC_T:PB, :], row_a[s * DEC_T:(s + 1) * DEC_T, :]).then_inc(S["out_stored"], 16)
                sp.dma_start(A["out_6"][0, s], row_b[(s + 1) * DEC_T - CB:(s + 1) * DEC_T, :]).then_inc(S["out_stored"], 16)
            sp.dma_start(A["out_7"][0], row_c[0:DEC_B, :]).then_inc(S["out_stored"], 16)

            sp.wait_ge(S["mod_stored"], 16)
            for n, row in enumerate((mod_d[0, G1:G1 + D], A["ln1_g"][0], A["ln1_b"][0], mod_d[0, SC2:SC2 + D], mod_d[0, SH2:SH2 + D])):
                sp.dma_start(row_tiles[:, n, :], all_parts(row)).then_inc(S["tiles_in"], 16)
            for n, off in enumerate((G1, SC2, SH2)):
                for s in range(DEC_B):
                    sp.dma_start(row_tiles_s[s * DEC_T:(s + 1) * DEC_T, n, :], all_parts(mod_d[s + 1, off:off + D], DEC_T)).then_inc(S["tiles_s_in"], 16)
            sp.dma_start(w_rt[:, :, 0:NGR], A["w_group"][0].rearrange("(k p) n -> p k n", p=P)).then_inc(S["rt_in"], 16)
            sp.dma_start(w_rt[:, :, NGR:NR], A["w_route"][0].rearrange("(k p) n -> p k n", p=P)).then_inc(S["rt_in"], 16)
            sp.dma_start(b_rt[:, 0:NGR], all_parts(A["b_group"][0])).then_inc(S["rt_in"], 16)
            sp.dma_start(b_rt[:, NGR:NR], all_parts(A["b_route"][0])).then_inc(S["rt_in"], 16)
            sp.wait_ge(S["y_stored"], 64 * NCH + 16)

            def load_tile(t, b, n=P):
                src_y = yT_d[ds(t, 1)].rearrange("a p k n -> p (a k) n") if n == P else yT_d[NT - 1][:, :, 0:n]
                src_x = xpt_d[ds(t, 1)].rearrange("a p d -> (a p) d") if n == P else xs_d
                sp.dma_start(yTt[b][:, :, 0:n], src_y).then_inc(S[f"yTt{b}"], 16)
                sp.dma_start(xres[b][0:n, :], src_x).then_inc(S[f"xres{b}"], 16)

            def store_tile(t, b, n=P):
                sp.wait_ge(S["x1_ready"], t + 1)
                sp.wait_ge(S["u2_ready"], t + 1)
                dst_x = x1_t[ds(t, 1)].rearrange("a p d -> (a p) d") if n == P else x1_d[SEQ:NTOK, :]
                dst_u = u2_t[ds(t, 1)].rearrange("a p d -> (a p) d") if n == P else u2_d[SEQ:NTOK, :]
                sp.dma_start(dst_x, x1[b][0:n, :]).then_inc(S[f"x1_st{b}"], 16)
                sp.dma_start(dst_u, u2[b][0:n, :]).then_inc(S[f"u2_st{b}"], 16)

            load_tile(0, 0)
            load_tile(1, 1)
            with sp.Fori(0, NT // 2 - 1) as j:
                for b in range(2):
                    sp.wait_ge(S["mix_ready"], 2 * j + b + 1)
                    sp.wait_ge(S["mix_used"], 2 * j + b + 1)
                    load_tile(2 * j + 2 + b, b)
                    store_tile(2 * j + b, b)
            sp.wait_ge(S["mix_ready"], NT - 2)
            sp.wait_ge(S["mix_used"], NT - 2)
            load_tile(NT - 1, 0, NS)
            store_tile(NT - 3, 0)
            store_tile(NT - 2, 1)
            for e in range(2):
                if e:
                    sp.wait_ge(S["w_exp_in"], 48)
                sp.dma_start(w_gu[e][:, :, 0:F], gate_d[e]).then_inc(S["w_exp_in"], 16)
                sp.dma_start(w_gu[e][:, :, F:2 * F], up_d[e]).then_inc(S["w_exp_in"], 16)
                sp.dma_start(w_dn[e], down_d[e]).then_inc(S["w_exp_in"], 16)
            store_tile(NT - 1, 0, NS)
            sp.wait_ge(S["idx_ready"], 1)
            for n, row in enumerate((mod_d[0, G2:G2 + D], A["ln2_g"][0], A["ln2_b"][0])):
                sp.dma_start(fin_tiles[:, n, :], all_parts(row)).then_inc(S["fin_in"], 16)
            for s in range(DEC_B):
                sp.dma_start(fin_tile_s[s * DEC_T:(s + 1) * DEC_T, :], all_parts(mod_d[s + 1, G2:G2 + D], DEC_T)).then_inc(S["fin_s_in"], 16)
            with sp.Fori(1, NE // 2) as j:
                for b in range(2):
                    last_slot = sp.value_load(end_i[0:1, ds(2 * j + b - 2, 1)], min_val=1, max_val=SLOTS)
                    sp.wait_ge(S["w_exp_in"], 48 * (2 * j + b))
                    sp.wait_ge(S["dn_mm"], last_slot)
                    sp.dma_start(w_gu[b][:, :, 0:F], gate_d[ds(2 * j + b, 1)].rearrange("a p k f -> p (a k) f")).then_inc(S["w_exp_in"], 16)
                    sp.dma_start(w_gu[b][:, :, F:2 * F], up_d[ds(2 * j + b, 1)].rearrange("a p k f -> p (a k) f")).then_inc(S["w_exp_in"], 16)
                    sp.dma_start(w_dn[b], down_d[ds(2 * j + b, 1)].rearrange("a p k n -> p (a k) n")).then_inc(S["w_exp_in"], 16)

            def load_x1(t, b, n=P):
                src = x1_t[ds(t, 1)].rearrange("a p d -> (a p) d") if n == P else x1_d[SEQ:NTOK, :]
                sp.dma_start(xo[b][0:n, :], src).then_inc(S[f"xo{b}"], 16)

            def store_o(t, b, n=P):
                sp.wait_ge(S["fo_ok"], t + 1)
                dst = yt_p[ds(t, 1)].rearrange("a p d -> (a p) d") if n == P else yt_s
                sp.dma_start(dst, oo[b][0:n, :]).then_inc(S[f"os{b}"], 16)

            load_x1(0, 0)
            load_x1(1, 1)
            with sp.Fori(0, NT // 2 - 1) as j:
                for b in range(2):
                    store_o(2 * j + b, b)
                    load_x1(2 * j + 2 + b, b)
            store_o(NT - 3, 0)
            load_x1(NT - 1, 0, NS)
            store_o(NT - 2, 1)
            store_o(NT - 1, 0, NS)
            sp.wait_ge(S["os0"], 16 * (NT // 2 + 1))
            sp.wait_ge(S["os1"], 16 * (NT // 2))
            sp.wait_ge(S["out_stored"], 16 * (5 + 2 * DEC_B))

        @block.gpsimd
        def _(pool):
            o = Order(pool, S["pool_order"])
            o.did(pool.memset(ident[:], 0.0))
            o.did(pool.memset(tri[:], 1.0))
            o.did(pool.memset(lt16[:], 1.0))
            o.did(pool.memset(valid[:], 1.0))
            o.did(pool.iota(iota17[:], pattern=[[P, NT]], base=0, channel_multiplier=0, allow_small_or_imprecise_dtypes=True))
            o.did(pool.iota(iota_s[:], pattern=[[1, SLOTS]], base=0, channel_multiplier=0, allow_small_or_imprecise_dtypes=True))
            o.did(pool.iota(iota_r[:], pattern=[[1, P]], base=0, channel_multiplier=0, allow_small_or_imprecise_dtypes=True))
            o.did(pool.iota(part_i[:], pattern=[[0, 1]], base=0, channel_multiplier=1, allow_small_or_imprecise_dtypes=True))
            o.did(pool.iota(prio[:], pattern=[[-1, EPG]], base=EPG, channel_multiplier=0, allow_small_or_imprecise_dtypes=True))
            o.did(pool.memset(wa, 0.0))
            pool.memset(wx, 0.0).then_inc(S["gates_zero"], 1)
            o.did(pool.memset(ones[:], 1.0))
            o.wait()
            pool.affine_select(out=ident[:], in_=ident[:], compare_op=ALU.not_equal, fill=1.0, base=0,
                               pattern=[[-1, P]], channel_multiplier=1).then_inc(S["consts"], 1)
            pool.affine_select(out=tri[:], in_=tri[:], compare_op=ALU.is_gt, fill=0.0, base=0,
                               pattern=[[1, P]], channel_multiplier=-1).then_inc(S["consts"], 1)
            pool.affine_select(out=lt16[:], in_=lt16[:], compare_op=ALU.is_gt, fill=0.0, base=0,
                               pattern=[[1, NE], [-1, NE]], channel_multiplier=0).then_inc(S["consts"], 1)
            pool.affine_select(out=valid[:, NT - 1:NT], in_=valid[:, NT - 1:NT], compare_op=ALU.is_gt, fill=0.0, base=NS,
                               pattern=[[0, 1]], channel_multiplier=-1).then_inc(S["consts"], 1)

            pool.wait_ge(S["tiles_in"], 80)

            def x1_tile(t, b, n=P, first=False):
                pool.wait_ge(S["z_norm"], t + 1)
                if not first:
                    pool.wait_ge(S[f"x1_st{b}"], 16 * x1_tile.uses(t))
                o.step(pool.tensor_tensor(x1[b][0:n, :], z[b][0:n, :], row_tiles[0:n, 1, :], ALU.mult))
                pool.tensor_tensor(x1[b][0:n, :], x1[b][0:n, :], row_tiles[0:n, 2, :], ALU.add).then_inc(S["x1_ready"], 1)

            x1_tile.uses = lambda t: t
            for b in range(2):
                x1_tile(b, b, first=True)
            with pool.Fori(1, NT // 2) as j:
                o.enter(j, 1, 2)
                x1_tile.uses = lambda t: j
                for b in range(2):
                    x1_tile(2 * j + b, b)
            o.leave(NT // 2 - 1)
            x1_tile.uses = lambda t: NT // 2
            x1_tile(NT - 1, 0, NS)

            pool.wait_ge(S["idx_ready"], 1)
            for b, n in ((0, NT // 2 + 1), (1, NT // 2)):
                pool.wait_ge(S[f"u2_st{b}"], 16 * n)

            def gather(s, b):
                o.did(pool.tensor_copy(tok_now[b][:], tok_i[:, ds(s, 1)]))
                o.wait()
                pool.tensor_tensor(spare[0:1, 1:2], ones[0:1, 0:1], ones[0:1, 0:1], ALU.mult)
                pool.indirect_dma_start(out=xg[b], out_offset=None, in_=u2_d,
                                        in_offset=bass.IndirectOffsetOnAxis(ap=tok_now[b][:, 0:1], axis=0)).then_inc(S[f"xg{b}"], 16)

            gather(0, 0)
            gather(1, 1)
            with pool.Fori(1, SLOTS // 2) as j:
                o.enter(j, 1, 2)
                for b in range(2):
                    pool.wait_ge(S["xgT_mm"], 4 * j + 2 * b - 2)
                    gather(2 * j + b, b)
            o.leave(SLOTS // 2 - 1)

            for b in range(2):
                pool.wait_ge(S[f"ys{b}"], 16 * (SLOTS // 2))

            def gather_y(t, b, n=P):
                for k in range(2):
                    o.did(pool.tensor_copy(pos_now[b][:, k:k + 1], pos_i[:, k, ds(t, 1)]))
                o.wait()
                pool.tensor_tensor(spare[0:1, 1:2], ones[0:1, 0:1], ones[0:1, 0:1], ALU.mult)
                for buf, k, name in ((ya, 0, "ya"), (yb, 1, "yb")):
                    pool.indirect_dma_start(out=buf[b][0:n, :], out_offset=None, in_=ys_d,
                                            in_offset=bass.IndirectOffsetOnAxis(ap=pos_now[b][0:n, k:k + 1], axis=0)
                                            ).then_inc(S[f"{name}{b}"], 16)

            gather_y(0, 0)
            gather_y(1, 1)
            with pool.Fori(1, NT // 2) as j:
                o.enter(j, 1, 4)
                for b in range(2):
                    pool.wait_ge(S["fg_ok"], 2 * j + b - 1)
                    gather_y(2 * j + b, b)
            o.leave(NT // 2 - 1)
            pool.wait_ge(S["fg_ok"], NT - 2)
            gather_y(NT - 1, 0, NS)

        @block.scalar
        def _(act):
            o = Order(act, S["act_order"])
            act.wait_ge(S["vec_ok"], 1)
            o.step(act.activation(sp_t[:, 0, :], vecT[:, :, V_LAM], ACT.Abs))
            o.did(act.activation(sp_t[:, 1, :], sp_t[:, 0, :], ACT.Exp, scale=-1.0))

            def chunk(i, first=False):
                for k in range(KD):
                    act.wait_ge(S["xT_ready"], 8 * i + k + 1)
                    act.activation(uT[:, k, :], bank[k % 2][:, :], ACT.Identity, bias=modT[:, k, 0:1],
                                   scale=modT[:, KD + k, 0:1]).then_inc(S["uT_ready"], 1)
                for m in range(2 * NG):
                    j = m % NG
                    act.wait_ge(S["proj_ready"], 12 * i + m + 1)
                    if m < NG:
                        if not first:
                            act.wait_ge(S["xr_free"], NG * i - NG + j + 1)
                        dst = xr_buf[:, j, CB:CB + C]
                    else:
                        if not first:
                            act.wait_ge(S["p_free"], NG * i - NG + j + 1)
                        dst = p_buf[:, j, PB:PB + C]
                    act.activation(dst, bank[2 + m % 2][:, :], ACT.Copy).then_inc(S["proj_evac"], 1)
                gates(i, C, first)
                for j in range(NG):
                    act.wait_ge(S["proj_ready"], 12 * i + 2 * NG + j + 1)
                    if not first:
                        act.wait_ge(S["ylru_ready"], NG * i - NG + j + 1)
                    act.activation(gel[:, j, :], bank[2 + j % 2][:, :], ACT.Gelu_apprx_tanh).then_inc(S["proj_evac"], 1)
                roots_and_pool(i, C, first)

            def gates(i, n, first):
                for j in range(NG):
                    if not first:
                        act.wait_ge(S["ylru_ready"], NG * i - NG + j + 1)
                    for q, dst in ((0, tT), (1, tI)):
                        act.wait_ge(S["gates_mm"], 2 * NG * i + 2 * j + q + 1)
                        act.activation(dst[:, j, 0:n], bank[4 + q][:, 0:n], ACT.Tanh, bias=half_b[:, j, q:q + 1],
                                       scale=0.5).then_inc(S["gates_evac"], 1)
                    act.wait_ge(S["gates_evac"], 2 * NG * i + 2 * j + 2)
                    act.activation(tT[:, j, 0:n], tT[:, j, 0:n], ACT.Tanh, bias=sp2[:, j:j + 1],
                                   scale=sp2[:, j:j + 1]).then_inc(S["T_ready"], 1)

            def roots_and_pool(i, n, first):
                for j in range(NG):
                    act.wait_ge(S["T_guard"], NG * i + j + 1)
                    act.activation(tS[:, j, 0:n], tT[:, j, 0:n], ACT.Sqrt).then_inc(S["S_ready"], 1)
                if not first:
                    act.wait_ge(S["y_stored"], 64 * i)
                for g in range(NG):
                    act.wait_ge(S["pool_mm"], NG * i + g + 1)
                    act.activation(yT[:, g, 0:n], bank[6 + g % 2][:, 0:n], ACT.Copy,
                                   scale=vecT[:, g, V_PSCALE:V_PSCALE + 1]).then_inc(S["pool_evac"], 1)

            act.wait_ge(S["modT_ok"], 1)
            act.wait_ge(S["vec_ok"], 2)
            chunk(0, first=True)
            with act.Fori(1, NCH) as i:
                chunk(i)
            i = NCH
            for m in range(2 * NG):
                j = m % NG
                act.wait_ge(S["proj_ready"], 12 * i + m + 1)
                dst = xr_s[:, j, :, CB:CB + DEC_T] if m < NG else p_s[:, j, :, PB:PB + DEC_T]
                act.activation(dst, bank[2 + m % 2][:, 0:NS].rearrange("p (s t) -> p s t", s=DEC_B),
                               ACT.Copy).then_inc(S["proj_evac"], 1)
            gates(i, NS, False)
            for j in range(NG):
                act.wait_ge(S["proj_ready"], 12 * i + 2 * NG + j + 1)
                act.activation(gel[:, j, 0:NS], bank[2 + j % 2][:, 0:NS], ACT.Gelu_apprx_tanh).then_inc(S["proj_evac"], 1)
            roots_and_pool(i, NS, False)
            for n, (dst, rows, cols) in enumerate(((row_v, PB, DH), (row_d, CB, DH), (hP, NG, P),
                                                   (row_a, NS, DH), (row_b, NS, DH), (row_c, DEC_B, DH))):
                act.wait_ge(S["out_mm"], n + 1)
                act.activation(dst[0:rows, 0:cols], bank[n % 2][0:rows, 0:cols], ACT.Copy).then_inc(S["out_evac"], 1)

            def u2T_evac(t):
                for h in range(2):
                    act.wait_ge(S["u2T_mm"], 2 * t + h + 1)
                    act.activation(u2T[:, 4 * h:4 * h + 4, :], bank[4 + h][:, :].rearrange("p (k n) -> p k n", n=P),
                                   ACT.Copy).then_inc(S["u2T_ok"], 1)

            def norm(t, b, n=P):
                act.wait_ge(S["var_ready"], 2 * t + 1)
                act.activation(sd[b][0:n, :], mv[b][0:n, 1:2], ACT.Sqrt).then_inc(S["sd_ready"], 1)
                act.wait_ge(S["var_ready"], 2 * t + 2)
                act.activation(z[b][0:n, :], z[b][0:n, :], ACT.Identity, bias=rs[b][0:n, 1:2],
                               scale=rs[b][0:n, 0:1]).then_inc(S["z_norm"], 1)

            norm(0, 0)
            norm(1, 1)
            with act.Fori(1, NT // 2) as j:
                for b in range(2):
                    norm(2 * j + b, b)
                    u2T_evac(2 * j + b - 2)
            norm(NT - 1, 0, NS)
            for t in range(NT - 3, NT - 1):
                u2T_evac(t)
            for h in range(2):
                act.wait_ge(S["u2T_mm"], 2 * (NT - 1) + h + 1)
                act.activation(u2T[:, 4 * h:4 * h + 4, 0:NS], bank[4 + h][:, :].rearrange("p (k n) -> p k n", n=P)[:, :, 0:NS],
                               ACT.Copy).then_inc(S["u2T_ok"], 1)
            act.wait_ge(S["w_exp"], 1)
            act.activation(rt_f[8], rt_f[8], ACT.Exp).then_inc(S["w_expd"], 1)
            act.activation(r17[4], r17[4], ACT.Exp).then_inc(S["w_expd"], 1)

            def x_evac(s):
                act.wait_ge(S["xgT_mm"], 2 * s + 1)
                act.activation(xT[:, 0:4, :], bank[0][:, :].rearrange("p (k n) -> p k n", n=P), ACT.Copy).then_inc(S["xT_act"], 1)

            def silu(s, b):
                act.wait_ge(S["gu_mm"], s + 1)
                act.activation(sil, bank[2 + b][:, 0:F], ACT.Silu).then_inc(S["sil_ok"], 1)

            def hT_evac(s):
                act.wait_ge(S["hT_mm"], s + 1)
                act.activation(hT, bank[4][:, 0:F].rearrange("p (k n) -> p k n", n=P), ACT.Copy).then_inc(S["hT_ok"], 1)

            def y_evac(s, b, before=None):
                act.wait_ge(S["dn_mm"], s + 1)
                if before is not None:
                    act.wait_ge(S[f"ys{b}"], 16 * before)
                act.activation(y_sb[b][:, 0:512], bank[5][:, :], ACT.Copy).then_inc(S["y_act"], 1)
                act.wait_ge(S["y_act"], s + 1)
                act.wait_ge(S["y_dve"], s + 1)
                act.dma_start(ys_t[ds(s, 1)].rearrange("a p d -> (a p) d"), y_sb[b]).then_inc(S[f"ys{b}"], 16)

            x_evac(0)
            silu(0, 0)
            x_evac(1)
            hT_evac(0)
            for s in (1, 2):
                silu(s, s % 2)
                x_evac(s + 1)
                y_evac(s - 1, (s - 1) % 2)
                hT_evac(s)
            with act.Fori(1, SLOTS // 2 - 1) as j:
                for b in range(2):
                    s = 2 * j + 1 + b
                    silu(s, 1 - b)
                    x_evac(s + 1)
                    y_evac(s - 1, b, j)
                    hT_evac(s)
            s = SLOTS - 1
            silu(s, 1)
            y_evac(s - 1, 0, SLOTS // 2 - 1)
            hT_evac(s)
            y_evac(s, 1, SLOTS // 2 - 1)

            def fin(t, b, n=P, uses=1):
                act.wait_ge(S[f"ya{b}"], 16 * uses)
                act.activation(ya[b][0:n, :], ya[b][0:n, :], ACT.Copy, scale=wgt[0:n, 0, ds(t, 1)]).then_inc(S["ya_scaled"], 1)
                act.wait_ge(S["fvar_ready"], 2 * t + 1)
                act.activation(sd[b][0:n, :], mv[b][0:n, 1:2], ACT.Sqrt).then_inc(S["fsd_ready"], 1)
                act.wait_ge(S["fvar_ready"], 2 * t + 2)
                act.activation(ya[b][0:n, :], ya[b][0:n, :], ACT.Identity, bias=rs[b][0:n, 1:2],
                               scale=rs[b][0:n, 0:1]).then_inc(S["fnorm"], 1)

            with act.Fori(0, NT // 2) as j:
                for b in range(2):
                    fin(2 * j + b, b, uses=j + 1)
            fin(NT - 1, 0, NS, NT // 2 + 1)

        @block.vector
        def _(dve):
            o = Order(dve, S["dve_order"])
            dve.wait_ge(S["vec_mm"], 1)
            dve.tensor_copy(vecT[:], bank[7][:, 0:NG * NV].rearrange("p (g v) -> p g v", v=NV)).then_inc(S["vec_ok"], 1)
            dve.wait_ge(S["vec_ok"], 1)
            lam = vecT[:, :, V_LAM]
            o.did(dve.tensor_scalar(half_b[:, :, 0], vecT[:, :, V_BA], 0.5, None, ALU.mult))
            o.did(dve.tensor_scalar(half_b[:, :, 1], vecT[:, :, V_BX], 0.5, None, ALU.mult))
            dve.wait_ge(S["act_order"], 2)
            o.step(dve.tensor_scalar(sp_t[:, 2, :], sp_t[:, 1, :], 2.0, None, ALU.add))
            o.step(dve.reciprocal(sp_t[:, 2, :], sp_t[:, 2, :]))
            o.step(dve.tensor_tensor(sp_t[:, 1, :], sp_t[:, 1, :], sp_t[:, 2, :], ALU.mult))
            o.step(dve.tensor_tensor(sp_t[:, 2, :], sp_t[:, 1, :], sp_t[:, 1, :], ALU.mult))
            o.step(dve.tensor_scalar(sp_t[:, 3, :], sp_t[:, 2, :], 1.0 / 17, 1.0 / 15, ALU.mult, ALU.add))
            for odd in (13, 11, 9, 7, 5, 3, 1):
                o.step(dve.tensor_tensor(sp_t[:, 3, :], sp_t[:, 3, :], sp_t[:, 2, :], ALU.mult))
                o.step(dve.tensor_scalar(sp_t[:, 3, :], sp_t[:, 3, :], 1.0 / odd, None, ALU.add))
            o.step(dve.tensor_tensor(sp_t[:, 3, :], sp_t[:, 3, :], sp_t[:, 1, :], ALU.mult))
            o.step(dve.tensor_scalar(sp_t[:, 4, :], lam, -1.0, 0.0, ALU.mult, ALU.max))
            o.step(dve.scalar_tensor_tensor(sp_t[:, 4, :], sp_t[:, 3, :], 2.0, sp_t[:, 4, :], ALU.mult, ALU.add))
            dve.tensor_scalar(sp2[:], sp_t[:, 4, :], LRU_C / 4, None, ALU.mult).then_inc(S["vec_ok"], 1)
            dve.wait_ge(S["cT_mm"], 1)
            dve.tensor_copy(cT[:], bank[6][:, 0:KD * NM].rearrange("p (k r) -> p k r", r=NM)).then_inc(S["cT_ok"], 1)
            dve.wait_ge(S["ba_in"], 16)
            with dve.Fori(0, 4) as j:
                for n in range(3):
                    dve.wait_ge(S["ada_mm"], 3 * j + n + 1)
                    cols = mod[0:NM, ds(1536 * j + 512 * n, 512)]
                    dve.tensor_tensor(cols, bank[n][0:NM, :], cols, ALU.add).then_inc(S["ada_ok"], 1)
            dve.wait_ge(S["ada_ok"], 12)
            o.step(dve.tensor_scalar(mod[0:NM, SC1:SH2], mod[0:NM, SC1:SH2], 1.0, None, ALU.add))
            dve.tensor_scalar(mod[0:NM, SC2:6 * D], mod[0:NM, SC2:6 * D], 1.0, None, ALU.add).then_inc(S["mod_ok"], 1)
            dve.wait_ge(S["modT_mm"], 1)
            dve.tensor_copy(modT[:], bank[6][:, 0:2 * KD * NM].rearrange("p (k r) -> p k r", r=NM)).then_inc(S["modT_ok"], 1)
            dve.wait_ge(S["st_mm"], 1)
            for g in range(NG):
                o.did(dve.tensor_copy(p_s[:, g, :, 0:PB], bank[4][:, g * 120:(g + 1) * 120].rearrange("p (s t) -> p s t", s=DEC_B)))
                o.did(dve.tensor_copy(xr_s[:, g, :, 0:CB], bank[5][:, g * 24:(g + 1) * 24].rearrange("p (s t) -> p s t", s=DEC_B)))
            o.did(dve.tensor_copy(h0_s[:], bank[5][:, 128:128 + NG * DEC_B].rearrange("p (g s) -> p g s", s=DEC_B)))
            o.did(dve.memset(p_buf[:, :, 0:PB], 0.0))
            o.did(dve.memset(xr_buf[:, :, 0:CB], 0.0))
            o.did(dve.memset(h_last[:], 0.0))
            for g, w in enumerate(WINDOWS):
                for t in range(PB):
                    o.did(dve.memset(inv_cnt[:, g, t:t + 1], 1.0 / min(w, t + 1)))
            o.wait()
            dve.wait_ge(S["xsT_mm"], 1)
            seqs = lambda v: v.rearrange("p k (s t) -> p k s t", s=DEC_B)
            over_t = lambda v: v.unsqueeze(3).to_broadcast([P, KD, DEC_B, DEC_T])
            o.step(dve.tensor_tensor(seqs(uTs), bank[7][:, :].rearrange("p (k s t) -> p k s t", k=KD, s=DEC_B),
                                     over_t(modT[:, KD:2 * KD, 1:NM]), ALU.mult))
            dve.tensor_tensor(seqs(uTs), seqs(uTs), over_t(modT[:, 0:KD, 1:NM]), ALU.add).then_inc(S["uTs_ready"], 1)

            def conv(i, j, out, inp, free_views):
                taps = [inp(k) for k in range(4)]
                o.step(dve.tensor_scalar(out, taps[0], vecT[:, j, V_WCONV:V_WCONV + 1], vecT[:, j, V_BCONV:V_BCONV + 1],
                                         ALU.mult, ALU.add))
                for k in range(1, 4):
                    last = dve.scalar_tensor_tensor(out, taps[k], vecT[:, j, V_WCONV + k:V_WCONV + k + 1], out, ALU.mult, ALU.add)
                    if k < 3:
                        o.step(last)
                last.then_inc(S["xc_ready"], 1)

            def guard(i, n):
                for j in range(NG):
                    dve.wait_ge(S["T_ready"], NG * i + j + 1)
                    dve.tensor_scalar(tT[:, j, 0:n], tT[:, j, 0:n], 0.0, None, ALU.max).then_inc(S["T_guard"], 1)

            def lru_coefficients(i, j, n, a_out, b_out):
                dve.wait_ge(S["S_ready"], NG * i + j + 1)
                o.step(dve.tensor_scalar(q_t[:, 0:n], tT[:, j, 0:n], 1.0, None, ALU.add))
                o.did(dve.scalar_tensor_tensor(b_out, tI[:, j, 0:n], 1.0, xc[:, j, 0:n], ALU.add, ALU.mult))
                o.step(dve.reciprocal(q_t[:, 0:n], q_t[:, 0:n]))
                o.did(dve.tensor_scalar(a_out, q_t[:, 0:n], 2.0, -1.0, ALU.mult, ALU.add))
                o.step(dve.tensor_tensor(q_t[:, 0:n], q_t[:, 0:n], tS[:, j, 0:n], ALU.mult))
                o.step(dve.tensor_tensor(b_out, b_out, q_t[:, 0:n], ALU.mult))

            def chunk(i, first=False):
                for j in range(NG):
                    dve.wait_ge(S["proj_evac"], 12 * i + j + 1)
                    conv(i, j, xc[:, j, :], lambda k: xr_buf[:, j, k:k + C], None)
                    dve.wait_ge(S["xc_ready"], NG * i + j + 1)
                    dve.tensor_copy(xr_buf[:, j, 0:CB], xr_buf[:, j, C:C + CB]).then_inc(S["xr_free"], 1)
                for g, w in enumerate(WINDOWS):
                    dve.wait_ge(S["proj_evac"], 12 * i + NG + g + 1)
                    src, span, nb = p_buf[:, g, :], 1, 0
                    while span < w:
                        dst = wsum[nb]
                        lo = PB - w + 2 * span
                        o.step(dve.tensor_tensor(dst[:, lo:PB + C], src[:, lo:PB + C], src[:, lo - span:PB + C - span], ALU.add))
                        src, span, nb = dst, 2 * span, 1 - nb
                    if not (first and g < 2):
                        dve.wait_ge(S["pool_mm"], NG * i + g - 1)
                    dd = dif[:, g % 2, :]
                    o.did(dve.scalar_tensor_tensor(dd[:, PB:C], src[:, 2 * PB:PB + C], 1.0 / w, p_buf[:, g, 2 * PB:PB + C],
                                                   ALU.mult, ALU.subtract))
                    o.step(dve.tensor_tensor(fix[:, 0:PB], src[:, PB:2 * PB], inv_cnt[:, g, 0:PB], ALU.mult))
                    dve.tensor_tensor(dd[:, 0:PB], fix[:, 0:PB], p_buf[:, g, PB:2 * PB], ALU.subtract).then_inc(S["d_ready"], 1)
                    dve.wait_ge(S["d_ready"], NG * i + g + 1)
                    o.did(dve.memset(inv_cnt[:, g, 0:PB], 1.0 / w))
                    dve.tensor_copy(p_buf[:, g, 0:PB], p_buf[:, g, C:C + PB]).then_inc(S["p_free"], 1)
                guard(i, C)
                if not first:
                    dve.wait_ge(S["y_stored"], 64 * i)
                for j in range(NG):
                    lru_coefficients(i, j, C, a_t, b_t)
                    o.step(dve.tensor_tensor_scan(h_t, a_t, b_t, h_last[:, j:j + 1], ALU.mult, ALU.add))
                    o.did(dve.tensor_copy(h_last[:, j:j + 1], h_t[:, C - 1:C]))
                    dve.wait_ge(S["proj_evac"], 12 * i + 2 * NG + j + 1)
                    dve.tensor_tensor(yT[:, NG + j, :], h_t, gel[:, j, :], ALU.mult).then_inc(S["ylru_ready"], 1)
                o.wait()

            dve.wait_ge(S["mod_stored"], 16)
            chunk(0, first=True)
            with dve.Fori(1, NCH) as i:
                o.enter(i, 1, CHUNK_STEPS)
                chunk(i)
            o.leave(NCH - 1)

            i = NCH
            bs = lambda v: v.rearrange("p (s t) -> p s t", s=DEC_B)
            for j in range(NG):
                dve.wait_ge(S["proj_evac"], 12 * i + j + 1)
                conv(i, j, bs(xc[:, j, 0:NS]), lambda k: xr_s[:, j, :, k:k + DEC_T], None)
            for g, w in enumerate(WINDOWS):
                dve.wait_ge(S["proj_evac"], 12 * i + NG + g + 1)
                wv = [v[:, 0:DEC_B * (PB + DEC_T)].rearrange("p (s t) -> p s t", s=DEC_B) for v in wsum]
                src, span, end, nb = p_s[:, g], 1, PB + DEC_T, 0
                while span < w:
                    lo = PB - w + 2 * span
                    o.step(dve.tensor_tensor(wv[nb][:, :, lo:end], src[:, :, lo:end], src[:, :, lo - span:end - span], ALU.add))
                    src, span, nb = wv[nb], 2 * span, 1 - nb
                dve.wait_ge(S["pool_mm"], NG * i + g - 1)
                dve.scalar_tensor_tensor(bs(dif[:, g % 2, 0:NS]), src[:, :, PB:end], 1.0 / w, p_s[:, g, :, PB:end],
                                         ALU.mult, ALU.subtract).then_inc(S["d_ready"], 1)
                dve.wait_ge(S["d_ready"], NG * i + g + 1)
            for g in range(NG):
                o.did(dve.tensor_copy(bs(prj_s[:, g, :]), p_s[:, g, :, PB:PB + DEC_T]))
                o.did(dve.tensor_copy(bs(prj_s[:, NG + g, :]), xr_s[:, g, :, CB:CB + DEC_T]))
            guard(i, NS)
            av, bv, hv = (v[:, 0:NG * NS].rearrange("p (g s t) -> p g s t", g=NG, s=DEC_B) for v in (a_t, b_t, h_t))
            for j in range(NG):
                lru_coefficients(i, j, NS, a_t[:, j * NS:(j + 1) * NS], b_t[:, j * NS:(j + 1) * NS])
            for t in range(DEC_T):
                before = h0_s[:] if t == 0 else hv[:, :, :, t - 1]
                o.step(dve.tensor_tensor(hv[:, :, :, t], av[:, :, :, t], before, ALU.mult))
                o.step(dve.tensor_tensor(hv[:, :, :, t], hv[:, :, :, t], bv[:, :, :, t], ALU.add))
            dve.tensor_copy(h0_s[:], hv[:, :, :, DEC_T - 1]).then_inc(S["prj_copied"], 1)
            dve.wait_ge(S["proj_evac"], 12 * i + 12)
            dve.wait_ge(S["y_stored"], 64 * i)
            for j in range(NG):
                dve.tensor_tensor(yT[:, NG + j, 0:NS], h_t[:, j * NS:(j + 1) * NS], gel[:, j, 0:NS], ALU.mult).then_inc(S["ylru_ready"], 1)

            dve.wait_ge(S["tiles_in"], 80)
            dve.wait_ge(S["rt_in"], 64)

            def ln_in(t, b, n, rows, uses, first):
                dve.wait_ge(S["mix_ready"], t + 1)
                for h in range(2):
                    o.did(dve.tensor_tensor(z[b][0:n, 512 * h:512 * h + 512], bank[2 * b + h][0:n, :],
                                            rows[0][0:n, 512 * h:512 * h + 512], ALU.mult))
                o.wait()
                dve.wait_ge(S[f"xres{b}"], 16 * uses)
                dve.scalar_tensor_tensor(z[b][0:n, :], xres[b][0:n, :], ALPHA, z[b][0:n, :], ALU.mult, ALU.add).then_inc(S["mix_used"], 1)
                dve.wait_ge(S["mix_used"], t + 1)
                stats(b, n, z[b], S["var_ready"], S["sd_ready"], t)

            def stats(b, n, zz, ready, sd_ready, t):
                for h in range(2):
                    o.did(dve.bn_stats(st6[b][0:n, h, :], zz[0:n, 512 * h:512 * h + 512]))
                o.wait()
                dve.memset(spare[0:1, 0:1], 0.0)
                o.step(dve.bn_aggr(mv[b][0:n, :], st6[b][0:n, :, :].rearrange("p a b -> p (a b)")))
                dve.tensor_scalar(mv[b][0:n, 1:2], mv[b][0:n, 1:2], LN_EPS, None, ALU.add).then_inc(ready, 1)
                dve.wait_ge(sd_ready, t + 1)
                o.step(dve.reciprocal(rs[b][0:n, 0:1], sd[b][0:n, :]))
                dve.scalar_tensor_tensor(rs[b][0:n, 1:2], mv[b][0:n, 0:1], -1.0, rs[b][0:n, 0:1], ALU.mult, ALU.mult).then_inc(ready, 1)

            def ln_out(t, b, n, rows, uses, first):
                dve.wait_ge(S["x1_ready"], t + 1)
                if not first:
                    dve.wait_ge(S[f"u2_st{b}"], 16 * (uses - 1))
                    dve.wait_ge(S["u2T_mm"], 2 * t - 2)
                o.step(dve.tensor_tensor(u2[b][0:n, :], x1[b][0:n, :], rows[1][0:n, :], ALU.mult))
                dve.tensor_tensor(u2[b][0:n, :], u2[b][0:n, :], rows[2][0:n, :], ALU.add).then_inc(S["u2_ready"], 1)

            def router_out(t, n=P):
                dve.wait_ge(S["rt_mm"], t + 1)
                dve.tensor_tensor(logits[0:n, ds(t, 1), :].rearrange("p a r -> p (a r)"), bank[6][0:n, 0:NR], b_rt[0:n, :],
                                  ALU.add).then_inc(S["rt_ok"], 1)

            o.did(dve.memset(logits, 0.0))
            prompt_rows = (row_tiles[:, 0, :], row_tiles[:, 3, :], row_tiles[:, 4, :])
            sample_rows = (row_tiles_s[:, 0, :], row_tiles_s[:, 1, :], row_tiles_s[:, 2, :])
            for b in range(2):
                ln_in(b, b, P, prompt_rows, 1, True)
                ln_out(b, b, P, prompt_rows, 1, True)
            with dve.Fori(1, NT // 2) as j:
                o.enter(j, 1, LN_STEPS)
                for b in range(2):
                    ln_in(2 * j + b, b, P, prompt_rows, j + 1, False)
                    ln_out(2 * j + b, b, P, prompt_rows, j + 1, False)
                    router_out(2 * j + b - 2)
            o.leave(NT // 2 - 1)
            dve.wait_ge(S["tiles_s_in"], 16 * 3 * DEC_B)
            ln_in(NT - 1, 0, NS, sample_rows, NT // 2 + 1, False)
            ln_out(NT - 1, 0, NS, sample_rows, NT // 2 + 1, False)
            router_out(NT - 3)
            router_out(NT - 2)
            router_out(NT - 1, NS)
            dve.wait_ge(S["rt_ok"], NT)

            bc = lambda v, n: v.unsqueeze(2).to_broadcast([P, v.shape[1], n])
            gl, el = logits[:, :, 0:NGR], logits[:, :, NGR:NR]
            hot_g, hot_1, hot_2, esel, f4 = rt_f[0], rt_f[1], rt_f[2], rt_f[3], rt_f[4]
            gm, m1, m2, mx = r17[0], r17[1], r17[2], r17[3]

            def first_max(v, top, hot):
                o.step(dve.tensor_reduce(top, v, axis=AX, op=ALU.max))
                o.step(dve.tensor_tensor(f4, v, bc(top, EPG), ALU.is_equal))
                o.step(dve.tensor_tensor(f4, f4, prio[:].unsqueeze(1).to_broadcast([P, NT, EPG]), ALU.mult))
                o.step(dve.tensor_reduce(mx, f4, axis=AX, op=ALU.max))
                o.step(dve.tensor_tensor(hot, f4, bc(mx, EPG), ALU.is_equal))

            dve.wait_ge(S["consts"], 4)
            first_max(gl, gm, hot_g)
            prod, e1, e2, both, rank, base = rt[0], rt[1], rt[2], rt[3], rt[4], rt[5]
            g4 = lambda v: v.rearrange("p t (g e) -> p t g e", g=NGR)
            over_e = hot_g.unsqueeze(3).to_broadcast([P, NT, NGR, EPG])
            o.step(dve.tensor_tensor(g4(prod), g4(el), over_e, ALU.mult))
            o.step(dve.tensor_reduce(esel, prod.rearrange("p t (g e) -> p t e g", g=NGR), axis=AX, op=ALU.add))
            first_max(esel, m1, hot_1)
            o.step(dve.scalar_tensor_tensor(esel, hot_1, -BIG, esel, ALU.mult, ALU.add))
            first_max(esel, m2, hot_2)
            o.step(dve.tensor_tensor(hot_g, hot_g, bc(valid[:], NGR), ALU.mult))
            for e_hot, hot in ((e1, hot_1), (e2, hot_2)):
                o.step(dve.tensor_tensor(g4(e_hot), over_e, hot.unsqueeze(2).to_broadcast([P, NT, NGR, EPG]), ALU.mult))
            dve.tensor_tensor(both, e1, e2, ALU.add).then_inc(S["m_ready"], 1)
            o.did(dve.tensor_tensor(rt_f[8], gl, bc(gm, NGR), ALU.subtract))
            dve.tensor_tensor(r17[4], m2, m1, ALU.subtract).then_inc(S["w_exp"], 1)
            dve.wait_ge(S["cnt_mm"], 2)
            tot = bank[1][:, 0:NT * NE].rearrange("p (t e) -> p t e", e=NE)
            o.step(dve.memset(base[:, 0, :], 0.0))
            n_e, slots_n, start_e, end_e = e16[0], e16[1], e16[2], e16[3]
            for t in range(NT):
                dst = base[:, t + 1, :] if t + 1 < NT else n_e
                o.step(dve.tensor_tensor(dst, base[:, t, :], tot[:, t, :], ALU.add))
            o.step(dve.tensor_tensor(rank, bank[0][:, 0:NT * NE].rearrange("p (t e) -> p t e", e=NE), base, ALU.add))
            o.step(dve.tensor_tensor(big_t, bc(n_e, NT), iota17[:].unsqueeze(1).to_broadcast([P, NE, NT]), ALU.is_gt))
            o.step(dve.tensor_reduce(slots_n, big_t, axis=AX, op=ALU.add))
            o.step(dve.tensor_scalar(slots_n, slots_n, 1.0, None, ALU.max))
            o.step(dve.tensor_tensor(lt_prod, lt16[:], slots_n.unsqueeze(1).to_broadcast([P, NE, NE]), ALU.mult))
            o.step(dve.tensor_reduce(start_e, lt_prod, axis=AX, op=ALU.add))
            o.step(dve.tensor_tensor(end_e, start_e, slots_n, ALU.add))
            o.did(dve.tensor_copy(end_i[:], end_e))
            o.step(dve.tensor_tensor(slot_ge, bc(iota_s[:], NE), end_e.unsqueeze(1).to_broadcast([P, SLOTS, NE]), ALU.is_ge))
            o.step(dve.tensor_reduce(slot_e[:], slot_ge, axis=AX, op=ALU.add))
            o.step(dve.tensor_scalar(slot_ei[:, 0, :], slot_e[:], float(NE - 1), None, ALU.min))
            o.step(dve.tensor_scalar(slot_ei[:, 1, :], slot_ei[:, 0, :], 1, None, ALU.bitwise_and))
            o.step(dve.tensor_scalar(e16[4], start_e, float(P), None, ALU.mult))
            o.step(dve.tensor_tensor(rank, rank, e16[4].unsqueeze(1).to_broadcast([P, NT, NE]), ALU.add))
            o.step(dve.tensor_scalar(r17[5], valid[:], -8192.0, 8192.0, ALU.mult, ALU.add))
            for k, e_hot in enumerate((e1, e2)):
                o.step(dve.tensor_tensor(prod, e_hot, rank, ALU.mult))
                o.step(dve.tensor_reduce(r17[6], prod, axis=AX, op=ALU.add))
                o.step(dve.tensor_tensor(pos_a[:, k, :], r17[6], r17[5], ALU.add))
            o.step(dve.tensor_scalar(pos_b[:], pos_a[:], 7, None, ALU.arith_shift_right))
            o.did(dve.tensor_scalar(pos_a[:], pos_a[:], P - 1, None, ALU.bitwise_and))
            o.step(dve.tensor_copy(pos_f[:, 2:4, :], pos_b[:]))
            o.step(dve.tensor_copy(pos_f[:, 0:2, :], pos_a[:]))
            o.did(dve.scalar_tensor_tensor(pos_i[:], pos_f[:, 0:2, :], float(SLOTS), pos_f[:, 2:4, :], ALU.mult, ALU.add))
            o.step(dve.tensor_scalar(r17[7], iota17[:], 1.0 / P, None, ALU.mult))
            with dve.Fori(0, NT) as t:
                o.enter(t, 0, 4)
                for k in range(2):
                    dve.wait_ge(S["hot_used"], 2 * t + k)
                    o.did(dve.tensor_scalar(hot_a[k], iota_r[:], pos_f[:, k, ds(t, 1)], None, ALU.is_equal))
                    o.did(dve.tensor_scalar(hot_b[k][:, 0:SLOTS], iota_s[:], pos_f[:, 2 + k, ds(t, 1)], r17[7][:, ds(t, 1)],
                                            ALU.is_equal, ALU.mult))
                    dve.tensor_scalar(hot_b[k][:, SLOTS:2 * SLOTS], iota_s[:], pos_f[:, 2 + k, ds(t, 1)], part_i[:, 0:1],
                                      ALU.is_equal, ALU.mult).then_inc(S["hot_ready"], 1)
            o.leave(NT)
            dve.wait_ge(S["idx_mm"], 1)
            o.step(dve.tensor_copy(slot_ge[:, 0:6, :].rearrange("p a b -> p (a b)"), bank[2][:, 0:2 * SLOTS]))
            lo_hi = slot_ge[:, 0:6, :].rearrange("p a b -> p (a b)")
            dve.scalar_tensor_tensor(tok_i[:], lo_hi[:, 0:SLOTS], float(P), lo_hi[:, SLOTS:2 * SLOTS], ALU.mult, ALU.add).then_inc(S["idx_ready"], 1)
            dve.wait_ge(S["w_expd"], 2)
            o.step(dve.tensor_reduce(r17[8], rt_f[8], axis=AX, op=ALU.add))
            o.did(dve.tensor_scalar(r17[9], r17[4], 1.0, None, ALU.add))
            o.wait()
            o.step(dve.tensor_tensor(r17[8], r17[8], r17[9], ALU.mult))
            o.step(dve.reciprocal(wgt[:, 0, :], r17[8]))
            o.did(dve.tensor_tensor(wgt[:, 1, :], wgt[:, 0, :], r17[4], ALU.mult))

            def x_evac(s):
                dve.wait_ge(S["xgT_mm"], 2 * s + 2)
                dve.tensor_copy(xT[:, 4:8, :], bank[1][:, :].rearrange("p (k n) -> p k n", n=P)).then_inc(S["xT_dve"], 1)

            def hidden(s, b):
                dve.wait_ge(S["sil_ok"], s + 1)
                dve.tensor_tensor(hid, sil, bank[2 + b][:, F:2 * F], ALU.mult).then_inc(S["hid_ok"], 1)

            def y_evac(s, b, before=None):
                dve.wait_ge(S["dn_mm"], s + 1)
                if before is not None:
                    dve.wait_ge(S[f"ys{b}"], 16 * before)
                dve.tensor_copy(y_sb[b][:, 512:1024], bank[6][:, :]).then_inc(S["y_dve"], 1)

            x_evac(0)
            hidden(0, 0)
            x_evac(1)
            for s in (1, 2):
                hidden(s, s % 2)
                x_evac(s + 1)
                y_evac(s - 1, (s - 1) % 2)
            with dve.Fori(1, SLOTS // 2 - 1) as j:
                for b in range(2):
                    s = 2 * j + 1 + b
                    hidden(s, 1 - b)
                    x_evac(s + 1)
                    y_evac(s - 1, b, j)
            s = SLOTS - 1
            hidden(s, 1)
            y_evac(s - 1, 0, SLOTS // 2 - 1)
            y_evac(s, 1, SLOTS // 2 - 1)

            dve.wait_ge(S["fin_in"], 48)
            o.wait()

            def fin(t, b, n, gate2, uses, before):
                dve.wait_ge(S["ya_scaled"], t + 1)
                dve.wait_ge(S[f"yb{b}"], 16 * uses)
                o.step(dve.scalar_tensor_tensor(ya[b][0:n, :], yb[b][0:n, :], wgt[0:n, 1, ds(t, 1)], ya[b][0:n, :], ALU.mult, ALU.add))
                o.step(dve.tensor_tensor(ya[b][0:n, :], ya[b][0:n, :], gate2[0:n, :], ALU.mult))
                dve.wait_ge(S[f"xo{b}"], 16 * uses)
                o.step(dve.scalar_tensor_tensor(ya[b][0:n, :], xo[b][0:n, :], ALPHA, ya[b][0:n, :], ALU.mult, ALU.add))
                stats(b, n, ya[b], S["fvar_ready"], S["fsd_ready"], t)
                dve.wait_ge(S["fnorm"], t + 1)
                if before is not None:
                    dve.wait_ge(S[f"os{b}"], 16 * before)
                dve.tensor_tensor(oo[b][0:n, :], ya[b][0:n, :], fin_tiles[0:n, 1, :], ALU.mult).then_inc(S["fg_ok"], 1)
                dve.wait_ge(S["fg_ok"], t + 1)
                dve.tensor_tensor(oo[b][0:n, :], oo[b][0:n, :], fin_tiles[0:n, 2, :], ALU.add).then_inc(S["fo_ok"], 1)

            for b in range(2):
                fin(b, b, P, fin_tiles[:, 0, :], 1, None)
            with dve.Fori(1, NT // 2) as j:
                o.enter(j, 1, FIN_STEPS)
                for b in range(2):
                    fin(2 * j + b, b, P, fin_tiles[:, 0, :], j + 1, j)
            o.leave(NT // 2 - 1)
            dve.wait_ge(S["fin_s_in"], 16 * DEC_B)
            fin(NT - 1, 0, NS, fin_tile_s, NT // 2 + 1, NT // 2)

        @block.tensor
        def _(pe):
            def turn(out, in_, rows):
                return pe.transpose(out, in_, ident[0:rows, 0:rows])

            pe.wait_ge(S["consts"], 1)
            pe.wait_ge(S["c_in"], 32)
            for k in range(KD):
                last = turn(bank[6][:, k * NM:(k + 1) * NM], c_rows[0:NM, k * P:(k + 1) * P], NM)
            last.then_inc(S["cT_mm"], 1)
            pe.wait_ge(S["vec_in"], 96)
            for g in range(NG):
                last = turn(bank[7][:, g * NV:(g + 1) * NV], row_v[0:NV, g * P:(g + 1) * P], NV)
            last.then_inc(S["vec_mm"], 1)
            pe.wait_ge(S["cT_ok"], 1)

            def ada(j, first=False):
                for n in range(3):
                    pe.wait_ge(S[f"ada{n}"], 16 * (j + 1))
                    if not first:
                        pe.wait_ge(S["ada_ok"], 3 * j + n - 2)
                    for k in range(KD):
                        last = pe.matmul(bank[n][0:NM, :], cT[:, k, :], w_ada[n][:, k, :], start=k == 0, stop=k == KD - 1)
                    last.then_inc(S["ada_mm"], 1)

            ada(0, first=True)
            with pe.Fori(1, 4) as j:
                ada(j)
            pe.wait_ge(S["mod_ok"], 1)
            for k in range(2 * KD):
                last = turn(bank[6][:, k * NM:(k + 1) * NM], mod[0:NM, k * P:(k + 1) * P], NM)
            last.then_inc(S["modT_mm"], 1)
            pe.wait_ge(S["st_in"], 48)
            for g in range(NG):
                turn(bank[4][:, g * 120:(g + 1) * 120], row_a[0:120, g * P:(g + 1) * P], 120)
                turn(bank[5][:, g * 24:(g + 1) * 24], row_b[0:24, g * P:(g + 1) * P], 24)
                last = turn(bank[5][:, 128 + g * DEC_B:128 + (g + 1) * DEC_B], row_c[0:DEC_B, g * P:(g + 1) * P], DEC_B)
            last.then_inc(S["st_mm"], 1)
            pe.wait_ge(S["xs_loaded"], 16)
            for k in range(KD):
                last = turn(bank[7][:, k * NS:(k + 1) * NS], xs[0:NS, k * P:(k + 1) * P], NS)
            last.then_inc(S["xsT_mm"], 1)
            pe.wait_ge(S["w_in_in"], 16)
            pe.wait_ge(S["gates_in"], 64)
            pe.wait_ge(S["wpool_in"], 16)

            def project(i, m, order, src, n, wait_k=None):
                for k in range(KD):
                    if wait_k is not None:
                        pe.wait_ge(S["uT_ready"], wait_k + k + 1)
                    last = pe.matmul(bank[2 + order % 2][:, 0:n], w_in[:, k, m * P:(m + 1) * P], src[:, k, 0:n],
                                     start=k == 0, stop=k == KD - 1)
                last.then_inc(S["proj_ready"], 1)

            def mixers(i, src, n, first, prompt):
                for order in range(2 * NG):
                    if not (first and order < 2):
                        pe.wait_ge(S["proj_evac"], 12 * i + order - 1)
                    m = NG + order if order < NG else order - NG
                    project(i, m, order, src, n, 8 * i if prompt and order == 0 else None)
                for j in range(NG):
                    pe.wait_ge(S["xc_ready"], NG * i + j + 1)
                    for q, w in ((0, wa), (1, wx)):
                        if not (first and j == 0):
                            pe.wait_ge(S["gates_evac"], 2 * NG * i + 2 * j + q - 1)
                        pe.matmul(bank[4 + q][:, 0:n], w[:, j, :], xc[:, j, 0:n], start=True, stop=True).then_inc(S["gates_mm"], 1)
                for j in range(NG):
                    pe.wait_ge(S["proj_evac"], 12 * i + 2 * NG + j - 1)
                    project(i, 2 * NG + j, j, src, n)
                for g in range(NG):
                    pe.wait_ge(S["d_ready"], NG * i + g + 1)
                    if not (first and g < 2):
                        pe.wait_ge(S["pool_evac"], NG * i + g - 1)
                    pe.matmul(bank[6 + g % 2][:, 0:n], wp[:, g, :], dif[:, g % 2, 0:n], start=True, stop=True).then_inc(S["pool_mm"], 1)

            def chunk(i, first=False):
                pe.wait_ge(S["x_loaded"], 16 * (i + 1))
                for k in range(KD):
                    if not (first and k < 2):
                        pe.wait_ge(S["uT_ready"], 8 * i + k - 1)
                    for t in range(TPC):
                        last = turn(bank[k % 2][:, t * P:(t + 1) * P], xin[:, t, k * P:(k + 1) * P], P)
                    last.then_inc(S["xT_ready"], 1)
                mixers(i, uT, C, first, True)

            chunk(0, first=True)
            with pe.Fori(1, NCH) as i:
                chunk(i)
            pe.wait_ge(S["uTs_ready"], 1)
            mixers(NCH, uTs, NS, False, False)
            pe.wait_ge(S["prj_copied"], 1)
            outs = [(lambda g: p_buf[:, g, 0:PB], PB), (lambda g: xr_buf[:, g, 0:CB], CB), None,
                    (lambda g: prj_s[:, g, :], NS), (lambda g: prj_s[:, NG + g, :], NS), (lambda g: h0_s[:, g, :], DEC_B)]
            for n, what in enumerate(outs):
                if n >= 2:
                    pe.wait_ge(S["out_evac"], n - 1)
                if what is None:
                    last = pe.transpose(bank[n % 2][0:NG, 0:P], h_last[:], ident[:])
                else:
                    for g in range(NG):
                        last = pe.transpose(bank[n % 2][0:what[1], g * P:(g + 1) * P], what[0](g), ident[:])
                last.then_inc(S["out_mm"], 1)

            pe.wait_ge(S["w_out_in"], 16)
            pe.wait_ge(S["out_evac"], 6)
            pe.wait_ge(S["rt_in"], 64)

            def out_proj(t, b, uses, n=P, first=False):
                pe.wait_ge(S[f"yTt{b}"], 16 * uses)
                if not first:
                    pe.wait_ge(S["mix_used"], t - 1)
                for h in range(2):
                    for k in range(KD):
                        last = pe.matmul(bank[2 * b + h][0:n, :], yTt[b][:, k, 0:n], w_out[:, k, 512 * h:512 * h + 512],
                                         start=k == 0, stop=k == KD - 1)
                last.then_inc(S["mix_ready"], 1)

            def router(t, b, n=P, first=False):
                pe.wait_ge(S["u2_ready"], t + 1)
                for h in range(2):
                    if not first:
                        pe.wait_ge(S["u2T_ok"], 2 * t + h - 1)
                    for k in range(4):
                        last = turn(bank[4 + h][:, k * P:k * P + n], u2[b][0:n, (4 * h + k) * P:(4 * h + k + 1) * P], n)
                    last.then_inc(S["u2T_mm"], 1)
                pe.wait_ge(S["u2T_ok"], 2 * t + 2)
                if not first:
                    pe.wait_ge(S["rt_ok"], t)
                for k in range(KD):
                    last = pe.matmul(bank[6][0:n, 0:NR], u2T[:, k, 0:n], w_rt[:, k, :], start=k == 0, stop=k == KD - 1)
                last.then_inc(S["rt_mm"], 1)

            out_proj(0, 0, 1, first=True)
            out_proj(1, 1, 1, first=True)
            out_proj(2, 0, 2)
            router(0, 0, first=True)
            out_proj(3, 1, 2)
            router(1, 1)
            with pe.Fori(2, NT // 2) as j:
                for b in range(2):
                    out_proj(2 * j + b, b, j + 1)
                    router(2 * j + b - 2, b)
            out_proj(NT - 1, 0, NT // 2 + 1, NS)
            router(NT - 3, 0)
            router(NT - 2, 1)
            router(NT - 1, 0, NS)
            pe.wait_ge(S["m_ready"], 1)
            m_all = rt[3].rearrange("p t e -> p (t e)")
            pe.matmul(bank[0][:, 0:NT * NE], tri[:], m_all, start=True, stop=True).then_inc(S["cnt_mm"], 1)
            pe.matmul(bank[1][:, 0:NT * NE], ones[:], m_all, start=True, stop=True).then_inc(S["cnt_mm"], 1)

            def dispatch(t, start, stop):
                for k in range(2):
                    pe.wait_ge(S["hot_ready"], 2 * t + k + 1)
                    last = pe.matmul(bank[2][:, 0:2 * SLOTS], hot_a[k], hot_b[k], start=start and k == 0, stop=stop and k == 1)
                    last.then_inc(S["hot_used"], 1)
                return last

            dispatch(0, True, False)
            with pe.Fori(1, NT - 1) as t:
                dispatch(t, False, False)
            dispatch(NT - 1, False, True)
            pe.wait_ge(S["hot_used"], 2 * NT + 0)
            turn(bank[7][0:2, 0:2], ident[0:2, 0:2], 2).then_inc(S["idx_mm"], 1)

            pe.wait_ge(S["idx_ready"], 1)

            def turn_x(s, b, uses, first=False):
                pe.wait_ge(S[f"xg{b}"], 16 * uses)
                for h in range(2):
                    if not first:
                        pe.wait_ge(S["xT_act" if h == 0 else "xT_dve"], s)
                    for k in range(4):
                        last = turn(bank[h][:, k * P:(k + 1) * P], xg[b][:, (4 * h + k) * P:(4 * h + k + 1) * P], P)
                    last.then_inc(S["xgT_mm"], 1)

            def gate_up(s, b):
                e = pe.value_load(slot_ei[0:1, 0, ds(s, 1)], min_val=0, max_val=NE - 1)
                buf = pe.value_load(slot_ei[0:1, 1, ds(s, 1)], min_val=0, max_val=1)
                pe.wait_ge(S["xT_act"], s + 1)
                pe.wait_ge(S["xT_dve"], s + 1)
                pe.wait_ge(S["w_exp_in"], e * 48 + 48)
                for k in range(KD):
                    last = pe.matmul(bank[2 + b][:, :], xT[:, k, :],
                                     w_gu2[:, ds(buf, 1), k * 2 * F:(k + 1) * 2 * F].rearrange("p a n -> p (a n)"),
                                     start=k == 0, stop=k == KD - 1)
                last.then_inc(S["gu_mm"], 1)
                return buf

            def turn_h(s):
                pe.wait_ge(S["hid_ok"], s + 1)
                for k in range(F // P):
                    last = turn(bank[4][:, k * P:(k + 1) * P], hid[:, k * P:(k + 1) * P], P)
                last.then_inc(S["hT_mm"], 1)

            def down(s, first=False):
                buf = pe.value_load(slot_ei[0:1, 1, ds(s, 1)], min_val=0, max_val=1)
                pe.wait_ge(S["hT_ok"], s + 1)
                if not first:
                    pe.wait_ge(S["y_act"], s)
                    pe.wait_ge(S["y_dve"], s)
                for h in range(2):
                    for k in range(F // P):
                        off = KD * 2 * F + k * D + 512 * h
                        last = pe.matmul(bank[5 + h][:, :], hT[:, k, :],
                                         w_gu2[:, ds(buf, 1), off:off + 512].rearrange("p a n -> p (a n)"),
                                         start=k == 0, stop=k == F // P - 1)
                last.then_inc(S["dn_mm"], 1)

            turn_x(0, 0, 1, first=True)
            gate_up(0, 0)
            turn_x(1, 1, 1)
            turn_h(0)
            for s in (1, 2):
                gate_up(s, s % 2)
                turn_x(s + 1, (s + 1) % 2, (s + 1) // 2 + 1)
                down(s - 1, first=s == 1)
                turn_h(s)
            with pe.Fori(1, SLOTS // 2 - 1) as j:
                for b in range(2):
                    s = 2 * j + 1 + b
                    gate_up(s, 1 - b)
                    turn_x(s + 1, b, j + 2 if b else j + 2)
                    down(s - 1)
                    turn_h(s)
            s = SLOTS - 1
            gate_up(s, 1)
            down(s - 1)
            turn_h(s)
            down(s)


CHUNK_STEPS = 66
LN_STEPS = 14
FIN_STEPS = 14

_INS = ['x_prompt', 'x_sample', 'c_prompt', 'c_sample', 'state_pool', 'state_conv', 'state_lru', 'w_ada', 'b_ada', 'w_in',
        'w_pool', 'pool_scale', 'w_conv', 'b_conv', 'w_a', 'b_a', 'w_x', 'b_x', 'lru_lambda', 'w_out', 'ln1_g', 'ln1_b',
        'w_group', 'b_group', 'w_route', 'b_route', 'w_gate', 'w_up', 'w_down', 'ln2_g', 'ln2_b']
_OUTS = [(1, SEQ, D), (DEC_B, DEC_T, D), (1, 1, PB, DH), (1, 1, CB, DH), (1, 1, DH),
         (1, DEC_B, PB, DH), (1, DEC_B, CB, DH), (1, DEC_B, DH)]


def kernel(**inputs):
    import numpy as _np
    import concourse.bacc as _bacc
    from concourse.bass_utils import run_bass_kernel_spmd as _run

    nc = _bacc.Bacc("TRN2", target_bir_lowering=False, num_devices=1)
    arrays, aps = {}, {}
    for name in _INS:
        a = _np.ascontiguousarray(inputs[name])
        arrays[f"in_{name}"] = a
        aps[name] = nc.dram_tensor(f"in_{name}", a.shape, mybir.dt.from_np(a.dtype), kind="ExternalInput").ap()
    for i, shape in enumerate(_OUTS):
        aps[f"out_{i}"] = nc.dram_tensor(f"result_{i}", shape, F32, kind="ExternalOutput").ap()
    build(nc, aps)
    r = _run(nc, [arrays], core_ids=[0])
    return tuple(r.results[0][f"result_{i}"] for i in range(len(_OUTS)))
```

```python
from contextlib import ExitStack

import concourse.bass as bass
from concourse import mybir

P = 128
D = 1024
KD = D // P
SEQ, DEC_B, DEC_T = 2048, 8, 8
NS = DEC_B * DEC_T
NTOK = SEQ + NS
C = 512
NCH = SEQ // C
TPC = C // P
NT = SEQ // P + 1
DH = 512
NG = DH // P
PB, CB = 15, 3
WINDOWS = (2, 4, 8, 16)
NM = DEC_B + 1
NE, NGR, EPG, F = 16, 4, 4, 256
GU, DN = KD * 2 * F, (F // P) * D
WE = GU + DN
SPLIT = 1024
GU_PARTS, DN_PARTS = GU // SPLIT, DN // SPLIT
E_PARTS = GU_PARTS + DN_PARTS
HI_LO = 4 * WE + 2 * KD * P + 2 * F
ARENA = 49840
NR = NGR + NE
SLOTS = (2 * NTOK + NE * P - 1) // P
ALPHA = 2.0 ** 0.25
LN_EPS = 1e-5
LRU_C = 8.0
BIG = 3.0e38

ALU = mybir.AluOpType
ACT = mybir.ActivationFunctionType
F32 = mybir.dt.float32
BF16 = mybir.dt.bfloat16
F32R = mybir.dt.float32r
I32 = mybir.dt.int32
AX = mybir.AxisListType.X
ds = bass.ds

SH1, SC1, G1, SH2, SC2, G2 = (n * D for n in range(6))
V_BCONV, V_BA, V_BX, V_LAM, V_PSCALE, V_WCONV = 0, 1, 2, 3, 4, 5
NV = 9


class Order:

    def __init__(self, eng, sem):
        self.eng, self.sem, self.base, self.n = eng, sem, 0, 0

    def did(self, ins):
        ins.then_inc(self.sem, 1)
        self.n += 1

    def wait(self):
        self.eng.wait_ge(self.sem, self.base + self.n)

    def step(self, ins):
        self.did(ins)
        self.wait()

    def enter(self, i, first, per):
        self.entry, self.per, self.first = self.base + self.n, per, first
        self.base, self.n = self.entry + (i - first) * per, 0

    def leave(self, trips):
        assert self.n == self.per, f"the loop's body counts {self.n}"
        self.base, self.n = self.entry + trips * self.per, 0


def build(nc, A):
    with ExitStack() as ctx:
        def sb(name, shape, dt=F32):
            return ctx.enter_context(nc.sbuf_tensor(name, shape, dt))

        def sem(name):
            return ctx.enter_context(nc.semaphore(name))

        bank = [ctx.enter_context(nc.psum_tensor(f"bank{n}", [P, 512], F32)) for n in range(8)]

        mod_d = nc.dram_tensor("mod_d", [NM, 6 * D], F32).ap()
        yT_d = nc.dram_tensor("yT_d", [NT, P, KD, P], F32).ap()
        x1_d = nc.dram_tensor("x1_d", [NTOK, D], F32).ap()
        u2_d = nc.dram_tensor("u2_d", [NTOK, D], F32).ap()
        ys_d = nc.dram_tensor("ys_d", [P * SLOTS, D], F32).ap()

        def place(arena, off, *shape):
            n = 1
            for s in shape:
                n *= s
            v = arena[:, off:off + n]
            if len(shape) == 2:
                v = v.rearrange("p (a b) -> p a b", b=shape[1])
            if len(shape) == 3:
                v = v.rearrange("p (a b c) -> p a b c", b=shape[1], c=shape[2])
            return v

        with nc.sbuf_tensor("mixer_arena", [P, ARENA], F32) as mixer_arena:
            arena = mixer_arena[:, :]
        expert_arena = sb("expert_arena", [P, ARENA - HI_LO])
        w_hi = sb("w_hi", [P, 2, WE], F32R)
        w_lo = sb("w_lo", [P, 2, WE], F32R)
        xT_hi, xT_lo = sb("xT_hi", [P, KD, P], F32R), sb("xT_lo", [P, KD, P], F32R)
        hT_hi, hT_lo = sb("hT_hi", [P, F // P, P], F32R), sb("hT_lo", [P, F // P, P], F32R)

        def at(off, *shape):
            return place(arena, off, *shape)

        def ex(off, *shape):
            return place(expert_arena, off, *shape)

        w_in = at(0, KD, 3 * DH)
        xin = at(12288, TPC, D)
        uT = at(16384, KD, C)
        p_buf = at(20480, NG, PB + C)
        xr_buf = at(22592, NG, CB + C)
        xc = at(24656, NG, C)
        gel = at(26704, NG, C)
        tT = at(28752, NG, C)
        tI = at(30800, NG, C)
        tS = at(32848, NG, C)
        q_t, a_t, b_t, h_t = at(34896, C), at(35408, C), at(35920, C), at(36432, C)
        wsum = [at(36944, PB + C), at(37472, PB + C)]
        dif = at(38000, 2, C)
        yT = at(39024, KD, C)
        wa, wx, wp = at(43120, NG, P), at(43632, NG, P), at(44144, NG, P)
        xs = at(44656, D)
        uTs = at(45680, KD, NS)
        p_s = arena[:, 46192:46192 + NG * DEC_B * (PB + DEC_T)].rearrange(
            "p (g s t) -> p g s t", g=NG, s=DEC_B)
        xr_s = arena[:, 46928:46928 + NG * DEC_B * (CB + DEC_T)].rearrange("p (g s t) -> p g s t", g=NG, s=DEC_B)
        prj_s = at(47280, 2 * NG, NS)
        row_a, row_b, row_c, row_v = at(48304, DH), at(48816, DH), at(49328, DH), at(47792, DH)
        row_d, row_e = at(38000, DH), at(38512, DH)
        w_ada = [at(20480 + n * 4096, KD, 512) for n in range(3)]
        mod = at(32768, 6 * D)
        c_rows = at(39024, D)
        w_out = at(12288, KD, D)
        yTt = [at(n * 1024, KD, P) for n in range(2)]
        xres = [at(2048 + n * 1024, D) for n in range(2)]
        z = [at(4096 + n * 1024, D) for n in range(2)]
        x1 = [at(6144 + n * 1024, D) for n in range(2)]
        u2 = [at(8192 + n * 1024, D) for n in range(2)]
        u2T = at(10240, KD, P)
        w_rt = at(11264, KD, NR)
        b_rt = at(11424, NR)
        row_tiles = at(44656, 5, D)
        row_tiles_s = at(20480, 3, D)
        w_raw = [ex(n * 12288, WE) for n in (1, 0)]
        w_gu = [w[:, 0:GU].rearrange("p (k n) -> p k n", k=KD) for w in w_raw]
        w_dn = [w[:, GU:WE].rearrange("p (k n) -> p k n", k=F // P) for w in w_raw]
        w_raw2 = expert_arena[:, 0:2 * 12288 - 6144].rearrange("p (a n) -> p a n", n=6144)
        xg = [ex(6144 + n * 1024, D) for n in range(2)]
        y_sb = [ex(8192 + n * 1024, D) for n in range(2)]
        hid, sil = ex(10240, F), ex(10496, F)
        ya = [ex(n * 1024, D) for n in range(2)]
        yb = [ex(2048 + n * 1024, D) for n in range(2)]
        xo = [ex(12288 + n * 1024, D) for n in range(2)]
        oo = [ex(14336 + n * 1024, D) for n in range(2)]
        z2 = [ex(16384 + n * 1024, D) for n in range(2)]
        dg = [ex(10752 + n * 256, 2, P) for n in range(2)]
        fin_tiles = ex(18432, 3, D)
        fin_tile_s = ex(21504, D)
        rt = [ex(n * 272, NT, NE) for n in range(6)]
        rt_f = [ex(1632 + n * 68, NT, NGR) for n in range(9)]
        r17 = [ex(2248 + n * NT, NT) for n in range(10)]
        big_t = ex(2424, NE, NT)
        lt_prod = ex(2700, NE, NE)
        slot_ge = ex(2960, SLOTS, NE)
        hot_a = [ex(3730 + n * 64, 64).bitcast(BF16) for n in range(2)]
        hot_b = [ex(3860 + n * SLOTS, SLOTS).bitcast(BF16) for n in range(2)]
        e48 = [ex(4050 + n * SLOTS, SLOTS) for n in range(2)]
        e16 = [ex(3960 + n * NE, NE) for n in range(5)]

        logits = sb("logits", [P, NT, NR])
        ident = sb("ident", [P, P])
        tri = sb("tri", [P, P])
        ones = sb("ones", [P, P])
        cT = sb("cT", [P, KD, NM])
        modT = sb("modT", [P, 2 * KD, NM])
        vecT = sb("vecT", [P, NG, NV])
        sp_t = sb("sp_t", [P, 5, NG])
        sp2 = sb("sp2", [P, NG])
        half_b = sb("half_b", [P, NG, 2])
        inv_cnt = sb("inv_cnt", [P, NG, 16])
        fix = sb("fix", [P, 16])
        h_last = sb("h_last", [P, NG])
        h0_s = sb("h0_s", [P, NG, DEC_B])
        st6 = [sb(f"st6_{n}", [P, 2, 6]) for n in range(2)]
        mv = [sb(f"mv{n}", [P, 2]) for n in range(2)]
        sd = [sb(f"sd{n}", [P, 1]) for n in range(2)]
        rs = [sb(f"rs{n}", [P, 2]) for n in range(2)]
        prio = sb("prio", [P, EPG])
        lt16 = sb("lt16", [P, NE, NE])
        iota17 = sb("iota17", [P, NT])
        iota_s = sb("iota_s", [P, SLOTS])
        iota_r = sb("iota_r", [P, P])
        part_i = sb("part_i", [P, 1])
        valid = sb("valid", [P, NT])
        wgt = sb("wgt", [P, 2, NT])
        pos_i = sb("pos_i", [P, 2, NT], I32)
        pos_a = sb("pos_a", [P, 2, NT], I32)
        pos_b = sb("pos_b", [P, 2, NT], I32)
        pos_f = sb("pos_f", [P, 4, NT])
        tok_i = sb("tok_i", [P, SLOTS], I32)
        slot_e = sb("slot_e", [P, SLOTS])
        slot_ei = sb("slot_ei", [P, 2, SLOTS], I32)
        tok_now = [sb(f"tok_now{n}", [P, 1], I32) for n in range(2)]
        pos_now = [sb(f"pos_now{n}", [P, 2], I32) for n in range(2)]
        spare = sb("spare", [1, 2])
        hP = sb("hP", [NG, P])

        S = {n: sem(n) for n in """consts small_in c_in vec_in ba_in gates_in gates_zero wpool_in st_in x_loaded xs_loaded w_in_in
            ada0 ada1 ada2 cT_mm cT_ok ada_mm ada_ok mod_ok modT_mm modT_ok vec_mm vec_ok st_mm xsT_mm mod_stored
            dve_order act_order pool_order xT_ready uT_ready uTs_ready proj_ready proj_evac xc_ready xr_free p_free
            gates_mm gates_evac T_ready T_guard S_ready d_ready pool_mm pool_evac ylru_ready y_stored prj_copied
            out_mm out_evac out_stored out_s_stored w_out_in tiles_in tiles_s_in rt_in yTt0 yTt1 xres0 xres1 mix_ready mix_used
            var_ready sd_ready z_scaled z_norm u2_ready x1_ready x1_st0 x1_st1 u2_st0 u2_st1 u2T_mm u2T_ok rt_mm rt_ok
            m_ready cnt_mm w_exp w_expd hot_ready hot_used idx_mm idx_ready w_raw0 w_raw1 xg0 xg1 xgT_mm w_hi w_lo w0_lo xT_hi_ok xT_lo_ok
            gu_mm sil_ok hid_ok hT_mm hT_hi_ok hT_lo_ok dn_mm y_act y_dve ys0 ys1 fin_in fin_s_in ya0 ya1 yb0 yb1 xo0 xo1
            diag_ok wgt_ok comb_mm comb_used fvar_ready fsd_ready fz_ok fnorm fg_ok fo_ok os0 os1""".split()}

        block = ctx.enter_context(nc.Block())
        xp_d = A["x_prompt"].rearrange("b (c t p) d -> c p (b t) d", t=TPC, p=P)
        xpt_d = A["x_prompt"].rearrange("b (t p) d -> (b t) p d", p=P)
        xs_d = A["x_sample"].rearrange("b t d -> (b t) d")
        ada_d = A["w_ada"][0].rearrange("(k p) (g n) -> g p k n", p=P, n=512)
        yt_p, yt_s = A["out_0"].rearrange("b (t p) d -> (b t) p d", p=P), A["out_1"].rearrange("b t d -> (b t) d")
        gate_d = A["w_gate"][0].rearrange("e (k p) f -> e p k f", p=P)
        up_d = A["w_up"][0].rearrange("e (k p) f -> e p k f", p=P)
        down_d = A["w_down"][0].rearrange("e (k p) n -> e p k n", p=P)
        x1_t = x1_d[0:SEQ, :].rearrange("(t p) d -> t p d", p=P)
        u2_t = u2_d[0:SEQ, :].rearrange("(t p) d -> t p d", p=P)
        ys_t = ys_d.rearrange("(p s) d -> s p d", s=SLOTS)

        def part(w, buf, n):
            return w[:, ds(buf, 1), n * SPLIT:(n + 1) * SPLIT].rearrange("p a n -> p (a n)")

        def raw_part(buf, n):
            return w_raw2[:, ds(buf * -2 + 2, 1), n * SPLIT:(n + 1) * SPLIT].rearrange("p a n -> p (a n)")

        def all_parts(row, n=P):
            return row.rearrange("(a d) -> a d", a=1).broadcast_to([n, row.shape[0]])

        @block.sync
        def _(sp):
            sp.dma_start(c_rows[0:1, :], A["c_prompt"]).then_inc(S["c_in"], 16)
            sp.dma_start(c_rows[1:NM, :], A["c_sample"]).then_inc(S["c_in"], 16)
            for n in range(3):
                sp.dma_start(w_ada[n], ada_d[n]).then_inc(S[f"ada{n}"], 16)
            sp.dma_start(mod[0:NM, :], all_parts(A["b_ada"][0], NM)).then_inc(S["ba_in"], 16)
            for r, name in enumerate(("b_conv", "b_a", "b_x", "lru_lambda", "pool_scale")):
                sp.dma_start(row_v[r:r + 1, :], A[name]).then_inc(S["vec_in"], 16)
            sp.dma_start(row_v[V_WCONV:NV, :], A["w_conv"][0]).then_inc(S["vec_in"], 16)
            sp.dma_start(row_a[0:DEC_B * PB, :], A["state_pool"][0].rearrange("b t c -> (b t) c")).then_inc(S["st_in"], 16)
            sp.dma_start(row_b[0:DEC_B * CB, :], A["state_conv"][0].rearrange("b t c -> (b t) c")).then_inc(S["st_in"], 16)
            sp.dma_start(row_c[0:DEC_B, :], A["state_lru"][0]).then_inc(S["st_in"], 16)
            sp.dma_start(xs[0:NS, :], xs_d).then_inc(S["xs_loaded"], 16)
            with sp.Fori(1, 4) as j:
                for n in range(3):
                    sp.wait_ge(S["ada_mm"], 3 * j + n - 2)
                    sp.dma_start(w_ada[n], ada_d[ds(3 * j + n, 1)].rearrange("a p k n -> p (a k) n")).then_inc(S[f"ada{n}"], 16)
            sp.dma_start(xin, xp_d[0]).then_inc(S["x_loaded"], 16)
            sp.dma_start(w_in, A["w_in"][0].rearrange("(k p) n -> p k n", p=P)).then_inc(S["w_in_in"], 16)
            sp.wait_ge(S["gates_zero"], 1)
            for w, name in ((wa, "w_a"), (wx, "w_x")):
                heads = A[name][0].rearrange("(j q) i o -> q i j o", q=2)
                for q in range(2):
                    sp.dma_start(w[64 * q:64 * q + 64, :, 64 * q:64 * q + 64], heads[q]).then_inc(S["gates_in"], 16)
            sp.dma_start(wp, A["w_pool"][0].rearrange("g i o -> i g o")).then_inc(S["wpool_in"], 16)
            sp.dma_start(A["out_5"][0][:, 0:PB - DEC_T, :], A["state_pool"][0][:, DEC_T:PB, :]).then_inc(S["out_stored"], 16)
            sp.wait_ge(S["mod_ok"], 1)
            sp.dma_start(mod_d[:, 2 * D:6 * D], mod[0:NM, 2 * D:6 * D]).then_inc(S["mod_stored"], 16)

            def load_x(i):
                sp.wait_ge(S["xT_ready"], KD * (i - 1))
                sp.dma_start(xin, xp_d[ds(i - 1, 1)].rearrange("a p t d -> p (a t) d")).then_inc(S["x_loaded"], 16)

            def store_y(i):
                sp.wait_ge(S["pool_evac"], NG * i + NG)
                sp.wait_ge(S["ylru_ready"], NG * i + NG)
                for t in range(TPC):
                    sp.dma_start(yT_d[ds(TPC * (i - 1) + t, 1)].rearrange("a p k n -> p (a k) n"),
                                 yT[:, :, t * P:(t + 1) * P]).then_inc(S["y_stored"], 16)

            sp.wait_ge(S["pool_evac"], NG)
            sp.wait_ge(S["ylru_ready"], NG)
            sp.dma_start(yT_d[NT - 1][:, :, 0:NS], yT[:, :, 0:NS]).then_inc(S["y_stored"], 16)
            with sp.Fori(1, NCH) as i:
                load_x(i + 1)
                store_y(i)
            w_out_d = A["w_out"][0].rearrange("(k p) n -> p k n", p=P)
            sp.wait_ge(S["xT_ready"], KD * NCH)
            sp.dma_start(w_out[:, 0:KD // 2, :], w_out_d[:, 0:KD // 2, :]).then_inc(S["w_out_in"], 16)
            sp.wait_ge(S["out_evac"], 3)
            for s in range(DEC_B):
                sp.dma_start(A["out_5"][0, s, PB - DEC_T:PB, :], row_a[s * DEC_T:(s + 1) * DEC_T, :]).then_inc(S["out_s_stored"], 16)
                sp.dma_start(A["out_6"][0, s], row_b[(s + 1) * DEC_T - CB:(s + 1) * DEC_T, :]).then_inc(S["out_s_stored"], 16)
            sp.dma_start(A["out_7"][0], row_c[0:DEC_B, :]).then_inc(S["out_s_stored"], 16)
            sp.wait_ge(S["out_s_stored"], 16 * (1 + 2 * DEC_B))
            sp.wait_ge(S["mod_stored"], 16)
            for n, row in enumerate((mod_d[0, G1:G1 + D], A["ln1_g"][0], A["ln1_b"][0], mod_d[0, SC2:SC2 + D], mod_d[0, SH2:SH2 + D])):
                sp.dma_start(row_tiles[:, n, :], all_parts(row)).then_inc(S["tiles_in"], 16)
            sp.wait_ge(S["proj_ready"], 12 * NCH + 12)
            sp.dma_start(w_out[:, KD // 2:KD, :], w_out_d[:, KD // 2:KD, :]).then_inc(S["w_out_in"], 16)

            def load_rows():
                sp.dma_start(w_rt[:, :, 0:NGR], A["w_group"][0].rearrange("(k p) n -> p k n", p=P)).then_inc(S["rt_in"], 16)
                sp.dma_start(w_rt[:, :, NGR:NR], A["w_route"][0].rearrange("(k p) n -> p k n", p=P)).then_inc(S["rt_in"], 16)
                sp.dma_start(b_rt[:, 0:NGR], all_parts(A["b_group"][0])).then_inc(S["rt_in"], 16)
                sp.dma_start(b_rt[:, NGR:NR], all_parts(A["b_route"][0])).then_inc(S["rt_in"], 16)
                store_y(NCH)
                sp.wait_ge(S["out_evac"], 6)
                sp.dma_start(A["out_2"][0, 0], row_d[0:PB, :]).then_inc(S["out_stored"], 16)
                sp.dma_start(A["out_3"][0, 0], row_e[0:CB, :]).then_inc(S["out_stored"], 16)
                sp.dma_start(A["out_4"].rearrange("a b (g c) -> (a b g) c", c=P), hP[:, :]).then_inc(S["out_stored"], 16)
                for n, off in enumerate((G1, SC2, SH2)):
                    for s in range(DEC_B):
                        sp.dma_start(row_tiles_s[s * DEC_T:(s + 1) * DEC_T, n, :],
                                     all_parts(mod_d[s + 1, off:off + D], DEC_T)).then_inc(S["tiles_s_in"], 16)
                sp.wait_ge(S["y_stored"], 64 * NCH + 16)
                sp.wait_ge(S["out_stored"], 64)

            sp.wait_ge(S["y_stored"], 64 * (NCH - 1) + 16)

            def load_tile(t, b, n=P):
                src_y = yT_d[ds(t, 1)].rearrange("a p k n -> p (a k) n") if n == P else yT_d[NT - 1][:, :, 0:n]
                src_x = xpt_d[ds(t, 1)].rearrange("a p d -> (a p) d") if n == P else xs_d
                sp.dma_start(yTt[b][:, :, 0:n], src_y).then_inc(S[f"yTt{b}"], 16)
                sp.dma_start(xres[b][0:n, :], src_x).then_inc(S[f"xres{b}"], 16)

            def store_tile(t, b, n=P):
                sp.wait_ge(S["x1_ready"], t + 1)
                sp.wait_ge(S["u2_ready"], t + 1)
                dst_x = x1_t[ds(t, 1)].rearrange("a p d -> (a p) d") if n == P else x1_d[SEQ:NTOK, :]
                dst_u = u2_t[ds(t, 1)].rearrange("a p d -> (a p) d") if n == P else u2_d[SEQ:NTOK, :]
                sp.dma_start(dst_x, x1[b][0:n, :]).then_inc(S[f"x1_st{b}"], 16)
                sp.dma_start(dst_u, u2[b][0:n, :]).then_inc(S[f"u2_st{b}"], 16)

            def tile_free(t):
                sp.wait_ge(S["mix_ready"], t + 1)
                sp.wait_ge(S["mix_used"], t + 1)

            def load_expert(e, b, static=False):
                for dst, src in ((w_gu[b][:, :, 0:F], gate_d), (w_gu[b][:, :, F:2 * F], up_d), (w_dn[b], down_d)):
                    src = src[e] if static else src[ds(e, 1)].rearrange("a p k n -> p (a k) n")
                    sp.dma_start(dst, src).then_inc(S[f"w_raw{b}"], 16)

            load_tile(0, 0)
            load_tile(1, 1)
            load_rows()
            tile_free(0)
            load_tile(2, 0)
            tile_free(1)
            load_tile(3, 1)
            store_tile(0, 0)
            with sp.Fori(1, NT // 2 - 1) as j:
                for b in range(2):
                    tile_free(2 * j + b)
                    load_tile(2 * j + 2 + b, b)
                    store_tile(2 * j + b - 1, 1 - b)
            tile_free(NT - 3)
            load_tile(NT - 1, 0, NS)
            store_tile(NT - 4, 1)
            store_tile(NT - 3, 0)
            store_tile(NT - 2, 1)
            sp.wait_ge(S["mix_ready"], NT)
            load_expert(0, 0, static=True)
            store_tile(NT - 1, 0, NS)
            sp.wait_ge(S["idx_ready"], 1)
            for n, row in enumerate((mod_d[0, G2:G2 + D], A["ln2_g"][0], A["ln2_b"][0])):
                sp.dma_start(fin_tiles[:, n, :], all_parts(row)).then_inc(S["fin_in"], 16)
            for s in range(DEC_B):
                sp.dma_start(fin_tile_s[s * DEC_T:(s + 1) * DEC_T, :], all_parts(mod_d[s + 1, G2:G2 + D], DEC_T)).then_inc(S["fin_s_in"], 16)
            sp.wait_ge(S["wgt_ok"], 1)
            load_expert(1, 1, static=True)
            with sp.Fori(1, NE // 2) as j:
                for b in range(2):
                    sp.wait_ge(S["w_lo"], E_PARTS * (2 * j + b - 1))
                    load_expert(2 * j + b, b)
            sp.wait_ge(S["w_lo"], E_PARTS * (NE - 1))

            def load_x1(t, b, n=P):
                src = x1_t[ds(t, 1)].rearrange("a p d -> (a p) d") if n == P else x1_d[SEQ:NTOK, :]
                sp.dma_start(xo[b][0:n, :], src).then_inc(S[f"xo{b}"], 16)

            def store_o(t, b, n=P):
                sp.wait_ge(S["fo_ok"], t + 1)
                dst = yt_p[ds(t, 1)].rearrange("a p d -> (a p) d") if n == P else yt_s
                sp.dma_start(dst, oo[b][0:n, :]).then_inc(S[f"os{b}"], 16)

            load_x1(0, 0)
            load_x1(1, 1)
            for t in range(2):
                sp.wait_ge(S["comb_used"], t + 1)
                load_x1(t + 2, t)
            with sp.Fori(1, NT // 2 - 1) as j:
                for b in range(2):
                    sp.wait_ge(S["comb_used"], 2 * j + b + 1)
                    load_x1(2 * j + 2 + b, b)
                    store_o(2 * j + b - 2, b)
            store_o(NT - 5, 0)
            sp.wait_ge(S["comb_used"], NT - 2)
            load_x1(NT - 1, 0, NS)
            store_o(NT - 4, 1)
            store_o(NT - 3, 0)
            store_o(NT - 2, 1)
            store_o(NT - 1, 0, NS)
            sp.wait_ge(S["os0"], 16 * (NT // 2 + 1))
            sp.wait_ge(S["os1"], 16 * (NT // 2))
            sp.wait_ge(S["out_stored"], 64)

        @block.gpsimd
        def _(pool):
            o = Order(pool, S["pool_order"])
            o.did(pool.memset(ident[:], 0.0))
            o.did(pool.memset(tri[:], 1.0))
            o.did(pool.memset(lt16[:], 1.0))
            o.did(pool.memset(valid[:], 1.0))
            o.did(pool.iota(iota17[:], pattern=[[P, NT]], base=0, channel_multiplier=0, allow_small_or_imprecise_dtypes=True))
            o.did(pool.iota(iota_s[:], pattern=[[1, SLOTS]], base=0, channel_multiplier=0, allow_small_or_imprecise_dtypes=True))
            o.did(pool.iota(iota_r[:], pattern=[[1, P]], base=0, channel_multiplier=0, allow_small_or_imprecise_dtypes=True))
            o.did(pool.iota(part_i[:], pattern=[[0, 1]], base=0, channel_multiplier=1, allow_small_or_imprecise_dtypes=True))
            o.did(pool.iota(prio[:], pattern=[[-1, EPG]], base=EPG, channel_multiplier=0, allow_small_or_imprecise_dtypes=True))
            o.did(pool.memset(wa, 0.0))
            pool.memset(wx, 0.0).then_inc(S["gates_zero"], 1)
            o.did(pool.memset(ones[:], 1.0))
            o.wait()
            pool.affine_select(out=ident[:], in_=ident[:], compare_op=ALU.not_equal, fill=1.0, base=0,
                               pattern=[[-1, P]], channel_multiplier=1).then_inc(S["consts"], 1)
            pool.affine_select(out=tri[:], in_=tri[:], compare_op=ALU.is_gt, fill=0.0, base=0,
                               pattern=[[1, P]], channel_multiplier=-1).then_inc(S["consts"], 1)
            pool.affine_select(out=lt16[:], in_=lt16[:], compare_op=ALU.is_gt, fill=0.0, base=0,
                               pattern=[[1, NE], [-1, NE]], channel_multiplier=0).then_inc(S["consts"], 1)
            pool.affine_select(out=valid[:, NT - 1:NT], in_=valid[:, NT - 1:NT], compare_op=ALU.is_gt, fill=0.0, base=NS,
                               pattern=[[0, 1]], channel_multiplier=-1).then_inc(S["consts"], 1)

            pool.wait_ge(S["tiles_in"], 80)

            def x1_tile(t, b, n=P, first=False):
                pool.wait_ge(S["z_norm"], t + 1)
                if not first:
                    pool.wait_ge(S[f"x1_st{b}"], 16 * x1_tile.uses(t))
                o.step(pool.tensor_tensor(x1[b][0:n, :], z[b][0:n, :], row_tiles[0:n, 1, :], ALU.mult))
                pool.tensor_tensor(x1[b][0:n, :], x1[b][0:n, :], row_tiles[0:n, 2, :], ALU.add).then_inc(S["x1_ready"], 1)

            x1_tile.uses = lambda t: t
            for b in range(2):
                x1_tile(b, b, first=True)
            with pool.Fori(1, NT // 2) as j:
                o.enter(j, 1, 2)
                x1_tile.uses = lambda t: j
                for b in range(2):
                    x1_tile(2 * j + b, b)
            o.leave(NT // 2 - 1)
            x1_tile.uses = lambda t: NT // 2
            x1_tile(NT - 1, 0, NS)

            for n in range(E_PARTS):
                cols = slice(n * SPLIT, (n + 1) * SPLIT)
                pool.wait_ge(S["w_hi"], n + 1)
                pool.tensor_tensor(w_lo[:, 0, cols], w_raw[0][:, cols], w_hi[:, 0, cols].bitcast(F32),
                                   ALU.subtract).then_inc(S["w0_lo"], 1)
            pool.wait_ge(S["idx_ready"], 1)
            for b, n in ((0, NT // 2 + 1), (1, NT // 2)):
                pool.wait_ge(S[f"u2_st{b}"], 16 * n)

            def gather(s, b):
                o.did(pool.tensor_copy(tok_now[b][:], tok_i[:, ds(s, 1)]))
                o.wait()
                pool.tensor_tensor(spare[0:1, 1:2], ones[0:1, 0:1], ones[0:1, 0:1], ALU.mult)
                pool.indirect_dma_start(out=xg[b], out_offset=None, in_=u2_d,
                                        in_offset=bass.IndirectOffsetOnAxis(ap=tok_now[b][:, 0:1], axis=0)).then_inc(S[f"xg{b}"], 16)

            gather(0, 0)
            gather(1, 1)
            with pool.Fori(1, SLOTS // 2) as j:
                o.enter(j, 1, 2)
                for b in range(2):
                    pool.wait_ge(S["xgT_mm"], 4 * j + 2 * b - 2)
                    gather(2 * j + b, b)
            o.leave(SLOTS // 2 - 1)

            for b in range(2):
                pool.wait_ge(S[f"ys{b}"], 16 * (SLOTS // 2))

            def gather_y(t, b, n=P):
                for k in range(2):
                    o.did(pool.tensor_copy(pos_now[b][:, k:k + 1], pos_i[:, k, ds(t, 1)]))
                o.wait()
                pool.tensor_tensor(spare[0:1, 1:2], ones[0:1, 0:1], ones[0:1, 0:1], ALU.mult)
                for buf, k, name in ((ya, 0, "ya"), (yb, 1, "yb")):
                    pool.indirect_dma_start(out=buf[b][0:n, :], out_offset=None, in_=ys_d,
                                            in_offset=bass.IndirectOffsetOnAxis(ap=pos_now[b][0:n, k:k + 1], axis=0)
                                            ).then_inc(S[f"{name}{b}"], 16)

            def scale_o(t, b, n=P):
                pool.wait_ge(S["fnorm"], t + 1)
                pool.tensor_tensor(z2[b][0:n, :], z2[b][0:n, :], fin_tiles[0:n, 1, :], ALU.mult).then_inc(S["fg_ok"], 1)

            gather_y(0, 0)
            gather_y(1, 1)
            pool.wait_ge(S["fin_in"], 48)
            with pool.Fori(1, NT // 2) as j:
                o.enter(j, 1, 4)
                for b in range(2):
                    pool.wait_ge(S["comb_mm"], 2 * j + b - 1)
                    gather_y(2 * j + b, b)
                    scale_o(2 * j + b - 2, b)
            o.leave(NT // 2 - 1)
            pool.wait_ge(S["comb_mm"], NT - 2)
            gather_y(NT - 1, 0, NS)
            scale_o(NT - 3, 0)
            scale_o(NT - 2, 1)
            scale_o(NT - 1, 0, NS)

        @block.scalar
        def _(act):
            o = Order(act, S["act_order"])
            act.wait_ge(S["vec_ok"], 1)
            o.step(act.activation(sp_t[:, 0, :], vecT[:, :, V_LAM], ACT.Abs))
            o.did(act.activation(sp_t[:, 1, :], sp_t[:, 0, :], ACT.Exp, scale=-1.0))

            def uT_evac(i):
                for k in range(KD):
                    act.wait_ge(S["xT_ready"], KD * (i - 1) + k + 1)
                    act.activation(uT[:, k, :], bank[k % 2][:, :], ACT.Identity, bias=modT[:, k, 0:1],
                                   scale=modT[:, KD + k, 0:1]).then_inc(S["uT_ready"], 1)

            def chunk(i, last=False):
                for m in range(2 * NG):
                    j = m % NG
                    act.wait_ge(S["proj_ready"], 12 * i + m + 1)
                    if m < NG:
                        act.wait_ge(S["xr_free"], NG * i - NG + j + 1)
                        dst = xr_buf[:, j, CB:CB + C]
                    else:
                        act.wait_ge(S["p_free"], NG * i - NG + j + 1)
                        dst = p_buf[:, j, PB:PB + C]
                    act.activation(dst, bank[2 + m % 2][:, :], ACT.Copy).then_inc(S["proj_evac"], 1)
                gates(i, C, False)
                for j in range(NG):
                    act.wait_ge(S["proj_ready"], 12 * i + 2 * NG + j + 1)
                    act.wait_ge(S["ylru_ready"], NG * i - NG + j + 1)
                    act.activation(gel[:, j, :], bank[2 + j % 2][:, :], ACT.Gelu_apprx_tanh).then_inc(S["proj_evac"], 1)
                if not last:
                    uT_evac(i + 1)
                roots_and_pool(i, C, False)

            def gates(i, n, first):
                for j in range(NG):
                    if not first:
                        act.wait_ge(S["ylru_ready"], NG * i - NG + j + 1)
                    for q, dst in ((0, tT), (1, tI)):
                        act.wait_ge(S["gates_mm"], 2 * NG * i + 2 * j + q + 1)
                        act.activation(dst[:, j, 0:n], bank[4 + q][:, 0:n], ACT.Tanh, bias=half_b[:, j, q:q + 1],
                                       scale=0.5).then_inc(S["gates_evac"], 1)
                    act.wait_ge(S["gates_evac"], 2 * NG * i + 2 * j + 2)
                    act.activation(tT[:, j, 0:n], tT[:, j, 0:n], ACT.Tanh, bias=sp2[:, j:j + 1],
                                   scale=sp2[:, j:j + 1]).then_inc(S["T_ready"], 1)

            def roots_and_pool(i, n, first):
                for j in range(NG):
                    act.wait_ge(S["T_guard"], NG * i + j + 1)
                    act.activation(tS[:, j, 0:n], tT[:, j, 0:n], ACT.Sqrt).then_inc(S["S_ready"], 1)
                if not first:
                    act.wait_ge(S["y_stored"], 64 * i - 48)
                for g in range(NG):
                    act.wait_ge(S["pool_mm"], NG * i + g + 1)
                    act.activation(yT[:, g, 0:n], bank[6 + g % 2][:, 0:n], ACT.Copy,
                                   scale=vecT[:, g, V_PSCALE:V_PSCALE + 1]).then_inc(S["pool_evac"], 1)

            act.wait_ge(S["modT_ok"], 1)
            act.wait_ge(S["vec_ok"], 2)
            for m in range(2 * NG):
                j = m % NG
                act.wait_ge(S["proj_ready"], m + 1)
                dst = xr_s[:, j, :, CB:CB + DEC_T] if m < NG else p_s[:, j, :, PB:PB + DEC_T]
                act.activation(dst, bank[2 + m % 2][:, 0:NS].rearrange("p (s t) -> p s t", s=DEC_B),
                               ACT.Copy).then_inc(S["proj_evac"], 1)
            gates(0, NS, True)
            for j in range(NG):
                act.wait_ge(S["proj_ready"], 2 * NG + j + 1)
                act.activation(gel[:, j, 0:NS], bank[2 + j % 2][:, 0:NS], ACT.Gelu_apprx_tanh).then_inc(S["proj_evac"], 1)
            uT_evac(1)
            roots_and_pool(0, NS, True)
            with act.Fori(1, NCH) as i:
                chunk(i)

            def state_rows(n, dst, rows, cols):
                act.wait_ge(S["out_mm"], n + 1)
                act.activation(dst[0:rows, 0:cols], bank[7][0:rows, 0:cols], ACT.Copy).then_inc(S["out_evac"], 1)

            for n, (dst, rows, cols) in enumerate(((row_a, NS, DH), (row_b, NS, DH), (row_c, DEC_B, DH))):
                state_rows(n, dst, rows, cols)
            chunk(NCH, last=True)

            def u2T_evac(t):
                for h in range(2):
                    act.wait_ge(S["u2T_mm"], 2 * t + h + 1)
                    act.activation(u2T[:, 4 * h:4 * h + 4, :], bank[4 + h][:, :].rearrange("p (k n) -> p k n", n=P),
                                   ACT.Copy).then_inc(S["u2T_ok"], 1)

            def norm(t, b, n=P):
                act.wait_ge(S["var_ready"], 2 * t + 1)
                act.activation(sd[b][0:n, :], mv[b][0:n, 1:2], ACT.Sqrt).then_inc(S["sd_ready"], 1)
                act.wait_ge(S["var_ready"], 2 * t + 2)
                act.activation(z[b][0:n, :], z[b][0:n, :], ACT.Identity, bias=rs[b][0:n, 1:2],
                               scale=rs[b][0:n, 0:1]).then_inc(S["z_norm"], 1)

            norm(0, 0)
            norm(1, 1)
            for n, (dst, rows, cols) in enumerate(((row_d, PB, DH), (row_e, CB, DH), (hP, NG, P))):
                state_rows(3 + n, dst, rows, cols)
            with act.Fori(1, NT // 2) as j:
                for b in range(2):
                    u2T_evac(2 * j + b - 2)
                    norm(2 * j + b, b)
            u2T_evac(NT - 3)
            norm(NT - 1, 0, NS)
            u2T_evac(NT - 2)
            for h in range(2):
                act.wait_ge(S["u2T_mm"], 2 * (NT - 1) + h + 1)
                act.activation(u2T[:, 4 * h:4 * h + 4, 0:NS], bank[4 + h][:, :].rearrange("p (k n) -> p k n", n=P)[:, :, 0:NS],
                               ACT.Copy).then_inc(S["u2T_ok"], 1)
            act.wait_ge(S["w_exp"], 1)
            act.activation(rt_f[8], rt_f[8], ACT.Exp).then_inc(S["w_expd"], 1)
            act.activation(r17[4], r17[4], ACT.Exp).then_inc(S["w_expd"], 1)

            act.wait_ge(S["w_raw0"], 48)
            for n in range(E_PARTS):
                cols = slice(n * SPLIT, (n + 1) * SPLIT)
                act.activation(w_hi[:, 0, cols], w_raw[0][:, cols], ACT.Copy).then_inc(S["w_hi"], 1)

            def next_expert(s):
                return act.value_load(slot_ei[0:1, 1, ds(s, 1)], min_val=0, max_val=NE - 1)

            def split_next(e, parts):
                with act.If(e > 0):
                    act.wait_ge(S["w_raw0"], (e >> 1) * 48 + 48)
                    act.wait_ge(S["w_raw1"], ((e + 1) >> 1) * 48)
                    for n in parts:
                        act.activation(part(w_hi, e & 1, n), raw_part(e & 1, n), ACT.Copy).then_inc(S["w_hi"], 1)

            def x_evac(s):
                for h in range(2):
                    act.wait_ge(S["xgT_mm"], 2 * s + h + 1)
                    act.activation(xT_hi[:, 4 * h:4 * h + 4, :], bank[h][:, :].rearrange("p (k n) -> p k n", n=P),
                                   ACT.Copy).then_inc(S["xT_hi_ok"], 1)

            def silu(s, b):
                act.wait_ge(S["gu_mm"], s + 1)
                act.activation(sil, bank[2 + b][:, 0:F], ACT.Silu).then_inc(S["sil_ok"], 1)

            def hT_evac(s):
                act.wait_ge(S["hT_mm"], s + 1)
                act.activation(hT_hi[:, :, :], bank[4][:, 0:F].rearrange("p (k n) -> p k n", n=P), ACT.Copy).then_inc(S["hT_hi_ok"], 1)

            def y_evac(s, b, before=None):
                act.wait_ge(S["dn_mm"], s + 1)
                if before is not None:
                    act.wait_ge(S[f"ys{b}"], 16 * before)
                act.activation(y_sb[b][:, 0:512], bank[5][:, :], ACT.Copy).then_inc(S["y_act"], 1)
                act.wait_ge(S["y_act"], s + 1)
                act.wait_ge(S["y_dve"], s + 1)
                act.dma_start(ys_t[ds(s, 1)].rearrange("a p d -> (a p) d"), y_sb[b]).then_inc(S[f"ys{b}"], 16)

            act.wait_ge(S["idx_ready"], 1)
            slots = [next_expert(s) for s in range(3)]
            x_evac(0)
            silu(0, 0)
            x_evac(1)
            hT_evac(0)
            split_next(slots[0], range(GU_PARTS))
            for s in (1, 2):
                silu(s, s % 2)
                x_evac(s + 1)
                split_next(slots[s - 1], range(GU_PARTS, E_PARTS))
                y_evac(s - 1, (s - 1) % 2)
                hT_evac(s)
                split_next(slots[s], range(GU_PARTS))
            with act.Fori(1, SLOTS // 2 - 1) as j:
                for b in range(2):
                    s = 2 * j + 1 + b
                    slots = [next_expert(s - 1), next_expert(s)]
                    silu(s, 1 - b)
                    x_evac(s + 1)
                    split_next(slots[0], range(GU_PARTS, E_PARTS))
                    y_evac(s - 1, b, j)
                    hT_evac(s)
                    split_next(slots[1], range(GU_PARTS))
            s = SLOTS - 1
            silu(s, 1)
            split_next(next_expert(s - 1), range(GU_PARTS, E_PARTS))
            y_evac(s - 1, 0, SLOTS // 2 - 1)
            hT_evac(s)
            y_evac(s, 1, SLOTS // 2 - 1)

            def diag(t, b):
                for k in range(2):
                    act.activation(dg[b][:, k, :], ident[:], ACT.Copy, scale=wgt[:, k, ds(t, 1)]).then_inc(S["diag_ok"], 1)

            def fin(t, b, n=P):
                act.wait_ge(S["fvar_ready"], 2 * t + 1)
                act.activation(sd[b][0:n, :], mv[b][0:n, 1:2], ACT.Sqrt).then_inc(S["fsd_ready"], 1)
                act.wait_ge(S["fvar_ready"], 2 * t + 2)
                act.activation(z2[b][0:n, :], z2[b][0:n, :], ACT.Identity, bias=rs[b][0:n, 1:2],
                               scale=rs[b][0:n, 0:1]).then_inc(S["fnorm"], 1)

            act.wait_ge(S["wgt_ok"], 1)
            diag(0, 0)
            diag(1, 1)
            with act.Fori(0, NT // 2 - 1) as j:
                for b in range(2):
                    fin(2 * j + b, b)
                    diag(2 * j + b + 2, b)
            fin(NT - 3, 0)
            diag(NT - 1, 0)
            fin(NT - 2, 1)
            fin(NT - 1, 0, NS)

        @block.vector
        def _(dve):
            o = Order(dve, S["dve_order"])
            dve.wait_ge(S["vec_mm"], 1)
            dve.tensor_copy(vecT[:], bank[7][:, 0:NG * NV].rearrange("p (g v) -> p g v", v=NV)).then_inc(S["vec_ok"], 1)
            dve.wait_ge(S["vec_ok"], 1)
            lam = vecT[:, :, V_LAM]
            o.did(dve.tensor_scalar(half_b[:, :, 0], vecT[:, :, V_BA], 0.5, None, ALU.mult))
            o.did(dve.tensor_scalar(half_b[:, :, 1], vecT[:, :, V_BX], 0.5, None, ALU.mult))
            dve.wait_ge(S["act_order"], 2)
            o.step(dve.tensor_scalar(sp_t[:, 2, :], sp_t[:, 1, :], 2.0, None, ALU.add))
            o.step(dve.reciprocal(sp_t[:, 2, :], sp_t[:, 2, :]))
            o.step(dve.tensor_tensor(sp_t[:, 1, :], sp_t[:, 1, :], sp_t[:, 2, :], ALU.mult))
            o.step(dve.tensor_tensor(sp_t[:, 2, :], sp_t[:, 1, :], sp_t[:, 1, :], ALU.mult))
            o.step(dve.tensor_scalar(sp_t[:, 3, :], sp_t[:, 2, :], 1.0 / 17, 1.0 / 15, ALU.mult, ALU.add))
            for odd in (13, 11, 9, 7, 5, 3, 1):
                o.step(dve.tensor_tensor(sp_t[:, 3, :], sp_t[:, 3, :], sp_t[:, 2, :], ALU.mult))
                o.step(dve.tensor_scalar(sp_t[:, 3, :], sp_t[:, 3, :], 1.0 / odd, None, ALU.add))
            o.step(dve.tensor_tensor(sp_t[:, 3, :], sp_t[:, 3, :], sp_t[:, 1, :], ALU.mult))
            o.step(dve.tensor_scalar(sp_t[:, 4, :], lam, -1.0, 0.0, ALU.mult, ALU.max))
            o.step(dve.scalar_tensor_tensor(sp_t[:, 4, :], sp_t[:, 3, :], 2.0, sp_t[:, 4, :], ALU.mult, ALU.add))
            dve.tensor_scalar(sp2[:], sp_t[:, 4, :], LRU_C / 4, None, ALU.mult).then_inc(S["vec_ok"], 1)
            dve.wait_ge(S["cT_mm"], 1)
            dve.tensor_copy(cT[:], bank[6][:, 0:KD * NM].rearrange("p (k r) -> p k r", r=NM)).then_inc(S["cT_ok"], 1)
            dve.wait_ge(S["ba_in"], 16)
            with dve.Fori(0, 4) as j:
                for n in range(3):
                    dve.wait_ge(S["ada_mm"], 3 * j + n + 1)
                    cols = mod[0:NM, ds(1536 * j + 512 * n, 512)]
                    dve.tensor_tensor(cols, bank[n][0:NM, :], cols, ALU.add).then_inc(S["ada_ok"], 1)
            dve.wait_ge(S["ada_ok"], 12)
            o.step(dve.tensor_scalar(mod[0:NM, SC1:SH2], mod[0:NM, SC1:SH2], 1.0, None, ALU.add))
            dve.tensor_scalar(mod[0:NM, SC2:6 * D], mod[0:NM, SC2:6 * D], 1.0, None, ALU.add).then_inc(S["mod_ok"], 1)
            dve.wait_ge(S["modT_mm"], 1)
            dve.tensor_copy(modT[:], bank[6][:, 0:2 * KD * NM].rearrange("p (k r) -> p k r", r=NM)).then_inc(S["modT_ok"], 1)
            dve.wait_ge(S["st_mm"], 1)
            for g in range(NG):
                o.did(dve.tensor_copy(p_s[:, g, :, 0:PB], bank[4][:, g * 120:(g + 1) * 120].rearrange("p (s t) -> p s t", s=DEC_B)))
                o.did(dve.tensor_copy(xr_s[:, g, :, 0:CB], bank[5][:, g * 24:(g + 1) * 24].rearrange("p (s t) -> p s t", s=DEC_B)))
            o.did(dve.tensor_copy(h0_s[:], bank[5][:, 128:128 + NG * DEC_B].rearrange("p (g s) -> p g s", s=DEC_B)))
            o.did(dve.memset(p_buf[:, :, 0:PB], 0.0))
            o.did(dve.memset(xr_buf[:, :, 0:CB], 0.0))
            o.did(dve.memset(h_last[:], 0.0))
            for g, w in enumerate(WINDOWS):
                for t in range(PB):
                    o.did(dve.memset(inv_cnt[:, g, t:t + 1], 1.0 / min(w, t + 1)))
            o.wait()
            dve.wait_ge(S["xsT_mm"], 1)
            seqs = lambda v: v.rearrange("p k (s t) -> p k s t", s=DEC_B)
            over_t = lambda v: v.unsqueeze(3).to_broadcast([P, KD, DEC_B, DEC_T])
            o.step(dve.tensor_tensor(seqs(uTs), bank[7][:, :].rearrange("p (k s t) -> p k s t", k=KD, s=DEC_B),
                                     over_t(modT[:, KD:2 * KD, 1:NM]), ALU.mult))
            dve.tensor_tensor(seqs(uTs), seqs(uTs), over_t(modT[:, 0:KD, 1:NM]), ALU.add).then_inc(S["uTs_ready"], 1)

            def conv(i, j, out, inp, free_views):
                taps = [inp(k) for k in range(4)]
                o.step(dve.tensor_scalar(out, taps[0], vecT[:, j, V_WCONV:V_WCONV + 1], vecT[:, j, V_BCONV:V_BCONV + 1],
                                         ALU.mult, ALU.add))
                for k in range(1, 4):
                    last = dve.scalar_tensor_tensor(out, taps[k], vecT[:, j, V_WCONV + k:V_WCONV + k + 1], out, ALU.mult, ALU.add)
                    if k < 3:
                        o.step(last)
                last.then_inc(S["xc_ready"], 1)

            def guard(i, n):
                for j in range(NG):
                    dve.wait_ge(S["T_ready"], NG * i + j + 1)
                    dve.tensor_scalar(tT[:, j, 0:n], tT[:, j, 0:n], 0.0, None, ALU.max).then_inc(S["T_guard"], 1)

            def lru_coefficients(i, j, n, a_out, b_out):
                dve.wait_ge(S["S_ready"], NG * i + j + 1)
                o.step(dve.tensor_scalar(q_t[:, 0:n], tT[:, j, 0:n], 1.0, None, ALU.add))
                o.did(dve.scalar_tensor_tensor(b_out, tI[:, j, 0:n], 1.0, xc[:, j, 0:n], ALU.add, ALU.mult))
                o.step(dve.reciprocal(q_t[:, 0:n], q_t[:, 0:n]))
                o.did(dve.tensor_scalar(a_out, q_t[:, 0:n], 2.0, -1.0, ALU.mult, ALU.add))
                o.step(dve.tensor_tensor(q_t[:, 0:n], q_t[:, 0:n], tS[:, j, 0:n], ALU.mult))
                o.step(dve.tensor_tensor(b_out, b_out, q_t[:, 0:n], ALU.mult))

            def chunk(i):
                for j in range(NG):
                    dve.wait_ge(S["proj_evac"], 12 * i + j + 1)
                    conv(i, j, xc[:, j, :], lambda k: xr_buf[:, j, k:k + C], None)
                    dve.wait_ge(S["xc_ready"], NG * i + j + 1)
                    dve.tensor_copy(xr_buf[:, j, 0:CB], xr_buf[:, j, C:C + CB]).then_inc(S["xr_free"], 1)
                for g, w in enumerate(WINDOWS):
                    dve.wait_ge(S["proj_evac"], 12 * i + NG + g + 1)
                    src, span, nb = p_buf[:, g, :], 1, 0
                    while span < w:
                        dst = wsum[nb]
                        lo = PB - w + 2 * span
                        o.step(dve.tensor_tensor(dst[:, lo:PB + C], src[:, lo:PB + C], src[:, lo - span:PB + C - span], ALU.add))
                        src, span, nb = dst, 2 * span, 1 - nb
                    dve.wait_ge(S["pool_mm"], NG * i + g - 1)
                    dd = dif[:, g % 2, :]
                    o.did(dve.scalar_tensor_tensor(dd[:, PB:C], src[:, 2 * PB:PB + C], 1.0 / w, p_buf[:, g, 2 * PB:PB + C],
                                                   ALU.mult, ALU.subtract))
                    o.step(dve.tensor_tensor(fix[:, 0:PB], src[:, PB:2 * PB], inv_cnt[:, g, 0:PB], ALU.mult))
                    dve.tensor_tensor(dd[:, 0:PB], fix[:, 0:PB], p_buf[:, g, PB:2 * PB], ALU.subtract).then_inc(S["d_ready"], 1)
                    dve.wait_ge(S["d_ready"], NG * i + g + 1)
                    o.did(dve.memset(inv_cnt[:, g, 0:PB], 1.0 / w))
                    dve.tensor_copy(p_buf[:, g, 0:PB], p_buf[:, g, C:C + PB]).then_inc(S["p_free"], 1)
                guard(i, C)
                dve.wait_ge(S["y_stored"], 64 * i - 48)
                for j in range(NG):
                    lru_coefficients(i, j, C, a_t, b_t)
                    o.step(dve.tensor_tensor_scan(h_t, a_t, b_t, h_last[:, j:j + 1], ALU.mult, ALU.add))
                    o.did(dve.tensor_copy(h_last[:, j:j + 1], h_t[:, C - 1:C]))
                    dve.wait_ge(S["proj_evac"], 12 * i + 2 * NG + j + 1)
                    dve.tensor_tensor(yT[:, NG + j, :], h_t, gel[:, j, :], ALU.mult).then_inc(S["ylru_ready"], 1)
                o.wait()

            dve.wait_ge(S["mod_stored"], 16)
            i = 0
            bs = lambda v: v.rearrange("p (s t) -> p s t", s=DEC_B)
            for j in range(NG):
                dve.wait_ge(S["proj_evac"], 12 * i + j + 1)
                conv(i, j, bs(xc[:, j, 0:NS]), lambda k: xr_s[:, j, :, k:k + DEC_T], None)
            for g, w in enumerate(WINDOWS):
                dve.wait_ge(S["proj_evac"], 12 * i + NG + g + 1)
                wv = [v[:, 0:DEC_B * (PB + DEC_T)].rearrange("p (s t) -> p s t", s=DEC_B) for v in wsum]
                src, span, end, nb = p_s[:, g], 1, PB + DEC_T, 0
                while span < w:
                    lo = PB - w + 2 * span
                    o.step(dve.tensor_tensor(wv[nb][:, :, lo:end], src[:, :, lo:end], src[:, :, lo - span:end - span], ALU.add))
                    src, span, nb = wv[nb], 2 * span, 1 - nb
                if g >= 2:
                    dve.wait_ge(S["pool_mm"], g - 1)
                dve.scalar_tensor_tensor(bs(dif[:, g % 2, 0:NS]), src[:, :, PB:end], 1.0 / w, p_s[:, g, :, PB:end],
                                         ALU.mult, ALU.subtract).then_inc(S["d_ready"], 1)
                dve.wait_ge(S["d_ready"], NG * i + g + 1)
            for g in range(NG):
                dve.tensor_copy(bs(prj_s[:, g, :]), p_s[:, g, :, PB:PB + DEC_T]).then_inc(S["p_free"], 1)
                dve.tensor_copy(bs(prj_s[:, NG + g, :]), xr_s[:, g, :, CB:CB + DEC_T]).then_inc(S["xr_free"], 1)
            guard(i, NS)
            av, bv, hv = (v[:, 0:NG * NS].rearrange("p (g s t) -> p g s t", g=NG, s=DEC_B) for v in (a_t, b_t, h_t))
            for j in range(NG):
                lru_coefficients(i, j, NS, a_t[:, j * NS:(j + 1) * NS], b_t[:, j * NS:(j + 1) * NS])
            for t in range(DEC_T):
                before = h0_s[:] if t == 0 else hv[:, :, :, t - 1]
                o.step(dve.tensor_tensor(hv[:, :, :, t], av[:, :, :, t], before, ALU.mult))
                o.step(dve.tensor_tensor(hv[:, :, :, t], hv[:, :, :, t], bv[:, :, :, t], ALU.add))
            dve.tensor_copy(h0_s[:], hv[:, :, :, DEC_T - 1]).then_inc(S["prj_copied"], 1)
            dve.wait_ge(S["proj_evac"], 12 * i + 12)
            for j in range(NG):
                dve.tensor_tensor(yT[:, NG + j, 0:NS], h_t[:, j * NS:(j + 1) * NS], gel[:, j, 0:NS], ALU.mult).then_inc(S["ylru_ready"], 1)

            with dve.Fori(1, NCH + 1) as i:
                o.enter(i, 1, CHUNK_STEPS)
                chunk(i)
            o.leave(NCH)

            dve.wait_ge(S["tiles_in"], 80)
            dve.wait_ge(S["rt_in"], 64)

            def ln_in(t, b, n, rows, uses, first):
                dve.wait_ge(S["mix_ready"], t + 1)
                for h in range(2):
                    o.did(dve.tensor_tensor(z[b][0:n, 512 * h:512 * h + 512], bank[2 * b + h][0:n, :],
                                            rows[0][0:n, 512 * h:512 * h + 512], ALU.mult))
                o.wait()
                dve.wait_ge(S[f"xres{b}"], 16 * uses)
                dve.scalar_tensor_tensor(z[b][0:n, :], xres[b][0:n, :], ALPHA, z[b][0:n, :], ALU.mult, ALU.add).then_inc(S["mix_used"], 1)
                dve.wait_ge(S["mix_used"], t + 1)
                stats(b, n, z[b], S["var_ready"], S["sd_ready"], t)

            def stats(b, n, zz, ready, sd_ready, t):
                for h in range(2):
                    o.did(dve.bn_stats(st6[b][0:n, h, :], zz[0:n, 512 * h:512 * h + 512]))
                o.wait()
                dve.memset(spare[0:1, 0:1], 0.0)
                o.step(dve.bn_aggr(mv[b][0:n, :], st6[b][0:n, :, :].rearrange("p a b -> p (a b)")))
                dve.tensor_scalar(mv[b][0:n, 1:2], mv[b][0:n, 1:2], LN_EPS, None, ALU.add).then_inc(ready, 1)
                dve.wait_ge(sd_ready, t + 1)
                o.step(dve.reciprocal(rs[b][0:n, 0:1], sd[b][0:n, :]))
                dve.scalar_tensor_tensor(rs[b][0:n, 1:2], mv[b][0:n, 0:1], -1.0, rs[b][0:n, 0:1], ALU.mult, ALU.mult).then_inc(ready, 1)

            def ln_out(t, b, n, rows, uses, first):
                dve.wait_ge(S["x1_ready"], t + 1)
                if not first:
                    dve.wait_ge(S[f"u2_st{b}"], 16 * (uses - 1))
                    dve.wait_ge(S["u2T_mm"], 2 * t - 2)
                o.step(dve.tensor_tensor(u2[b][0:n, :], x1[b][0:n, :], rows[1][0:n, :], ALU.mult))
                dve.tensor_tensor(u2[b][0:n, :], u2[b][0:n, :], rows[2][0:n, :], ALU.add).then_inc(S["u2_ready"], 1)

            def router_out(t, n=P):
                dve.wait_ge(S["rt_mm"], t + 1)
                dve.tensor_tensor(logits[0:n, ds(t, 1), :].rearrange("p a r -> p (a r)"), bank[6][0:n, 0:NR], b_rt[0:n, :],
                                  ALU.add).then_inc(S["rt_ok"], 1)

            o.did(dve.memset(logits[:], 0.0))
            prompt_rows = (row_tiles[:, 0, :], row_tiles[:, 3, :], row_tiles[:, 4, :])
            sample_rows = (row_tiles_s[:, 0, :], row_tiles_s[:, 1, :], row_tiles_s[:, 2, :])
            ln_in(0, 0, P, prompt_rows, 1, True)
            ln_in(1, 1, P, prompt_rows, 1, True)
            ln_out(0, 0, P, prompt_rows, 1, True)
            ln_in(2, 0, P, prompt_rows, 2, False)
            ln_out(1, 1, P, prompt_rows, 1, True)
            router_out(0)
            ln_in(3, 1, P, prompt_rows, 2, False)
            ln_out(2, 0, P, prompt_rows, 2, False)
            router_out(1)
            with dve.Fori(2, NT // 2) as j:
                o.enter(j, 2, LN_STEPS)
                for b in range(2):
                    ln_in(2 * j + b, b, P, prompt_rows, j + 1, False)
                    ln_out(2 * j + b - 1, 1 - b, P, prompt_rows, j + b, False)
                    router_out(2 * j + b - 2)
            o.leave(NT // 2 - 2)
            dve.wait_ge(S["tiles_s_in"], 16 * 3 * DEC_B)
            ln_in(NT - 1, 0, NS, sample_rows, NT // 2 + 1, False)
            ln_out(NT - 2, 1, P, prompt_rows, NT // 2, False)
            router_out(NT - 3)
            ln_out(NT - 1, 0, NS, sample_rows, NT // 2 + 1, False)
            router_out(NT - 2)
            router_out(NT - 1, NS)
            dve.wait_ge(S["rt_ok"], NT)

            bc = lambda v, n: v.unsqueeze(2).to_broadcast([P, v.shape[1], n])
            gl, el = logits[:, :, 0:NGR], logits[:, :, NGR:NR]
            hot_g, hot_1, hot_2, esel, f4 = rt_f[0], rt_f[1], rt_f[2], rt_f[3], rt_f[4]
            gm, m1, m2, mx = r17[0], r17[1], r17[2], r17[3]

            def first_max(v, top, hot):
                o.step(dve.tensor_reduce(top, v, axis=AX, op=ALU.max))
                o.step(dve.tensor_tensor(f4, v, bc(top, EPG), ALU.is_equal))
                o.step(dve.tensor_tensor(f4, f4, prio[:].unsqueeze(1).to_broadcast([P, NT, EPG]), ALU.mult))
                o.step(dve.tensor_reduce(mx, f4, axis=AX, op=ALU.max))
                o.step(dve.tensor_tensor(hot, f4, bc(mx, EPG), ALU.is_equal))

            dve.wait_ge(S["consts"], 4)
            first_max(gl, gm, hot_g)
            prod, e1, e2, both, rank, base = rt[0], rt[1], rt[2], rt[3], rt[4], rt[5]
            g4 = lambda v: v.rearrange("p t (g e) -> p t g e", g=NGR)
            over_e = hot_g.unsqueeze(3).to_broadcast([P, NT, NGR, EPG])
            o.step(dve.tensor_tensor(g4(prod), g4(el), over_e, ALU.mult))
            o.step(dve.tensor_reduce(esel, prod.rearrange("p t (g e) -> p t e g", g=NGR), axis=AX, op=ALU.add))
            first_max(esel, m1, hot_1)
            o.step(dve.scalar_tensor_tensor(esel, hot_1, -BIG, esel, ALU.mult, ALU.add))
            first_max(esel, m2, hot_2)
            o.step(dve.tensor_tensor(hot_g, hot_g, bc(valid[:], NGR), ALU.mult))
            for e_hot, hot in ((e1, hot_1), (e2, hot_2)):
                o.step(dve.tensor_tensor(g4(e_hot), over_e, hot.unsqueeze(2).to_broadcast([P, NT, NGR, EPG]), ALU.mult))
            dve.tensor_tensor(both, e1, e2, ALU.add).then_inc(S["m_ready"], 1)
            o.did(dve.tensor_tensor(rt_f[8], gl, bc(gm, NGR), ALU.subtract))
            dve.tensor_tensor(r17[4], m2, m1, ALU.subtract).then_inc(S["w_exp"], 1)
            dve.wait_ge(S["cnt_mm"], 2)
            tot = bank[1][:, 0:NT * NE].rearrange("p (t e) -> p t e", e=NE)
            o.step(dve.memset(base[:, 0, :], 0.0))
            n_e, slots_n, start_e, end_e = e16[0], e16[1], e16[2], e16[3]
            for t in range(NT):
                dst = base[:, t + 1, :] if t + 1 < NT else n_e
                o.step(dve.tensor_tensor(dst, base[:, t, :], tot[:, t, :], ALU.add))
            o.step(dve.tensor_tensor(rank, bank[0][:, 0:NT * NE].rearrange("p (t e) -> p t e", e=NE), base, ALU.add))
            o.step(dve.tensor_tensor(big_t, bc(n_e, NT), iota17[:].unsqueeze(1).to_broadcast([P, NE, NT]), ALU.is_gt))
            o.step(dve.tensor_reduce(slots_n, big_t, axis=AX, op=ALU.add))
            o.step(dve.tensor_scalar(slots_n, slots_n, 1.0, None, ALU.max))
            o.step(dve.tensor_tensor(lt_prod, lt16[:], slots_n.unsqueeze(1).to_broadcast([P, NE, NE]), ALU.mult))
            o.step(dve.tensor_reduce(start_e, lt_prod, axis=AX, op=ALU.add))
            o.step(dve.tensor_tensor(end_e, start_e, slots_n, ALU.add))
            o.step(dve.tensor_tensor(slot_ge, bc(iota_s[:], NE), end_e.unsqueeze(1).to_broadcast([P, SLOTS, NE]), ALU.is_ge))
            o.step(dve.tensor_reduce(slot_e[:], slot_ge, axis=AX, op=ALU.add))
            o.step(dve.tensor_scalar(slot_ei[:, 0, :], slot_e[:], float(NE - 1), None, ALU.min))
            nxt = e48[0]
            o.did(dve.memset(nxt[:, 0:1], 1.0))
            o.step(dve.tensor_tensor(nxt[:, 1:SLOTS], slot_e[:, 1:SLOTS], slot_e[:, 0:SLOTS - 1], ALU.is_gt))
            o.did(dve.tensor_scalar(e48[1], slot_e[:], float(NE - 1), None, ALU.is_lt))
            o.step(dve.scalar_tensor_tensor(nxt, slot_e[:], 1.0, nxt, ALU.add, ALU.mult))
            o.step(dve.tensor_tensor(slot_ei[:, 1, :], nxt, e48[1], ALU.mult))
            o.step(dve.tensor_scalar(e16[4], start_e, float(P), None, ALU.mult))
            o.step(dve.tensor_tensor(rank, rank, e16[4].unsqueeze(1).to_broadcast([P, NT, NE]), ALU.add))
            o.step(dve.tensor_scalar(r17[5], valid[:], -8192.0, 8192.0, ALU.mult, ALU.add))
            for k, e_hot in enumerate((e1, e2)):
                o.step(dve.tensor_tensor(prod, e_hot, rank, ALU.mult))
                o.step(dve.tensor_reduce(r17[6], prod, axis=AX, op=ALU.add))
                o.step(dve.tensor_tensor(pos_a[:, k, :], r17[6], r17[5], ALU.add))
            o.step(dve.tensor_scalar(pos_b[:], pos_a[:], 7, None, ALU.arith_shift_right))
            o.did(dve.tensor_scalar(pos_a[:], pos_a[:], P - 1, None, ALU.bitwise_and))
            o.step(dve.tensor_copy(pos_f[:, 2:4, :], pos_b[:]))
            o.step(dve.tensor_copy(pos_f[:, 0:2, :], pos_a[:]))
            o.did(dve.scalar_tensor_tensor(pos_i[:], pos_f[:, 0:2, :], float(SLOTS), pos_f[:, 2:4, :], ALU.mult, ALU.add))
            o.step(dve.tensor_scalar(r17[7], iota17[:], 1.0 / P, None, ALU.mult))
            with dve.Fori(0, NT) as t:
                o.enter(t, 0, 4)
                for k in range(2):
                    dve.wait_ge(S["hot_used"], 2 * t + k)
                    o.did(dve.tensor_scalar(hot_a[k], iota_r[:], pos_f[:, k, ds(t, 1)], None, ALU.is_equal))
                    o.did(dve.tensor_scalar(hot_b[k][:, 0:SLOTS], iota_s[:], pos_f[:, 2 + k, ds(t, 1)], r17[7][:, ds(t, 1)],
                                            ALU.is_equal, ALU.mult))
                    dve.tensor_scalar(hot_b[k][:, SLOTS:2 * SLOTS], iota_s[:], pos_f[:, 2 + k, ds(t, 1)], part_i[:, 0:1],
                                      ALU.is_equal, ALU.mult).then_inc(S["hot_ready"], 1)
            o.leave(NT)
            dve.wait_ge(S["idx_mm"], 1)
            o.step(dve.tensor_copy(slot_ge[:, 0:6, :].rearrange("p a b -> p (a b)"), bank[2][:, 0:2 * SLOTS]))
            lo_hi = slot_ge[:, 0:6, :].rearrange("p a b -> p (a b)")
            dve.scalar_tensor_tensor(tok_i[:], lo_hi[:, 0:SLOTS], float(P), lo_hi[:, SLOTS:2 * SLOTS], ALU.mult, ALU.add).then_inc(S["idx_ready"], 1)
            dve.wait_ge(S["w_expd"], 2)
            o.step(dve.tensor_reduce(r17[8], rt_f[8], axis=AX, op=ALU.add))
            o.did(dve.tensor_scalar(r17[9], r17[4], 1.0, None, ALU.add))
            o.wait()
            o.step(dve.tensor_tensor(r17[8], r17[8], r17[9], ALU.mult))
            o.step(dve.reciprocal(wgt[:, 0, :], r17[8]))
            dve.tensor_tensor(wgt[:, 1, :], wgt[:, 0, :], r17[4], ALU.mult).then_inc(S["wgt_ok"], 1)

            def next_expert(s):
                return dve.value_load(slot_ei[0:1, 1, ds(s, 1)], min_val=0, max_val=NE - 1)

            def split_next(e, parts):
                with dve.If(e > 0):
                    for n in parts:
                        dve.wait_ge(S["w_hi"], e * E_PARTS + n + 1)
                        dve.tensor_tensor(part(w_lo, e & 1, n), raw_part(e & 1, n), part(w_hi, e & 1, n).bitcast(F32),
                                          ALU.subtract).then_inc(S["w_lo"], 1)

            def x_evac(s):
                for h in range(2):
                    k = slice(4 * h, 4 * h + 4)
                    dve.wait_ge(S["xT_hi_ok"], 2 * s + h + 1)
                    dve.tensor_tensor(xT_lo[:, k, :], bank[h][:, :].rearrange("p (k n) -> p k n", n=P),
                                      xT_hi[:, k, :].bitcast(F32), ALU.subtract).then_inc(S["xT_lo_ok"], 1)

            def hidden(s, b):
                dve.wait_ge(S["sil_ok"], s + 1)
                dve.tensor_tensor(hid, sil, bank[2 + b][:, F:2 * F], ALU.mult).then_inc(S["hid_ok"], 1)

            def hT_evac(s):
                dve.wait_ge(S["hT_hi_ok"], s + 1)
                dve.tensor_tensor(hT_lo[:, :, :], bank[4][:, 0:F].rearrange("p (k n) -> p k n", n=P),
                                  hT_hi[:, :, :].bitcast(F32), ALU.subtract).then_inc(S["hT_lo_ok"], 1)

            def y_evac(s, b, before=None):
                dve.wait_ge(S["dn_mm"], s + 1)
                if before is not None:
                    dve.wait_ge(S[f"ys{b}"], 16 * before)
                dve.tensor_copy(y_sb[b][:, 512:1024], bank[6][:, :]).then_inc(S["y_dve"], 1)

            dve.wait_ge(S["w0_lo"], E_PARTS)
            dve.memset(spare[0:1, 0:1], 0.0).then_inc(S["w_lo"], E_PARTS)
            slots = [next_expert(s) for s in range(3)]
            x_evac(0)
            hidden(0, 0)
            x_evac(1)
            hT_evac(0)
            split_next(slots[0], range(GU_PARTS))
            for s in (1, 2):
                hidden(s, s % 2)
                x_evac(s + 1)
                split_next(slots[s - 1], range(GU_PARTS, E_PARTS))
                y_evac(s - 1, (s - 1) % 2)
                hT_evac(s)
                split_next(slots[s], range(GU_PARTS))
            with dve.Fori(1, SLOTS // 2 - 1) as j:
                for b in range(2):
                    s = 2 * j + 1 + b
                    slots = [next_expert(s - 1), next_expert(s)]
                    hidden(s, 1 - b)
                    x_evac(s + 1)
                    split_next(slots[0], range(GU_PARTS, E_PARTS))
                    y_evac(s - 1, b, j)
                    hT_evac(s)
                    split_next(slots[1], range(GU_PARTS))
            s = SLOTS - 1
            hidden(s, 1)
            split_next(next_expert(s - 1), range(GU_PARTS, E_PARTS))
            y_evac(s - 1, 0, SLOTS // 2 - 1)
            hT_evac(s)
            y_evac(s, 1, SLOTS // 2 - 1)

            dve.wait_ge(S["fin_in"], 48)

            def fin_in(t, b, n, gate2, uses):
                dve.wait_ge(S["comb_mm"], t + 1)
                for h in range(2):
                    o.did(dve.tensor_tensor(z2[b][0:n, 512 * h:512 * h + 512], bank[2 * b + h][0:n, :],
                                            gate2[0:n, 512 * h:512 * h + 512], ALU.mult))
                o.wait()
                dve.wait_ge(S[f"xo{b}"], 16 * uses)
                dve.scalar_tensor_tensor(z2[b][0:n, :], xo[b][0:n, :], ALPHA, z2[b][0:n, :], ALU.mult, ALU.add).then_inc(S["comb_used"], 1)
                dve.wait_ge(S["comb_used"], t + 1)
                stats(b, n, z2[b], S["fvar_ready"], S["fsd_ready"], t)

            def fin_out(t, b, n, before):
                dve.wait_ge(S["fg_ok"], t + 1)
                if before is not None:
                    dve.wait_ge(S[f"os{b}"], 16 * before)
                dve.tensor_tensor(oo[b][0:n, :], z2[b][0:n, :], fin_tiles[0:n, 2, :], ALU.add).then_inc(S["fo_ok"], 1)
                dve.wait_ge(S["fo_ok"], t + 1)

            g2 = fin_tiles[:, 0, :]
            fin_in(0, 0, P, g2, 1)
            fin_in(1, 1, P, g2, 1)
            fin_out(0, 0, P, None)
            fin_in(2, 0, P, g2, 2)
            fin_out(1, 1, P, None)
            fin_in(3, 1, P, g2, 2)
            fin_out(2, 0, P, 1)
            with dve.Fori(2, NT // 2) as j:
                o.enter(j, 2, FIN_STEPS)
                for b in range(2):
                    fin_in(2 * j + b, b, P, g2, j + 1)
                    fin_out(2 * j + b - 1, 1 - b, P, j + b - 1)
            o.leave(NT // 2 - 2)
            dve.wait_ge(S["fin_s_in"], 16 * DEC_B)
            fin_in(NT - 1, 0, NS, fin_tile_s, NT // 2 + 1)
            fin_out(NT - 2, 1, P, NT // 2 - 1)
            fin_out(NT - 1, 0, NS, NT // 2)

        @block.tensor
        def _(pe):
            def turn(out, in_, rows):
                return pe.transpose(out, in_, ident[0:rows, 0:rows])

            pe.wait_ge(S["consts"], 1)
            pe.wait_ge(S["c_in"], 32)
            for k in range(KD):
                last = turn(bank[6][:, k * NM:(k + 1) * NM], c_rows[0:NM, k * P:(k + 1) * P], NM)
            last.then_inc(S["cT_mm"], 1)
            pe.wait_ge(S["vec_in"], 96)
            for g in range(NG):
                last = turn(bank[7][:, g * NV:(g + 1) * NV], row_v[0:NV, g * P:(g + 1) * P], NV)
            last.then_inc(S["vec_mm"], 1)
            pe.wait_ge(S["cT_ok"], 1)

            def ada(j, first=False):
                for n in range(3):
                    pe.wait_ge(S[f"ada{n}"], 16 * (j + 1))
                    if not first:
                        pe.wait_ge(S["ada_ok"], 3 * j + n - 2)
                    for k in range(KD):
                        last = pe.matmul(bank[n][0:NM, :], cT[:, k, :], w_ada[n][:, k, :], start=k == 0, stop=k == KD - 1)
                    last.then_inc(S["ada_mm"], 1)

            ada(0, first=True)
            with pe.Fori(1, 4) as j:
                ada(j)
            pe.wait_ge(S["mod_ok"], 1)
            for k in range(2 * KD):
                last = turn(bank[6][:, k * NM:(k + 1) * NM], mod[0:NM, k * P:(k + 1) * P], NM)
            last.then_inc(S["modT_mm"], 1)
            pe.wait_ge(S["st_in"], 48)
            for g in range(NG):
                turn(bank[4][:, g * 120:(g + 1) * 120], row_a[0:120, g * P:(g + 1) * P], 120)
                turn(bank[5][:, g * 24:(g + 1) * 24], row_b[0:24, g * P:(g + 1) * P], 24)
                last = turn(bank[5][:, 128 + g * DEC_B:128 + (g + 1) * DEC_B], row_c[0:DEC_B, g * P:(g + 1) * P], DEC_B)
            last.then_inc(S["st_mm"], 1)
            pe.wait_ge(S["xs_loaded"], 16)
            for k in range(KD):
                last = turn(bank[7][:, k * NS:(k + 1) * NS], xs[0:NS, k * P:(k + 1) * P], NS)
            last.then_inc(S["xsT_mm"], 1)
            pe.wait_ge(S["w_in_in"], 16)
            pe.wait_ge(S["gates_in"], 64)
            pe.wait_ge(S["wpool_in"], 16)

            def project(i, m, order, src, n, wait_k=None):
                for k in range(KD):
                    if wait_k is not None:
                        pe.wait_ge(S["uT_ready"], wait_k + k + 1)
                    last = pe.matmul(bank[2 + order % 2][:, 0:n], w_in[:, k, m * P:(m + 1) * P], src[:, k, 0:n],
                                     start=k == 0, stop=k == KD - 1)
                last.then_inc(S["proj_ready"], 1)

            def mixers(i, src, n, first, turn_next):
                for order in range(2 * NG):
                    if not (first and order < 2):
                        pe.wait_ge(S["proj_evac"], 12 * i + order - 1)
                    m = NG + order if order < NG else order - NG
                    project(i, m, order, src, n, KD * (i - 1) if not first and order == 0 else None)
                for j in range(NG):
                    pe.wait_ge(S["xc_ready"], NG * i + j + 1)
                    for q, w in ((0, wa), (1, wx)):
                        if not (first and j == 0):
                            pe.wait_ge(S["gates_evac"], 2 * NG * i + 2 * j + q - 1)
                        pe.matmul(bank[4 + q][:, 0:n], w[:, j, :], xc[:, j, 0:n], start=True, stop=True).then_inc(S["gates_mm"], 1)
                for j in range(NG):
                    pe.wait_ge(S["proj_evac"], 12 * i + 2 * NG + j - 1)
                    project(i, 2 * NG + j, j, src, n)
                if turn_next is not None:
                    turn_next()
                for g in range(NG):
                    pe.wait_ge(S["d_ready"], NG * i + g + 1)
                    if not (first and g < 2):
                        pe.wait_ge(S["pool_evac"], NG * i + g - 1)
                    pe.matmul(bank[6 + g % 2][:, 0:n], wp[:, g, :], dif[:, g % 2, 0:n], start=True, stop=True).then_inc(S["pool_mm"], 1)

            def turn_chunk(i, first=False):
                pe.wait_ge(S["x_loaded"], 16 * i)
                for k in range(KD):
                    if not (first and k < 2):
                        pe.wait_ge(S["uT_ready"], KD * (i - 1) + k - 1)
                    for t in range(TPC):
                        last = turn(bank[k % 2][:, t * P:(t + 1) * P], xin[:, t, k * P:(k + 1) * P], P)
                    last.then_inc(S["xT_ready"], 1)

            pe.wait_ge(S["uTs_ready"], 1)
            mixers(0, uTs, NS, True, lambda: turn_chunk(1, first=True))
            with pe.Fori(1, NCH) as i:
                mixers(i, uT, C, False, lambda: turn_chunk(i + 1))

            def state_rows(n, src, rows):
                if n:
                    pe.wait_ge(S["out_evac"], n)
                for g in range(NG):
                    last = pe.transpose(bank[7][0:rows, g * P:(g + 1) * P], src(g), ident[:])
                last.then_inc(S["out_mm"], 1)

            pe.wait_ge(S["prj_copied"], 1)
            pe.wait_ge(S["pool_evac"], NG * NCH)
            state_rows(0, lambda g: prj_s[:, g, :], NS)
            state_rows(1, lambda g: prj_s[:, NG + g, :], NS)
            state_rows(2, lambda g: h0_s[:, g, :], DEC_B)
            pe.wait_ge(S["out_evac"], 3)
            mixers(NCH, uT, C, False, None)

            pe.wait_ge(S["w_out_in"], 32)

            def out_proj(t, b, uses, n=P, first=False):
                pe.wait_ge(S[f"yTt{b}"], 16 * uses)
                if not first:
                    pe.wait_ge(S["mix_used"], t - 1)
                for h in range(2):
                    for k in range(KD):
                        last = pe.matmul(bank[2 * b + h][0:n, :], yTt[b][:, k, 0:n], w_out[:, k, 512 * h:512 * h + 512],
                                         start=k == 0, stop=k == KD - 1)
                last.then_inc(S["mix_ready"], 1)

            def router(t, b, n=P, first=False):
                pe.wait_ge(S["u2_ready"], t + 1)
                for h in range(2):
                    if not first:
                        pe.wait_ge(S["u2T_ok"], 2 * t + h - 1)
                    for k in range(4):
                        last = turn(bank[4 + h][:, k * P:k * P + n], u2[b][0:n, (4 * h + k) * P:(4 * h + k + 1) * P], n)
                    last.then_inc(S["u2T_mm"], 1)
                pe.wait_ge(S["u2T_ok"], 2 * t + 2)
                if not first:
                    pe.wait_ge(S["rt_ok"], t)
                for k in range(KD):
                    last = pe.matmul(bank[6][0:n, 0:NR], u2T[:, k, 0:n], w_rt[:, k, :], start=k == 0, stop=k == KD - 1)
                last.then_inc(S["rt_mm"], 1)

            out_proj(0, 0, 1, first=True)
            out_proj(1, 1, 1, first=True)
            pe.wait_ge(S["ylru_ready"], NG * NCH + NG)
            pe.wait_ge(S["pool_evac"], NG * NCH + NG)
            state_rows(3, lambda g: p_buf[:, g, 0:PB], PB)
            state_rows(4, lambda g: xr_buf[:, g, 0:CB], CB)
            pe.wait_ge(S["out_evac"], 5)
            pe.transpose(bank[7][0:NG, 0:P], h_last[:], ident[:]).then_inc(S["out_mm"], 1)
            pe.wait_ge(S["rt_in"], 64)
            out_proj(2, 0, 2)
            router(0, 0, first=True)
            out_proj(3, 1, 2)
            router(1, 1)
            with pe.Fori(2, NT // 2) as j:
                for b in range(2):
                    out_proj(2 * j + b, b, j + 1)
                    router(2 * j + b - 2, b)
            out_proj(NT - 1, 0, NT // 2 + 1, NS)
            router(NT - 3, 0)
            router(NT - 2, 1)
            router(NT - 1, 0, NS)
            pe.wait_ge(S["m_ready"], 1)
            m_all = rt[3].rearrange("p t e -> p (t e)")
            pe.matmul(bank[0][:, 0:NT * NE], tri[:], m_all, start=True, stop=True).then_inc(S["cnt_mm"], 1)
            pe.matmul(bank[1][:, 0:NT * NE], ones[:], m_all, start=True, stop=True).then_inc(S["cnt_mm"], 1)

            def dispatch(t, start, stop):
                for k in range(2):
                    pe.wait_ge(S["hot_ready"], 2 * t + k + 1)
                    last = pe.matmul(bank[2][:, 0:2 * SLOTS], hot_a[k], hot_b[k], start=start and k == 0, stop=stop and k == 1)
                    last.then_inc(S["hot_used"], 1)
                return last

            dispatch(0, True, False)
            with pe.Fori(1, NT - 1) as t:
                dispatch(t, False, False)
            dispatch(NT - 1, False, True)
            pe.wait_ge(S["hot_used"], 2 * NT + 0)
            turn(bank[7][0:2, 0:2], ident[0:2, 0:2], 2).then_inc(S["idx_mm"], 1)

            pe.wait_ge(S["idx_ready"], 1)

            def turn_x(s, b, uses, first=False):
                pe.wait_ge(S[f"xg{b}"], 16 * uses)
                for h in range(2):
                    if not first:
                        pe.wait_ge(S["xT_lo_ok"], 2 * s + h - 1)
                    for k in range(4):
                        last = turn(bank[h][:, k * P:(k + 1) * P], xg[b][:, (4 * h + k) * P:(4 * h + k + 1) * P], P)
                    last.then_inc(S["xgT_mm"], 1)

            def product(out, x_hi, x_lo, buf, off, start, stop):
                hi, lo = (w[:, ds(buf, 1), off:off + 512].rearrange("p a n -> p (a n)") for w in (w_hi, w_lo))
                pe.matmul(out, x_hi, hi, start=start, stop=False)
                pe.matmul(out, x_hi, lo, start=False, stop=False)
                return pe.matmul(out, x_lo, hi, start=False, stop=stop)

            def gate_up(s, b):
                e = pe.value_load(slot_ei[0:1, 0, ds(s, 1)], min_val=0, max_val=NE - 1)
                pe.wait_ge(S["xT_lo_ok"], 2 * s + 2)
                pe.wait_ge(S["w_lo"], e * E_PARTS + GU_PARTS)
                for k in range(KD):
                    last = product(bank[2 + b][:, :], xT_hi[:, k, :], xT_lo[:, k, :], e & 1, k * 2 * F, k == 0, k == KD - 1)
                last.then_inc(S["gu_mm"], 1)

            def turn_h(s):
                pe.wait_ge(S["hid_ok"], s + 1)
                for k in range(F // P):
                    last = turn(bank[4][:, k * P:(k + 1) * P], hid[:, k * P:(k + 1) * P], P)
                last.then_inc(S["hT_mm"], 1)

            def down(s, first=False):
                e = pe.value_load(slot_ei[0:1, 0, ds(s, 1)], min_val=0, max_val=NE - 1)
                pe.wait_ge(S["hT_lo_ok"], s + 1)
                pe.wait_ge(S["w_lo"], e * E_PARTS + E_PARTS)
                if not first:
                    pe.wait_ge(S["y_act"], s)
                    pe.wait_ge(S["y_dve"], s)
                for h in range(2):
                    for k in range(F // P):
                        last = product(bank[5 + h][:, :], hT_hi[:, k, :], hT_lo[:, k, :], e & 1, GU + k * D + 512 * h,
                                       k == 0, k == F // P - 1)
                last.then_inc(S["dn_mm"], 1)

            turn_x(0, 0, 1, first=True)
            gate_up(0, 0)
            turn_x(1, 1, 1)
            turn_h(0)
            for s in (1, 2):
                gate_up(s, s % 2)
                turn_x(s + 1, (s + 1) % 2, (s + 1) // 2 + 1)
                down(s - 1, first=s == 1)
                turn_h(s)
            with pe.Fori(1, SLOTS // 2 - 1) as j:
                for b in range(2):
                    s = 2 * j + 1 + b
                    gate_up(s, 1 - b)
                    turn_x(s + 1, b, j + 2 if b else j + 2)
                    down(s - 1)
                    turn_h(s)
            s = SLOTS - 1
            gate_up(s, 1)
            down(s - 1)
            turn_h(s)
            down(s)

            def combine(t, b, uses, n=P, first=False):
                pe.wait_ge(S["diag_ok"], 2 * t + 2)
                pe.wait_ge(S[f"ya{b}"], 16 * uses)
                pe.wait_ge(S[f"yb{b}"], 16 * uses)
                if not first:
                    pe.wait_ge(S["comb_used"], t - 1)
                for h in range(2):
                    for k, rows in enumerate((ya[b], yb[b])):
                        last = pe.matmul(bank[2 * b + h][0:n, :], dg[b][0:n, k, 0:n], rows[0:n, 512 * h:512 * h + 512],
                                         start=k == 0, stop=k == 1)
                last.then_inc(S["comb_mm"], 1)

            pe.wait_ge(S["y_dve"], SLOTS)
            combine(0, 0, 1, first=True)
            combine(1, 1, 1, first=True)
            with pe.Fori(1, NT // 2) as j:
                for b in range(2):
                    combine(2 * j + b, b, j + 1)
            combine(NT - 1, 0, NT // 2 + 1, NS)


CHUNK_STEPS = 66
LN_STEPS = 14
FIN_STEPS = 12

_INS = ['x_prompt', 'x_sample', 'c_prompt', 'c_sample', 'state_pool', 'state_conv', 'state_lru', 'w_ada', 'b_ada', 'w_in',
        'w_pool', 'pool_scale', 'w_conv', 'b_conv', 'w_a', 'b_a', 'w_x', 'b_x', 'lru_lambda', 'w_out', 'ln1_g', 'ln1_b',
        'w_group', 'b_group', 'w_route', 'b_route', 'w_gate', 'w_up', 'w_down', 'ln2_g', 'ln2_b']
_OUTS = [(1, SEQ, D), (DEC_B, DEC_T, D), (1, 1, PB, DH), (1, 1, CB, DH), (1, 1, DH),
         (1, DEC_B, PB, DH), (1, DEC_B, CB, DH), (1, DEC_B, DH)]


def kernel(**inputs):
    import numpy as _np
    import concourse.bacc as _bacc
    from concourse.bass_utils import run_bass_kernel_spmd as _run

    nc = _bacc.Bacc("TRN2", target_bir_lowering=False, num_devices=1)
    arrays, aps = {}, {}
    for name in _INS:
        a = _np.ascontiguousarray(inputs[name])
        arrays[f"in_{name}"] = a
        aps[name] = nc.dram_tensor(f"in_{name}", a.shape, mybir.dt.from_np(a.dtype), kind="ExternalInput").ap()
    for i, shape in enumerate(_OUTS):
        aps[f"out_{i}"] = nc.dram_tensor(f"result_{i}", shape, F32, kind="ExternalOutput").ap()
    build(nc, aps)
    r = _run(nc, [arrays], core_ids=[0])
    return tuple(r.results[0][f"result_{i}"] for i in range(len(_OUTS)))
```

```python
from contextlib import ExitStack

import concourse.bass as bass
from concourse import mybir

P = 128
D = 1024
KD = D // P
SEQ, DEC_B, DEC_T = 2048, 8, 8
NS = DEC_B * DEC_T
NTOK = SEQ + NS
C = 256
NCH = SEQ // C
TPC = C // P
NT = SEQ // P + 1
DH = 512
NG = DH // P
PB, CB = 15, 3
WINDOWS = (2, 4, 8, 16)
NM = DEC_B + 1
NE, NGR, EPG, F = 16, 4, 4, 256
GU, DN = KD * 2 * F, (F // P) * D
WE = GU + DN
SPLIT = 1024
GU_PARTS, DN_PARTS = GU // SPLIT, DN // SPLIT
E_PARTS = GU_PARTS + DN_PARTS
WIDE = 3 * DH
W_IN = KD * WIDE
PARTS = 2 * W_IN + 2 * KD * C
ARENA = 21168
NR = NGR + NE
SLOTS = (2 * NTOK + NE * P - 1) // P
ALPHA = 2.0 ** 0.25
LN_EPS = 1e-5
LRU_C = 8.0
BIG = 3.0e38

ALU = mybir.AluOpType
ACT = mybir.ActivationFunctionType
F32 = mybir.dt.float32
BF16 = mybir.dt.bfloat16
F32R = mybir.dt.float32r
I32 = mybir.dt.int32
AX = mybir.AxisListType.X
ds = bass.ds

SH1, SC1, G1, SH2, SC2, G2 = (n * D for n in range(6))
V_BCONV, V_BA, V_BX, V_LAM, V_PSCALE, V_WCONV = 0, 1, 2, 3, 4, 5
NV = 9


class Order:

    def __init__(self, eng, sem):
        self.eng, self.sem, self.base, self.n = eng, sem, 0, 0

    def did(self, ins):
        ins.then_inc(self.sem, 1)
        self.n += 1

    def wait(self):
        self.eng.wait_ge(self.sem, self.base + self.n)

    def step(self, ins):
        self.did(ins)
        self.wait()

    def enter(self, i, first, per):
        self.entry, self.per, self.first = self.base + self.n, per, first
        self.base, self.n = self.entry + (i - first) * per, 0

    def leave(self, trips):
        assert self.n == self.per, f"the loop's body counts {self.n}"
        self.base, self.n = self.entry + trips * self.per, 0


def build(nc, A):
    with ExitStack() as ctx:
        def sb(name, shape, dt=F32):
            return ctx.enter_context(nc.sbuf_tensor(name, shape, dt))

        def sem(name):
            return ctx.enter_context(nc.semaphore(name))

        bank = [ctx.enter_context(nc.psum_tensor(f"bank{n}", [P, 512], F32)) for n in range(8)]

        mod_d = nc.dram_tensor("mod_d", [NM, 6 * D], F32).ap()
        yT_d = nc.dram_tensor("yT_d", [NT, P, KD, P], F32).ap()
        x1_d = nc.dram_tensor("x1_d", [NTOK, D], F32).ap()
        u2_d = nc.dram_tensor("u2_d", [NTOK, D], F32).ap()
        ys_d = nc.dram_tensor("ys_d", [P * SLOTS, D], F32).ap()

        def place(arena, off, *shape):
            n = 1
            for s in shape:
                n *= s
            v = arena[:, off:off + n]
            if len(shape) == 2:
                v = v.rearrange("p (a b) -> p a b", b=shape[1])
            if len(shape) == 3:
                v = v.rearrange("p (a b c) -> p a b c", b=shape[1], c=shape[2])
            return v

        arena = sb("arena", [P, ARENA])
        with nc.sbuf_tensor("ada_arena", [P, PARTS], F32) as ada_arena:
            pass
        parts = sb("parts", [P, PARTS], F32R)

        def at(off, *shape):
            return place(arena, off, *shape)

        def part_at(off, *shape):
            return place(parts, off, *shape)

        w_in_hi, w_in_lo = part_at(0, KD, WIDE), part_at(W_IN, KD, WIDE)
        uT_hi, uT_lo = part_at(2 * W_IN, KD, C), part_at(2 * W_IN + KD * C, KD, C)
        w_in = at(8880, KD, WIDE)
        xin = at(0, TPC, D)
        xs = at(2048, D)
        gel_s = at(6728, NG, NS)
        rows_s = at(2048, 3, DH)
        uTs = at(6208, KD, NS + 1)
        p_s = arena[:, 3584:3584 + NG * DEC_B * (PB + DEC_T)].rearrange("p (g s t) -> p g s t", g=NG, s=DEC_B)
        xr_s = arena[:, 4320:4320 + NG * DEC_B * (CB + DEC_T)].rearrange("p (g s t) -> p g s t", g=NG, s=DEC_B)
        prj_s = at(4672, 2 * NG, NS)
        row_a, row_b, row_c, row_v = at(5184, DH), at(5696, DH), at(6208, DH), at(6720, DH)
        wa, wx, wp = at(7232, NG, P), at(7744, NG, P), at(8256, NG, P)
        p_buf = at(9792, NG, PB + C)
        xr_buf = at(10876, NG, CB + C)
        xc = at(11912, NG, C)
        gel = at(12936, NG, C)
        tT, tI, tS = at(13960, NG, C), at(14984, NG, C), at(16008, NG, C)
        q_t, a_t, b_t, h_t = at(17032, C), at(17288, C), at(17544, C), at(17800, C)
        wsum = [at(18056, PB + C), at(18328, PB + C)]
        dif = at(18600, 2, C)
        yT = at(19112, KD, C)
        row_d, row_e = at(18600, DH), at(18056, DH)
        w_ada = [place(ada_arena, 10240 + n * 4096, KD, 512) for n in range(3)]
        mod = place(ada_arena, 22528, 6 * D)
        c_rows = at(0, D)
        w_out_hi, w_out_lo = part_at(0, KD, D), part_at(KD * D, KD, D)
        yT_hi = [part_at(2 * KD * D + n * 2048, KD, P) for n in range(2)]
        yT_lo = [part_at(2 * KD * D + 1024 + n * 2048, KD, P) for n in range(2)]
        w_out = [at(k * D if k < KD - 1 else 8768, D) for k in range(KD)]
        yTt = [at(n * 1024, KD, P) for n in range(2)]
        xres = [at(2048 + n * 1024, D) for n in range(2)]
        row_tiles = at(4096, 5, D)
        w_rt = at(9216, KD, NR)
        b_rt = at(9376, NR)
        u2T = at(9792, KD, P)
        z = [at(11912 + n * 1024, D) for n in range(2)]
        x1 = [at(13960 + n * 1024, D) for n in range(2)]
        u2 = [at(16008 + n * 1024, D) for n in range(2)]
        row_tiles_s = at(18056, 3, D)
        w_hi, w_lo = part_at(0, 2, WE), part_at(2 * WE, 2, WE)
        xT_hi, xT_lo = part_at(4 * WE, KD, P), part_at(4 * WE + KD * P, KD, P)
        hT_hi, hT_lo = (part_at(4 * WE + 2 * KD * P + n * F, F // P, P) for n in range(2))
        w_raw = [at(n * WE, WE) for n in (1, 0)]
        w_gu = [w[:, 0:GU].rearrange("p (k n) -> p k n", k=KD) for w in w_raw]
        w_dn = [w[:, GU:WE].rearrange("p (k n) -> p k n", k=F // P) for w in w_raw]
        w_raw2 = at(0, 2, WE)
        xg = [at(12288 + n * 1024, D) for n in range(2)]
        y_sb = [at(14336 + n * 1024, D) for n in range(2)]
        hid, sil = at(16384, F), at(16640, F)
        ya = [at(n * 1024, D) for n in range(4)]
        yb = [at(off, D) for off in (4096, 5120, 12288, 13312)]
        xo = [at(6144 + n * 1024, D) for n in range(2)]
        oo = [at(8192 + n * 1024, D) for n in range(2)]
        z2 = [at(10240 + n * 1024, D) for n in range(2)]
        dg = [at(16384 + n * 256, 2, P) for n in range(2)]
        fin_tiles = at(16896, 3, D)
        fin_tile_s = at(19968, D)
        rt = [at(n * 272, NT, NE) for n in range(6)]
        rt_f = [at(1632 + n * 68, NT, NGR) for n in range(9)]
        r17 = [at(2248 + n * NT, NT) for n in range(10)]
        big_t = at(2424, NE, NT)
        lt_prod = at(2700, NE, NE)
        slot_ge = at(2960, SLOTS, NE)
        hot_b = at(12288, 2 * NT * SLOTS).bitcast(BF16).rearrange("p (k t v s) -> p k t v s", k=2, t=NT, v=2)
        hot_a = at(13960, 2 * NT * P // 2).bitcast(BF16).rearrange("p (k t r) -> p k t r", k=2, t=NT)
        e48 = [at(4050 + n * SLOTS, SLOTS) for n in range(2)]
        e16 = [at(3960 + n * NE, NE) for n in range(5)]

        uI = sb("uI", [P, C])
        logits = sb("logits", [P, NT, NR])
        proj_b = sb("proj_b", [P, 3 * NG])
        ident = sb("ident", [P, P])
        tri = sb("tri", [P, P])
        ones = sb("ones", [P, P])
        cT = sb("cT", [P, KD, NM])
        modT = sb("modT", [P, 2 * KD, NM])
        vecT = sb("vecT", [P, NG, NV])
        sp_t = sb("sp_t", [P, 5, NG])
        sp2 = sb("sp2", [P, NG])
        half_b = sb("half_b", [P, NG, 2])
        inv_cnt = sb("inv_cnt", [P, NG, 16])
        fix = sb("fix", [P, 16])
        h_last = sb("h_last", [P, NG])
        h0_s = sb("h0_s", [P, NG, DEC_B])
        st6 = [sb(f"st6_{n}", [P, 2, 6]) for n in range(2)]
        mv = [sb(f"mv{n}", [P, 2]) for n in range(2)]
        sd = [sb(f"sd{n}", [P, 1]) for n in range(2)]
        rs = [sb(f"rs{n}", [P, 2]) for n in range(2)]
        prio = sb("prio", [P, EPG])
        lt16 = sb("lt16", [P, NE, NE])
        iota17 = sb("iota17", [P, NT])
        iota_s = sb("iota_s", [P, SLOTS])
        iota_r = sb("iota_r", [P, P])
        part_i = sb("part_i", [P, 1])
        valid = sb("valid", [P, NT])
        wgt = sb("wgt", [P, 2, NT])
        pos_i = sb("pos_i", [P, 2, NT], I32)
        pos_a = sb("pos_a", [P, 2, NT], I32)
        pos_b = sb("pos_b", [P, 2, NT], I32)
        pos_f = sb("pos_f", [P, 4, NT])
        tok_i = sb("tok_i", [P, SLOTS], I32)
        slot_e = sb("slot_e", [P, SLOTS])
        slot_ei = sb("slot_ei", [P, 2, SLOTS], I32)
        tok_now = [sb(f"tok_now{n}", [P, 1], I32) for n in range(2)]
        pos_now = [sb(f"pos_now{n}", [P, 2], I32) for n in range(4)]
        spare = sb("spare", [1, 2])
        hP = sb("hP", [NG, P])

        S = {n: sem(n) for n in """consts small_in c_in vec_in ba_in gates_in gates_zero wpool_in st_in x_loaded xs_loaded w_in_in
            ada0 ada1 ada2 cT_mm cT_ok ada_mm ada_ok mod_ok modT_mm modT_ok vec_mm vec_ok st_mm xsT_mm mod_stored
            dve_order act_order pool_order xT_ready uT_hi_ok uT_lo_ok uTs_ready rows_mm rows_ok win_hi win_lo_pool win_lo_dve wout_hi wout_lo_pool wout_lo_dve yT_hi_ok yT_lo_ok gate_in proj_ready proj_evac xc_ready xr_free p_free
            gates_mm gates_evac T_ready T_guard S_ready gated_x h_ready d_ready pool_mm pool_evac ylru_ready y_stored prj_copied
            out_mm out_evac out_stored out_s_stored w_out_in tiles_in tiles_s_in rt_in yTt0 yTt1 xres0 xres1 mix_ready mix_used
            var_ready sd_ready z_scaled z_norm u2_ready x1_ready x1_st0 x1_st1 u2_st0 u2_st1 u2T_mm u2T_ok rt_mm rt_ok
            m_ready cnt_mm w_exp w_expd hot_ready idx_mm idx_ready w_raw0 w_raw1 xg0 xg1 xgT_mm w_hi w_lo w0_lo xT_hi_ok xT_lo_ok
            gu_mm sil_ok hid_ok hT_mm hT_hi_ok hT_lo_ok dn_mm y_act y_dve ys0 ys1 fin_in fin_s_in ya0 ya1 ya2 ya3 yb0 yb1 yb2 yb3 xo0 xo1
            diag_ok wgt_ok comb_mm comb_used fvar_ready fsd_ready fz_ok fnorm fg_ok fo_ok os0 os1""".split()}

        block = ctx.enter_context(nc.Block())
        xp_d = A["x_prompt"].rearrange("b (c t p) d -> c p (b t) d", t=TPC, p=P)
        xpt_d = A["x_prompt"].rearrange("b (t p) d -> (b t) p d", p=P)
        xs_d = A["x_sample"].rearrange("b t d -> (b t) d")
        ada_d = A["w_ada"][0].rearrange("(k p) (g n) -> g p k n", p=P, n=512)
        yt_p, yt_s = A["out_0"].rearrange("b (t p) d -> (b t) p d", p=P), A["out_1"].rearrange("b t d -> (b t) d")
        gate_d = A["w_gate"][0].rearrange("e (k p) f -> e p k f", p=P)
        up_d = A["w_up"][0].rearrange("e (k p) f -> e p k f", p=P)
        down_d = A["w_down"][0].rearrange("e (k p) n -> e p k n", p=P)
        x1_t = x1_d[0:SEQ, :].rearrange("(t p) d -> t p d", p=P)
        u2_t = u2_d[0:SEQ, :].rearrange("(t p) d -> t p d", p=P)
        ys_t = ys_d.rearrange("(p s) d -> s p d", s=SLOTS)

        def turn_bank(k):
            return (0, 1, 6, 7)[k % 4]

        def part(w, buf, n):
            return w[:, ds(buf, 1), n * SPLIT:(n + 1) * SPLIT].rearrange("p a n -> p (a n)")

        def raw_part(buf, n):
            return w_raw2[:, ds(buf * -1 + 1, 1), n * SPLIT:(n + 1) * SPLIT].rearrange("p a n -> p (a n)")

        def all_parts(row, n=P):
            return row.rearrange("(a d) -> a d", a=1).broadcast_to([n, row.shape[0]])

        @block.sync
        def _(sp):
            sp.dma_start(c_rows[0:1, :], A["c_prompt"]).then_inc(S["c_in"], 16)
            sp.dma_start(c_rows[1:NM, :], A["c_sample"]).then_inc(S["c_in"], 16)
            for n in range(3):
                sp.dma_start(w_ada[n], ada_d[n]).then_inc(S[f"ada{n}"], 16)
            sp.dma_start(mod[0:NM, :], all_parts(A["b_ada"][0], NM)).then_inc(S["ba_in"], 16)
            for r, name in enumerate(("b_conv", "b_a", "b_x", "lru_lambda", "pool_scale")):
                sp.dma_start(row_v[r:r + 1, :], A[name]).then_inc(S["vec_in"], 16)
            sp.dma_start(row_v[V_WCONV:NV, :], A["w_conv"][0]).then_inc(S["vec_in"], 16)
            sp.dma_start(row_a[0:DEC_B * PB, :], A["state_pool"][0].rearrange("b t c -> (b t) c")).then_inc(S["st_in"], 16)
            sp.dma_start(row_b[0:DEC_B * CB, :], A["state_conv"][0].rearrange("b t c -> (b t) c")).then_inc(S["st_in"], 16)
            sp.dma_start(row_c[0:DEC_B, :], A["state_lru"][0]).then_inc(S["st_in"], 16)
            sp.dma_start(xs[0:NS, :], xs_d).then_inc(S["xs_loaded"], 16)
            sp.dma_start(w_in, A["w_in"][0].rearrange("(k p) n -> p k n", p=P)).then_inc(S["w_in_in"], 16)
            with sp.Fori(1, 4) as j:
                for n in range(3):
                    sp.wait_ge(S["ada_mm"], 3 * j + n - 2)
                    sp.dma_start(w_ada[n], ada_d[ds(3 * j + n, 1)].rearrange("a p k n -> p (a k) n")).then_inc(S[f"ada{n}"], 16)
            sp.dma_start(xin, xp_d[0]).then_inc(S["x_loaded"], 16)
            sp.wait_ge(S["gates_zero"], 1)
            for w, name in ((wa, "w_a"), (wx, "w_x")):
                heads = A[name][0].rearrange("(j q) i o -> q i j o", q=2)
                for q in range(2):
                    sp.dma_start(w[64 * q:64 * q + 64, :, 64 * q:64 * q + 64], heads[q]).then_inc(S["gates_in"], 16)
            sp.dma_start(wp, A["w_pool"][0].rearrange("g i o -> i g o")).then_inc(S["wpool_in"], 16)
            sp.dma_start(A["out_5"][0][:, 0:PB - DEC_T, :], A["state_pool"][0][:, DEC_T:PB, :]).then_inc(S["out_stored"], 16)
            sp.wait_ge(S["mod_ok"], 1)
            sp.dma_start(mod_d[:, 2 * D:6 * D], mod[0:NM, 2 * D:6 * D]).then_inc(S["mod_stored"], 16)

            def load_x(i):
                sp.wait_ge(S["xT_ready"], KD * (i - 1))
                sp.dma_start(xin, xp_d[ds(i - 1, 1)].rearrange("a p t d -> p (a t) d")).then_inc(S["x_loaded"], 16)

            def store_y(i):
                sp.wait_ge(S["pool_evac"], NG * i + NG)
                sp.wait_ge(S["ylru_ready"], NG * i + NG)
                for t in range(TPC):
                    sp.dma_start(yT_d[ds(TPC * (i - 1) + t, 1)].rearrange("a p k n -> p (a k) n"),
                                 yT[:, :, t * P:(t + 1) * P]).then_inc(S["y_stored"], 16)

            sp.wait_ge(S["pool_evac"], NG)
            sp.wait_ge(S["ylru_ready"], NG)
            sp.dma_start(yT_d[NT - 1][:, :, 0:NS], yT[:, :, 0:NS]).then_inc(S["y_stored"], 16)
            with sp.Fori(1, NCH) as i:
                load_x(i + 1)
                store_y(i)
            sp.wait_ge(S["out_evac"], 3)
            for s in range(DEC_B):
                sp.dma_start(A["out_5"][0, s, PB - DEC_T:PB, :], row_a[s * DEC_T:(s + 1) * DEC_T, :]).then_inc(S["out_s_stored"], 16)
                sp.dma_start(A["out_6"][0, s], row_b[(s + 1) * DEC_T - CB:(s + 1) * DEC_T, :]).then_inc(S["out_s_stored"], 16)
            sp.dma_start(A["out_7"][0], row_c[0:DEC_B, :]).then_inc(S["out_s_stored"], 16)
            sp.wait_ge(S["out_s_stored"], 16 * (1 + 2 * DEC_B))
            w_out_d = A["w_out"][0].rearrange("(k p) n -> k p n", p=P)
            for k in (*range(2, KD), 0, 1):
                if k == 0:
                    sp.wait_ge(S["xT_ready"], KD * NCH)
                sp.dma_start(w_out[k], w_out_d[k]).then_inc(S["w_out_in"], 16)

            def load_rows():
                sp.wait_ge(S["wout_lo_dve"], KD // 2)
                sp.wait_ge(S["mod_stored"], 16)
                rows = (mod_d[0, G1:G1 + D], A["ln1_g"][0], A["ln1_b"][0], mod_d[0, SC2:SC2 + D], mod_d[0, SH2:SH2 + D])
                for n, row in enumerate(rows):
                    sp.dma_start(row_tiles[:, n, :], all_parts(row)).then_inc(S["gate_in" if n == 0 else "tiles_in"], 16)
                sp.dma_start(w_rt[:, :, 0:NGR], A["w_group"][0].rearrange("(k p) n -> p k n", p=P)).then_inc(S["rt_in"], 16)
                sp.dma_start(w_rt[:, :, NGR:NR], A["w_route"][0].rearrange("(k p) n -> p k n", p=P)).then_inc(S["rt_in"], 16)
                sp.dma_start(b_rt[:, 0:NGR], all_parts(A["b_group"][0])).then_inc(S["rt_in"], 16)
                sp.dma_start(b_rt[:, NGR:NR], all_parts(A["b_route"][0])).then_inc(S["rt_in"], 16)

            def store_states():
                sp.wait_ge(S["out_evac"], 6)
                sp.dma_start(A["out_2"][0, 0], row_d[0:PB, :]).then_inc(S["out_stored"], 16)
                sp.dma_start(A["out_3"][0, 0], row_e[0:CB, :]).then_inc(S["out_stored"], 16)
                sp.dma_start(A["out_4"].rearrange("a b (g c) -> (a b g) c", c=P), hP[:, :]).then_inc(S["out_stored"], 16)

            sp.wait_ge(S["y_stored"], 16 * TPC * (NCH - 1) + 16)
            sp.wait_ge(S["wout_lo_pool"], KD // 2)

            def load_y(t, b, n=P):
                src = yT_d[ds(t, 1)].rearrange("a p k n -> p (a k) n") if n == P else yT_d[NT - 1][:, :, 0:n]
                sp.dma_start(yTt[b][:, :, 0:n], src).then_inc(S[f"yTt{b}"], 16)

            def load_res(t, b, n=P):
                src = xpt_d[ds(t, 1)].rearrange("a p d -> (a p) d") if n == P else xs_d
                sp.dma_start(xres[b][0:n, :], src).then_inc(S[f"xres{b}"], 16)

            def load_next(t, b, n=P):
                sp.wait_ge(S["yT_lo_ok"], t + 1)
                load_y(t + 2, b, n)
                sp.wait_ge(S["mix_used"], t + 1)
                load_res(t + 2, b, n)

            def store_tile(t, b, n=P):
                sp.wait_ge(S["x1_ready"], t + 1)
                sp.wait_ge(S["u2_ready"], t + 1)
                dst_x = x1_t[ds(t, 1)].rearrange("a p d -> (a p) d") if n == P else x1_d[SEQ:NTOK, :]
                dst_u = u2_t[ds(t, 1)].rearrange("a p d -> (a p) d") if n == P else u2_d[SEQ:NTOK, :]
                sp.dma_start(dst_x, x1[b][0:n, :]).then_inc(S[f"x1_st{b}"], 16)
                sp.dma_start(dst_u, u2[b][0:n, :]).then_inc(S[f"u2_st{b}"], 16)

            def load_expert(e, b, static=False):
                for dst, src in ((w_gu[b][:, :, 0:F], gate_d), (w_gu[b][:, :, F:2 * F], up_d), (w_dn[b], down_d)):
                    src = src[e] if static else src[ds(e, 1)].rearrange("a p k n -> p (a k) n")
                    sp.dma_start(dst, src).then_inc(S[f"w_raw{b}"], 16)

            def load_sample_rows():
                sp.wait_ge(S["out_stored"], 64)
                for n, off in enumerate((G1, SC2, SH2)):
                    for s in range(DEC_B):
                        sp.dma_start(row_tiles_s[s * DEC_T:(s + 1) * DEC_T, n, :],
                                     all_parts(mod_d[s + 1, off:off + D], DEC_T)).then_inc(S["tiles_s_in"], 16)

            for b in range(2):
                load_y(b, b)
                load_res(b, b)
            load_rows()
            store_y(NCH)
            load_next(0, 0)
            load_next(1, 1)
            store_states()
            sp.wait_ge(S["y_stored"], 16 * TPC * NCH + 16)
            store_tile(0, 0)
            with sp.Fori(1, NT // 2 - 1) as j:
                for b in range(2):
                    load_next(2 * j + b, b)
                    store_tile(2 * j + b - 1, 1 - b)
            load_next(NT - 3, 0, NS)
            load_sample_rows()
            store_tile(NT - 4, 1)
            store_tile(NT - 3, 0)
            store_tile(NT - 2, 1)
            store_tile(NT - 1, 0, NS)
            sp.wait_ge(S["rt_ok"], NT)
            load_expert(0, 0, static=True)
            for b, n in ((0, NT // 2 + 1), (1, NT // 2)):
                sp.wait_ge(S[f"u2_st{b}"], 16 * n)
            sp.wait_ge(S["wgt_ok"], 1)
            load_expert(1, 1, static=True)
            with sp.Fori(1, NE // 2) as j:
                for b in range(2):
                    sp.wait_ge(S["w_lo"], E_PARTS * (2 * j + b - 1))
                    load_expert(2 * j + b, b)
            for n, row in enumerate((mod_d[0, G2:G2 + D], A["ln2_g"][0], A["ln2_b"][0])):
                sp.dma_start(fin_tiles[:, n, :], all_parts(row)).then_inc(S["fin_in"], 16)
            for s in range(DEC_B):
                sp.dma_start(fin_tile_s[s * DEC_T:(s + 1) * DEC_T, :], all_parts(mod_d[s + 1, G2:G2 + D], DEC_T)).then_inc(S["fin_s_in"], 16)
            sp.wait_ge(S["w_lo"], E_PARTS * (NE - 1))

            def load_x1(t, b, n=P):
                src = x1_t[ds(t, 1)].rearrange("a p d -> (a p) d") if n == P else x1_d[SEQ:NTOK, :]
                sp.dma_start(xo[b][0:n, :], src).then_inc(S[f"xo{b}"], 16)

            def store_o(t, b, n=P):
                sp.wait_ge(S["fo_ok"], t + 1)
                dst = yt_p[ds(t, 1)].rearrange("a p d -> (a p) d") if n == P else yt_s
                sp.dma_start(dst, oo[b][0:n, :]).then_inc(S[f"os{b}"], 16)

            load_x1(0, 0)
            load_x1(1, 1)
            for t in range(2):
                sp.wait_ge(S["comb_used"], t + 1)
                load_x1(t + 2, t)
            with sp.Fori(1, NT // 2 - 1) as j:
                for b in range(2):
                    sp.wait_ge(S["comb_used"], 2 * j + b + 1)
                    load_x1(2 * j + 2 + b, b)
                    store_o(2 * j + b - 2, b)
            store_o(NT - 5, 0)
            sp.wait_ge(S["comb_used"], NT - 2)
            load_x1(NT - 1, 0, NS)
            store_o(NT - 4, 1)
            store_o(NT - 3, 0)
            store_o(NT - 2, 1)
            store_o(NT - 1, 0, NS)
            sp.wait_ge(S["os0"], 16 * (NT // 2 + 1))
            sp.wait_ge(S["os1"], 16 * (NT // 2))
            sp.wait_ge(S["out_stored"], 64)

        @block.gpsimd
        def _(pool):
            o = Order(pool, S["pool_order"])
            o.did(pool.memset(ident[:], 0.0))
            o.did(pool.memset(tri[:], 1.0))
            o.did(pool.memset(lt16[:], 1.0))
            o.did(pool.memset(valid[:], 1.0))
            o.did(pool.iota(iota17[:], pattern=[[P, NT]], base=0, channel_multiplier=0, allow_small_or_imprecise_dtypes=True))
            o.did(pool.iota(iota_s[:], pattern=[[1, SLOTS]], base=0, channel_multiplier=0, allow_small_or_imprecise_dtypes=True))
            o.did(pool.iota(iota_r[:], pattern=[[1, P]], base=0, channel_multiplier=0, allow_small_or_imprecise_dtypes=True))
            o.did(pool.iota(part_i[:], pattern=[[0, 1]], base=0, channel_multiplier=1, allow_small_or_imprecise_dtypes=True))
            o.did(pool.iota(prio[:], pattern=[[-1, EPG]], base=EPG, channel_multiplier=0, allow_small_or_imprecise_dtypes=True))
            o.did(pool.memset(wa, 0.0))
            pool.memset(wx, 0.0).then_inc(S["gates_zero"], 1)
            o.did(pool.memset(ones[:], 1.0))
            o.wait()
            pool.affine_select(out=ident[:], in_=ident[:], compare_op=ALU.not_equal, fill=1.0, base=0,
                               pattern=[[-1, P]], channel_multiplier=1).then_inc(S["consts"], 1)
            pool.affine_select(out=tri[:], in_=tri[:], compare_op=ALU.is_gt, fill=0.0, base=0,
                               pattern=[[1, P]], channel_multiplier=-1).then_inc(S["consts"], 1)
            pool.affine_select(out=lt16[:], in_=lt16[:], compare_op=ALU.is_gt, fill=0.0, base=0,
                               pattern=[[1, NE], [-1, NE]], channel_multiplier=0).then_inc(S["consts"], 1)
            pool.affine_select(out=valid[:, NT - 1:NT], in_=valid[:, NT - 1:NT], compare_op=ALU.is_gt, fill=0.0, base=NS,
                               pattern=[[0, 1]], channel_multiplier=-1).then_inc(S["consts"], 1)

            for k in range(KD // 2):
                pool.wait_ge(S["win_hi"], k + 1)
                pool.wait_ge(S["ada_mm"], 10 + min(k, 1))
                pool.tensor_tensor(w_in_lo[:, k, :], w_in[:, k, :], w_in_hi[:, k, :].bitcast(F32),
                                   ALU.subtract).then_inc(S["win_lo_pool"], 1)
            def gate_input(i, n):
                for j in range(NG):
                    pool.wait_ge(S["gates_evac"], 2 * NG * i + 2 * j + 2)
                    o.step(pool.tensor_tensor(uI[:, 0:n], tI[:, j, 0:n], xc[:, j, 0:n], ALU.mult))
                    pool.tensor_tensor(tI[:, j, 0:n], uI[:, 0:n], xc[:, j, 0:n], ALU.add).then_inc(S["gated_x"], 1)
                    pool.wait_ge(S["gated_x"], NG * i + j + 1)

            def gate_output(i, n, h, gate):
                for j in range(NG):
                    pool.wait_ge(S["h_ready"], NG * i + j + 1)
                    pool.wait_ge(S["proj_evac"], 12 * i + 2 * NG + j + 1)
                    pool.tensor_tensor(yT[:, NG + j, 0:n], h(j), gate(j), ALU.mult).then_inc(S["ylru_ready"], 1)

            by_group = (lambda j: tI[:, j, :], lambda j: gel[:, j, :])
            gate_input(0, NS)
            gate_output(0, NS, lambda j: h_t[:, j * NS:(j + 1) * NS], lambda j: gel_s[:, j, :])
            with pool.Fori(1, NCH) as i:
                o.enter(i, 1, NG)
                gate_input(i, C)
                pool.wait_ge(S["y_stored"], 16 * TPC * i - 16 * TPC + 16)
                gate_output(i, C, *by_group)
            o.leave(NCH - 1)
            gate_input(NCH, C)

            def out_lo(k):
                pool.wait_ge(S["wout_hi"], k + 1)
                pool.tensor_tensor(w_out_lo[:, k, :], w_out[k], w_out_hi[:, k, :].bitcast(F32),
                                   ALU.subtract).then_inc(S["wout_lo_pool"], 1)

            def y_lo(t, b, n=P):
                pool.wait_ge(S["yT_hi_ok"], t + 1)
                pool.tensor_tensor(yT_lo[b][:, :, 0:n], yTt[b][:, :, 0:n], yT_hi[b][:, :, 0:n].bitcast(F32),
                                   ALU.subtract).then_inc(S["yT_lo_ok"], 1)

            for k in range(KD // 2):
                out_lo(k)
            y_lo(0, 0)
            y_lo(1, 1)
            pool.wait_ge(S["y_stored"], 16 * TPC * (NCH - 1) + 16)
            gate_output(NCH, C, *by_group)
            y_lo(2, 0)
            pool.wait_ge(S["tiles_in"], 64)

            def x1_tile(t, b, n=P, first=False):
                pool.wait_ge(S["z_norm"], t + 1)
                if not first:
                    pool.wait_ge(S[f"x1_st{b}"], 16 * x1_tile.uses(t))
                o.step(pool.tensor_tensor(x1[b][0:n, :], z[b][0:n, :], row_tiles[0:n, 1, :], ALU.mult))
                pool.tensor_tensor(x1[b][0:n, :], x1[b][0:n, :], row_tiles[0:n, 2, :], ALU.add).then_inc(S["x1_ready"], 1)

            x1_tile.uses = lambda t: t
            x1_tile(0, 0, first=True)
            y_lo(3, 1)
            x1_tile(1, 1, first=True)
            with pool.Fori(1, NT // 2 - 1) as j:
                o.enter(j, 1, 2)
                x1_tile.uses = lambda t: j
                for b in range(2):
                    y_lo(2 * j + b + 2, b)
                    x1_tile(2 * j + b, b)
            o.leave(NT // 2 - 2)
            x1_tile.uses = lambda t: t // 2
            y_lo(NT - 1, 0, NS)
            x1_tile(NT - 3, 0)
            x1_tile(NT - 2, 1)
            x1_tile(NT - 1, 0, NS)

            for n in range(E_PARTS):
                cols = slice(n * SPLIT, (n + 1) * SPLIT)
                pool.wait_ge(S["w_hi"], n + 1)
                pool.tensor_tensor(w_lo[:, 0, cols], w_raw[0][:, cols], w_hi[:, 0, cols].bitcast(F32),
                                   ALU.subtract).then_inc(S["w0_lo"], 1)
            pool.wait_ge(S["idx_ready"], 1)
            for b, n in ((0, NT // 2 + 1), (1, NT // 2)):
                pool.wait_ge(S[f"u2_st{b}"], 16 * n)
                pool.wait_ge(S[f"x1_st{b}"], 16 * n)

            def gather(s, b):
                o.did(pool.tensor_copy(tok_now[b][:], tok_i[:, ds(s, 1)]))
                o.wait()
                pool.tensor_tensor(spare[0:1, 1:2], ones[0:1, 0:1], ones[0:1, 0:1], ALU.mult)
                pool.indirect_dma_start(out=xg[b], out_offset=None, in_=u2_d,
                                        in_offset=bass.IndirectOffsetOnAxis(ap=tok_now[b][:, 0:1], axis=0)).then_inc(S[f"xg{b}"], 16)

            gather(0, 0)
            gather(1, 1)
            with pool.Fori(1, SLOTS // 2) as j:
                o.enter(j, 1, 2)
                for b in range(2):
                    pool.wait_ge(S["xgT_mm"], 4 * j + 2 * b - 2)
                    gather(2 * j + b, b)
            o.leave(SLOTS // 2 - 1)

            for b in range(2):
                pool.wait_ge(S[f"ys{b}"], 16 * (SLOTS // 2))

            def gather_y(t, b, n=P):
                for k in range(2):
                    o.did(pool.tensor_copy(pos_now[b][:, k:k + 1], pos_i[:, k, ds(t, 1)]))
                o.wait()
                pool.tensor_tensor(spare[0:1, 1:2], ones[0:1, 0:1], ones[0:1, 0:1], ALU.mult)
                for buf, k, name in ((ya, 0, "ya"), (yb, 1, "yb")):
                    pool.indirect_dma_start(out=buf[b][0:n, :], out_offset=None, in_=ys_d,
                                            in_offset=bass.IndirectOffsetOnAxis(ap=pos_now[b][0:n, k:k + 1], axis=0)
                                            ).then_inc(S[f"{name}{b}"], 16)

            def scale_o(t, b, n=P):
                pool.wait_ge(S["fnorm"], t + 1)
                pool.tensor_tensor(z2[b][0:n, :], z2[b][0:n, :], fin_tiles[0:n, 1, :], ALU.mult).then_inc(S["fg_ok"], 1)

            for t in range(4):
                gather_y(t, t)
            pool.wait_ge(S["fin_in"], 48)
            with pool.Fori(1, NT // 4) as j:
                o.enter(j, 1, 8)
                for b in range(4):
                    pool.wait_ge(S["comb_mm"], 4 * j + b - 3)
                    gather_y(4 * j + b, b)
                    scale_o(4 * j + b - 4, b % 2)
            o.leave(NT // 4 - 1)
            pool.wait_ge(S["comb_mm"], NT - 4)
            gather_y(NT - 1, 0, NS)
            for t in range(NT - 5, NT):
                scale_o(t, t % 2, P if t < NT - 1 else NS)

        @block.scalar
        def _(act):
            o = Order(act, S["act_order"])
            act.wait_ge(S["vec_ok"], 1)
            o.step(act.activation(sp_t[:, 0, :], vecT[:, :, V_LAM], ACT.Abs))
            o.did(act.activation(sp_t[:, 1, :], sp_t[:, 0, :], ACT.Exp, scale=-1.0))

            act.wait_ge(S["w_in_in"], 16)
            for k in range(KD):
                if k == 6:
                    act.wait_ge(S["ada_mm"], 10)
                act.activation(w_in_hi[:, k, :], w_in[:, k, :], ACT.Copy).then_inc(S["win_hi"], 1)

            def uT_evac(i):
                for k in range(KD):
                    act.wait_ge(S["xT_ready"], KD * (i - 1) + k + 1)
                    act.activation(uT_hi[:, k, :], bank[turn_bank(k)][:, 0:C], ACT.Copy,
                                   scale=modT[:, KD + k, 0:1]).then_inc(S["uT_hi_ok"], 1)

            def chunk(i, last=False):
                for m in range(2 * NG):
                    j = m % NG
                    act.wait_ge(S["proj_ready"], 12 * i + m + 1)
                    if m < NG:
                        act.wait_ge(S["xr_free"], NG * i - NG + j + 1)
                        dst = xr_buf[:, j, CB:CB + C]
                    else:
                        act.wait_ge(S["p_free"], NG * i - NG + j + 1)
                        dst = p_buf[:, j, PB:PB + C]
                    act.activation(dst, bank[2 + m % 2][:, 0:C], ACT.Identity, bias=proj_b[:, m:m + 1]).then_inc(S["proj_evac"], 1)
                gates(i, C, False)
                for j in range(NG):
                    act.wait_ge(S["proj_ready"], 12 * i + 2 * NG + j + 1)
                    act.wait_ge(S["ylru_ready"], NG * i - NG + j + 1)
                    act.activation(gel[:, j, :], bank[2 + j % 2][:, 0:C], ACT.Gelu_apprx_tanh,
                                   bias=proj_b[:, 2 * NG + j:2 * NG + j + 1]).then_inc(S["proj_evac"], 1)
                    if j == 0:
                        act.wait_ge(S["y_stored"], 16 * TPC * i - 16 * TPC + 16)
                    else:
                        pool_evac(i, j - 1, C)
                pool_evac(i, NG - 1, C)
                if not last:
                    uT_evac(i + 1)
                else:
                    act.wait_ge(S["w_out_in"], 16 * KD)
                    act.wait_ge(S["proj_ready"], 12 * NCH + 12)
                    for k in range(KD):
                        act.activation(w_out_hi[:, k, :], w_out[k], ACT.Copy).then_inc(S["wout_hi"], 1)
                roots(i, C)

            def gates(i, n, first):
                for j in range(NG):
                    if not first:
                        act.wait_ge(S["ylru_ready"], NG * i - NG + j + 1)
                    for q, dst in ((0, tT), (1, tI)):
                        act.wait_ge(S["gates_mm"], 2 * NG * i + 2 * j + q + 1)
                        act.activation(dst[:, j, 0:n], bank[4 + q][:, 0:n], ACT.Tanh, bias=half_b[:, j, q:q + 1],
                                       scale=0.5).then_inc(S["gates_evac"], 1)
                    act.wait_ge(S["gates_evac"], 2 * NG * i + 2 * j + 2)
                    act.activation(tT[:, j, 0:n], tT[:, j, 0:n], ACT.Tanh, bias=sp2[:, j:j + 1],
                                   scale=sp2[:, j:j + 1]).then_inc(S["T_ready"], 1)

            def roots(i, n):
                for j in range(NG):
                    act.wait_ge(S["T_guard"], NG * i + j + 1)
                    act.activation(tS[:, j, 0:n], tT[:, j, 0:n], ACT.Sqrt).then_inc(S["S_ready"], 1)

            def pool_evac(i, g, n):
                act.wait_ge(S["pool_mm"], NG * i + g + 1)
                act.activation(yT[:, g, 0:n], bank[6 + g % 2][:, 0:n], ACT.Copy,
                               scale=vecT[:, g, V_PSCALE:V_PSCALE + 1]).then_inc(S["pool_evac"], 1)

            act.wait_ge(S["modT_ok"], 1)
            act.wait_ge(S["vec_ok"], 2)
            for n in range(3):
                act.wait_ge(S["rows_mm"], n + 1)
                act.activation(rows_s[0:NS + 1, n, :], bank[2 + n][0:NS + 1, :], ACT.Copy).then_inc(S["rows_ok"], 1)
            for n, dst in enumerate((xr_s[:, :, :, CB:CB + DEC_T], p_s[:, :, :, PB:PB + DEC_T], None)):
                act.wait_ge(S["proj_ready"], NG * (n + 1))
                src = bank[2 + n][:, 0:NG * (NS + 1)].rearrange("p (g t) -> p g t", g=NG)
                o.did(act.activation(proj_b[:, NG * n:NG * n + NG].unsqueeze(2), src[:, :, NS:NS + 1], ACT.Copy))
                if dst is not None:
                    for g in range(NG):
                        act.activation(dst[:, g], src[:, g, 0:NS].rearrange("p (s t) -> p s t", s=DEC_B),
                                       ACT.Copy).then_inc(S["proj_evac"], 1)
                else:
                    act.activation(gel_s, src[:, :, 0:NS], ACT.Gelu_apprx_tanh).then_inc(S["proj_evac"], NG)
            gates(0, NS, True)
            for g in range(NG):
                pool_evac(0, g, NS)
            uT_evac(1)
            roots(0, NS)
            o.wait()
            with act.Fori(1, NCH) as i:
                chunk(i)

            def state_rows(n, dst, rows, cols):
                act.wait_ge(S["out_mm"], n + 1)
                act.activation(dst[0:rows, 0:cols], bank[7][0:rows, 0:cols], ACT.Copy).then_inc(S["out_evac"], 1)

            for n, (dst, rows, cols) in enumerate(((row_a, NS, DH), (row_b, NS, DH), (row_c, DEC_B, DH))):
                state_rows(n, dst, rows, cols)
            chunk(NCH, last=True)

            def split_y(t, b, uses, n=P, first=False):
                act.wait_ge(S[f"yTt{b}"], 16 * uses)
                if not first:
                    act.wait_ge(S["mix_ready"], t - 1)
                act.activation(yT_hi[b][:, :, 0:n], yTt[b][:, :, 0:n], ACT.Copy).then_inc(S["yT_hi_ok"], 1)

            def u2T_evac(t):
                for h in range(2):
                    act.wait_ge(S["u2T_mm"], 2 * t + h + 1)
                    act.activation(u2T[:, 4 * h:4 * h + 4, :], bank[4 + h][:, :].rearrange("p (k n) -> p k n", n=P),
                                   ACT.Copy).then_inc(S["u2T_ok"], 1)

            def norm(t, b, n=P):
                act.wait_ge(S["var_ready"], 2 * t + 1)
                act.activation(sd[b][0:n, :], mv[b][0:n, 1:2], ACT.Sqrt).then_inc(S["sd_ready"], 1)
                act.wait_ge(S["var_ready"], 2 * t + 2)
                act.activation(z[b][0:n, :], z[b][0:n, :], ACT.Identity, bias=rs[b][0:n, 1:2],
                               scale=rs[b][0:n, 0:1]).then_inc(S["z_norm"], 1)

            split_y(0, 0, 1, first=True)
            split_y(1, 1, 1, first=True)
            split_y(2, 0, 2)
            norm(0, 0)
            split_y(3, 1, 2)
            norm(1, 1)
            for n, (dst, rows, cols) in enumerate(((row_d, PB, DH), (row_e, CB, DH), (hP, NG, P))):
                state_rows(3 + n, dst, rows, cols)
            with act.Fori(1, NT // 2 - 1) as j:
                for b in range(2):
                    u2T_evac(2 * j + b - 2)
                    split_y(2 * j + b + 2, b, j + 2)
                    norm(2 * j + b, b)
            u2T_evac(NT - 5)
            split_y(NT - 1, 0, NT // 2 + 1, NS)
            norm(NT - 3, 0)
            u2T_evac(NT - 4)
            norm(NT - 2, 1)
            u2T_evac(NT - 3)
            norm(NT - 1, 0, NS)
            u2T_evac(NT - 2)
            for h in range(2):
                act.wait_ge(S["u2T_mm"], 2 * (NT - 1) + h + 1)
                act.activation(u2T[:, 4 * h:4 * h + 4, 0:NS], bank[4 + h][:, :].rearrange("p (k n) -> p k n", n=P)[:, :, 0:NS],
                               ACT.Copy).then_inc(S["u2T_ok"], 1)
            act.wait_ge(S["w_exp"], 1)
            act.activation(rt_f[8], rt_f[8], ACT.Exp).then_inc(S["w_expd"], 1)
            act.activation(r17[4], r17[4], ACT.Exp).then_inc(S["w_expd"], 1)

            act.wait_ge(S["w_raw0"], 48)
            for n in range(E_PARTS):
                cols = slice(n * SPLIT, (n + 1) * SPLIT)
                act.activation(w_hi[:, 0, cols], w_raw[0][:, cols], ACT.Copy).then_inc(S["w_hi"], 1)

            def next_expert(s):
                return act.value_load(slot_ei[0:1, 1, ds(s, 1)], min_val=0, max_val=NE - 1)

            def split_next(e, parts):
                with act.If(e > 0):
                    act.wait_ge(S["w_raw0"], (e >> 1) * 48 + 48)
                    act.wait_ge(S["w_raw1"], ((e + 1) >> 1) * 48)
                    for n in parts:
                        act.activation(part(w_hi, e & 1, n), raw_part(e & 1, n), ACT.Copy).then_inc(S["w_hi"], 1)

            def x_evac(s):
                for h in range(2):
                    act.wait_ge(S["xgT_mm"], 2 * s + h + 1)
                    act.activation(xT_hi[:, 4 * h:4 * h + 4, :], bank[h][:, :].rearrange("p (k n) -> p k n", n=P),
                                   ACT.Copy).then_inc(S["xT_hi_ok"], 1)

            def silu(s, b):
                act.wait_ge(S["gu_mm"], s + 1)
                act.activation(sil, bank[2 + b][:, 0:F], ACT.Silu).then_inc(S["sil_ok"], 1)

            def hT_evac(s):
                act.wait_ge(S["hT_mm"], s + 1)
                act.activation(hT_hi[:, :, :], bank[4][:, 0:F].rearrange("p (k n) -> p k n", n=P), ACT.Copy).then_inc(S["hT_hi_ok"], 1)

            def y_evac(s, b, before=None):
                act.wait_ge(S["dn_mm"], s + 1)
                if before is not None:
                    act.wait_ge(S[f"ys{b}"], 16 * before)
                act.activation(y_sb[b][:, 0:512], bank[5][:, :], ACT.Copy).then_inc(S["y_act"], 1)
                act.wait_ge(S["y_act"], s + 1)
                act.wait_ge(S["y_dve"], s + 1)
                act.dma_start(ys_t[ds(s, 1)].rearrange("a p d -> (a p) d"), y_sb[b]).then_inc(S[f"ys{b}"], 16)

            act.wait_ge(S["idx_ready"], 1)
            slots = [next_expert(s) for s in range(3)]
            x_evac(0)
            silu(0, 0)
            x_evac(1)
            hT_evac(0)
            split_next(slots[0], range(GU_PARTS))
            for s in (1, 2):
                silu(s, s % 2)
                x_evac(s + 1)
                split_next(slots[s - 1], range(GU_PARTS, E_PARTS))
                y_evac(s - 1, (s - 1) % 2)
                hT_evac(s)
                split_next(slots[s], range(GU_PARTS))
            with act.Fori(1, SLOTS // 2 - 1) as j:
                for b in range(2):
                    s = 2 * j + 1 + b
                    slots = [next_expert(s - 1), next_expert(s)]
                    silu(s, 1 - b)
                    x_evac(s + 1)
                    split_next(slots[0], range(GU_PARTS, E_PARTS))
                    y_evac(s - 1, b, j)
                    hT_evac(s)
                    split_next(slots[1], range(GU_PARTS))
            s = SLOTS - 1
            silu(s, 1)
            split_next(next_expert(s - 1), range(GU_PARTS, E_PARTS))
            y_evac(s - 1, 0, SLOTS // 2 - 1)
            hT_evac(s)
            y_evac(s, 1, SLOTS // 2 - 1)

            def diag(t, b):
                for k in range(2):
                    act.activation(dg[b][:, k, :], ident[:], ACT.Copy, scale=wgt[:, k, ds(t, 1)]).then_inc(S["diag_ok"], 1)

            def fin(t, b, n=P):
                act.wait_ge(S["fvar_ready"], 2 * t + 1)
                act.activation(sd[b][0:n, :], mv[b][0:n, 1:2], ACT.Sqrt).then_inc(S["fsd_ready"], 1)
                act.wait_ge(S["fvar_ready"], 2 * t + 2)
                act.activation(z2[b][0:n, :], z2[b][0:n, :], ACT.Identity, bias=rs[b][0:n, 1:2],
                               scale=rs[b][0:n, 0:1]).then_inc(S["fnorm"], 1)

            act.wait_ge(S["wgt_ok"], 1)
            diag(0, 0)
            diag(1, 1)
            with act.Fori(0, NT // 2 - 1) as j:
                for b in range(2):
                    fin(2 * j + b, b)
                    diag(2 * j + b + 2, b)
            fin(NT - 3, 0)
            diag(NT - 1, 0)
            fin(NT - 2, 1)
            fin(NT - 1, 0, NS)

        @block.vector
        def _(dve):
            o = Order(dve, S["dve_order"])
            dve.wait_ge(S["vec_mm"], 1)
            dve.tensor_copy(vecT[:], bank[7][:, 0:NG * NV].rearrange("p (g v) -> p g v", v=NV)).then_inc(S["vec_ok"], 1)
            dve.wait_ge(S["vec_ok"], 1)
            lam = vecT[:, :, V_LAM]
            o.did(dve.tensor_scalar(half_b[:, :, 0], vecT[:, :, V_BA], 0.5, None, ALU.mult))
            o.did(dve.tensor_scalar(half_b[:, :, 1], vecT[:, :, V_BX], 0.5, None, ALU.mult))
            dve.wait_ge(S["act_order"], 2)
            o.step(dve.tensor_scalar(sp_t[:, 2, :], sp_t[:, 1, :], 2.0, None, ALU.add))
            o.step(dve.reciprocal(sp_t[:, 2, :], sp_t[:, 2, :]))
            o.step(dve.tensor_tensor(sp_t[:, 1, :], sp_t[:, 1, :], sp_t[:, 2, :], ALU.mult))
            o.step(dve.tensor_tensor(sp_t[:, 2, :], sp_t[:, 1, :], sp_t[:, 1, :], ALU.mult))
            o.step(dve.tensor_scalar(sp_t[:, 3, :], sp_t[:, 2, :], 1.0 / 17, 1.0 / 15, ALU.mult, ALU.add))
            for odd in (13, 11, 9, 7, 5, 3, 1):
                o.step(dve.tensor_tensor(sp_t[:, 3, :], sp_t[:, 3, :], sp_t[:, 2, :], ALU.mult))
                o.step(dve.tensor_scalar(sp_t[:, 3, :], sp_t[:, 3, :], 1.0 / odd, None, ALU.add))
            o.step(dve.tensor_tensor(sp_t[:, 3, :], sp_t[:, 3, :], sp_t[:, 1, :], ALU.mult))
            o.step(dve.tensor_scalar(sp_t[:, 4, :], lam, -1.0, 0.0, ALU.mult, ALU.max))
            o.step(dve.scalar_tensor_tensor(sp_t[:, 4, :], sp_t[:, 3, :], 2.0, sp_t[:, 4, :], ALU.mult, ALU.add))
            dve.tensor_scalar(sp2[:], sp_t[:, 4, :], LRU_C / 4, None, ALU.mult).then_inc(S["vec_ok"], 1)
            for g, w in enumerate(WINDOWS):
                for t in range(PB):
                    o.did(dve.memset(inv_cnt[:, g, t:t + 1], 1.0 / min(w, t + 1)))
            dve.wait_ge(S["cT_mm"], 1)
            dve.tensor_copy(cT[:], bank[6][:, 0:KD * NM].rearrange("p (k r) -> p k r", r=NM)).then_inc(S["cT_ok"], 1)
            dve.wait_ge(S["ba_in"], 16)
            with dve.Fori(0, 4) as j:
                for n in range(3):
                    dve.wait_ge(S["ada_mm"], 3 * j + n + 1)
                    cols = mod[0:NM, ds(1536 * j + 512 * n, 512)]
                    dve.tensor_tensor(cols, bank[n][0:NM, :], cols, ALU.add).then_inc(S["ada_ok"], 1)
            dve.wait_ge(S["ada_ok"], 12)
            o.step(dve.tensor_scalar(mod[0:NM, SC1:SH2], mod[0:NM, SC1:SH2], 1.0, None, ALU.add))
            dve.tensor_scalar(mod[0:NM, SC2:6 * D], mod[0:NM, SC2:6 * D], 1.0, None, ALU.add).then_inc(S["mod_ok"], 1)
            dve.wait_ge(S["modT_mm"], 1)
            dve.tensor_copy(modT[:], bank[6][:, 0:2 * KD * NM].rearrange("p (k r) -> p k r", r=NM)).then_inc(S["modT_ok"], 1)
            dve.wait_ge(S["st_mm"], 1)
            for g in range(NG):
                o.did(dve.tensor_copy(p_s[:, g, :, 0:PB], bank[4][:, g * 120:(g + 1) * 120].rearrange("p (s t) -> p s t", s=DEC_B)))
                o.did(dve.tensor_copy(xr_s[:, g, :, 0:CB], bank[5][:, g * 24:(g + 1) * 24].rearrange("p (s t) -> p s t", s=DEC_B)))
            o.did(dve.tensor_copy(h0_s[:], bank[5][:, 128:128 + NG * DEC_B].rearrange("p (g s) -> p g s", s=DEC_B)))
            o.did(dve.memset(h_last[:], 0.0))
            dve.wait_ge(S["xsT_mm"], 1)
            u_s = uTs[:, :, 0:NS].rearrange("p k (s t) -> p k s t", s=DEC_B)
            over_t = lambda v: v.unsqueeze(3).to_broadcast([P, KD, DEC_B, DEC_T])
            dve.wait_ge(S["modT_ok"], 1)
            o.did(dve.tensor_copy(uTs[:, :, NS:NS + 1], modT[:, 0:KD, 0:1]))
            o.step(dve.tensor_tensor(u_s, bank[7][:, :].rearrange("p (k s t) -> p k s t", k=KD, s=DEC_B),
                                     over_t(modT[:, KD:2 * KD, 1:NM]), ALU.mult))
            dve.tensor_tensor(u_s, u_s, over_t(modT[:, 0:KD, 1:NM]), ALU.add).then_inc(S["uTs_ready"], 1)
            dve.wait_ge(S["ada_mm"], 12)
            for k in range(KD // 2, KD):
                dve.wait_ge(S["win_hi"], k + 1)
                if k == 6:
                    dve.wait_ge(S["mod_stored"], 16)
                dve.tensor_tensor(w_in_lo[:, k, :], w_in[:, k, :], w_in_hi[:, k, :].bitcast(F32),
                                  ALU.subtract).then_inc(S["win_lo_dve"], 1)
            dve.wait_ge(S["win_lo_pool"], KD // 2)
            dve.wait_ge(S["win_lo_dve"], KD // 2)
            dve.wait_ge(S["proj_ready"], 3 * NG)
            o.did(dve.memset(p_buf[:, :, 0:PB], 0.0))
            o.did(dve.memset(xr_buf[:, :, 0:CB], 0.0))
            o.wait()

            def u_low(i):
                for k in range(KD):
                    dve.wait_ge(S["uT_hi_ok"], KD * (i - 1) + k + 1)
                    dve.scalar_tensor_tensor(uT_lo[:, k, :], bank[turn_bank(k)][:, 0:C], modT[:, KD + k, 0:1],
                                             uT_hi[:, k, :].bitcast(F32), ALU.mult, ALU.subtract).then_inc(S["uT_lo_ok"], 1)

            def conv(i, j, out, inp):
                taps = [inp(k) for k in range(4)]
                o.step(dve.tensor_scalar(out, taps[0], vecT[:, j, V_WCONV:V_WCONV + 1], vecT[:, j, V_BCONV:V_BCONV + 1],
                                         ALU.mult, ALU.add))
                for k in range(1, 4):
                    last = dve.scalar_tensor_tensor(out, taps[k], vecT[:, j, V_WCONV + k:V_WCONV + k + 1], out, ALU.mult, ALU.add)
                    if k < 3:
                        o.step(last)
                last.then_inc(S["xc_ready"], 1)

            def guard(i, n):
                for j in range(NG):
                    dve.wait_ge(S["T_ready"], NG * i + j + 1)
                    dve.tensor_scalar(tT[:, j, 0:n], tT[:, j, 0:n], 0.0, None, ALU.max).then_inc(S["T_guard"], 1)

            def lru_coefficients(i, j, n, a_out, b_out):
                dve.wait_ge(S["S_ready"], NG * i + j + 1)
                o.step(dve.tensor_scalar(q_t[:, 0:n], tT[:, j, 0:n], 1.0, None, ALU.add))
                o.step(dve.reciprocal(q_t[:, 0:n], q_t[:, 0:n]))
                dve.wait_ge(S["gated_x"], NG * i + j + 1)
                o.did(dve.tensor_scalar(a_out, q_t[:, 0:n], 2.0, -1.0, ALU.mult, ALU.add))
                o.step(dve.tensor_tensor(q_t[:, 0:n], q_t[:, 0:n], tS[:, j, 0:n], ALU.mult))
                o.step(dve.tensor_tensor(b_out, tI[:, j, 0:n], q_t[:, 0:n], ALU.mult))

            def chunk(i, last=False):
                for j in range(NG):
                    dve.wait_ge(S["proj_evac"], 12 * i + j + 1)
                    conv(i, j, xc[:, j, :], lambda k: xr_buf[:, j, k:k + C])
                    dve.wait_ge(S["xc_ready"], NG * i + j + 1)
                    dve.tensor_copy(xr_buf[:, j, 0:CB], xr_buf[:, j, C:C + CB]).then_inc(S["xr_free"], 1)
                for g, w in enumerate(WINDOWS):
                    dve.wait_ge(S["proj_evac"], 12 * i + NG + g + 1)
                    src, span, nb = p_buf[:, g, :], 1, 0
                    while span < w:
                        dst = wsum[nb]
                        lo = PB - w + 2 * span
                        o.step(dve.tensor_tensor(dst[:, lo:PB + C], src[:, lo:PB + C], src[:, lo - span:PB + C - span], ALU.add))
                        src, span, nb = dst, 2 * span, 1 - nb
                    dve.wait_ge(S["pool_mm"], NG * i + g - 1)
                    dd = dif[:, g % 2, :]
                    o.did(dve.scalar_tensor_tensor(dd[:, PB:C], src[:, 2 * PB:PB + C], 1.0 / w, p_buf[:, g, 2 * PB:PB + C],
                                                   ALU.mult, ALU.subtract))
                    o.step(dve.tensor_tensor(fix[:, 0:PB], src[:, PB:2 * PB], inv_cnt[:, g, 0:PB], ALU.mult))
                    dve.tensor_tensor(dd[:, 0:PB], fix[:, 0:PB], p_buf[:, g, PB:2 * PB], ALU.subtract).then_inc(S["d_ready"], 1)
                    dve.wait_ge(S["d_ready"], NG * i + g + 1)
                    o.did(dve.memset(inv_cnt[:, g, 0:PB], 1.0 / w))
                    dve.tensor_copy(p_buf[:, g, 0:PB], p_buf[:, g, C:C + PB]).then_inc(S["p_free"], 1)
                guard(i, C)
                if not last:
                    u_low(i + 1)
                else:
                    for k in range(KD // 2, KD):
                        dve.wait_ge(S["wout_hi"], k + 1)
                        dve.tensor_tensor(w_out_lo[:, k, :], w_out[k], w_out_hi[:, k, :].bitcast(F32),
                                          ALU.subtract).then_inc(S["wout_lo_dve"], 1)
                for j in range(NG):
                    lru_coefficients(i, j, C, a_t, b_t)
                    o.step(dve.tensor_tensor_scan(tI[:, j, :], a_t, b_t, h_last[:, j:j + 1], ALU.mult, ALU.add))
                    dve.tensor_copy(h_last[:, j:j + 1], tI[:, j, C - 1:C]).then_inc(S["h_ready"], 1)
                dve.wait_ge(S["h_ready"], NG * i + NG)

            i = 0
            bs = lambda v: v.rearrange("p (s t) -> p s t", s=DEC_B)
            for j in range(NG):
                dve.wait_ge(S["proj_evac"], 12 * i + j + 1)
                conv(i, j, bs(xc[:, j, 0:NS]), lambda k: xr_s[:, j, :, k:k + DEC_T])
            for g, w in enumerate(WINDOWS):
                dve.wait_ge(S["proj_evac"], 12 * i + NG + g + 1)
                wv = [v[:, 0:DEC_B * (PB + DEC_T)].rearrange("p (s t) -> p s t", s=DEC_B) for v in wsum]
                src, span, end, nb = p_s[:, g], 1, PB + DEC_T, 0
                while span < w:
                    lo = PB - w + 2 * span
                    o.step(dve.tensor_tensor(wv[nb][:, :, lo:end], src[:, :, lo:end], src[:, :, lo - span:end - span], ALU.add))
                    src, span, nb = wv[nb], 2 * span, 1 - nb
                if g >= 2:
                    dve.wait_ge(S["pool_mm"], g - 1)
                dve.scalar_tensor_tensor(bs(dif[:, g % 2, 0:NS]), src[:, :, PB:end], 1.0 / w, p_s[:, g, :, PB:end],
                                         ALU.mult, ALU.subtract).then_inc(S["d_ready"], 1)
                dve.wait_ge(S["d_ready"], NG * i + g + 1)
            for g in range(NG):
                dve.tensor_copy(bs(prj_s[:, g, :]), p_s[:, g, :, PB:PB + DEC_T]).then_inc(S["p_free"], 1)
                dve.tensor_copy(bs(prj_s[:, NG + g, :]), xr_s[:, g, :, CB:CB + DEC_T]).then_inc(S["xr_free"], 1)
            guard(i, NS)
            u_low(1)
            av, bv, hv = (v[:, 0:NG * NS].rearrange("p (g s t) -> p g s t", g=NG, s=DEC_B) for v in (a_t, b_t, h_t))
            for j in range(NG):
                lru_coefficients(i, j, NS, a_t[:, j * NS:(j + 1) * NS], b_t[:, j * NS:(j + 1) * NS])
            for t in range(DEC_T):
                before = h0_s[:] if t == 0 else hv[:, :, :, t - 1]
                o.step(dve.tensor_tensor(hv[:, :, :, t], av[:, :, :, t], before, ALU.mult))
                o.step(dve.tensor_tensor(hv[:, :, :, t], hv[:, :, :, t], bv[:, :, :, t], ALU.add))
            dve.tensor_copy(h0_s[:], hv[:, :, :, DEC_T - 1]).then_inc(S["prj_copied"], 1)
            dve.memset(spare[0:1, 0:1], 0.0).then_inc(S["h_ready"], NG)

            with dve.Fori(1, NCH) as i:
                o.enter(i, 1, CHUNK_STEPS)
                chunk(i)
            o.leave(NCH - 1)
            chunk(NCH, last=True)

            dve.wait_ge(S["gate_in"], 16)

            def ln_in(t, b, n, rows, uses, first):
                dve.wait_ge(S["mix_ready"], t + 1)
                for h in range(2):
                    o.did(dve.tensor_tensor(z[b][0:n, 512 * h:512 * h + 512], bank[2 * b + h][0:n, :],
                                            rows[0][0:n, 512 * h:512 * h + 512], ALU.mult))
                o.wait()
                dve.wait_ge(S[f"xres{b}"], 16 * uses)
                dve.scalar_tensor_tensor(z[b][0:n, :], xres[b][0:n, :], ALPHA, z[b][0:n, :], ALU.mult, ALU.add).then_inc(S["mix_used"], 1)
                dve.wait_ge(S["mix_used"], t + 1)
                stats(b, n, z[b], S["var_ready"], S["sd_ready"], t)

            def stats(b, n, zz, ready, sd_ready, t):
                for h in range(2):
                    o.did(dve.bn_stats(st6[b][0:n, h, :], zz[0:n, 512 * h:512 * h + 512]))
                o.wait()
                dve.memset(spare[0:1, 0:1], 0.0)
                o.step(dve.bn_aggr(mv[b][0:n, :], st6[b][0:n, :, :].rearrange("p a b -> p (a b)")))
                dve.tensor_scalar(mv[b][0:n, 1:2], mv[b][0:n, 1:2], LN_EPS, None, ALU.add).then_inc(ready, 1)
                dve.wait_ge(sd_ready, t + 1)
                o.step(dve.reciprocal(rs[b][0:n, 0:1], sd[b][0:n, :]))
                dve.scalar_tensor_tensor(rs[b][0:n, 1:2], mv[b][0:n, 0:1], -1.0, rs[b][0:n, 0:1], ALU.mult, ALU.mult).then_inc(ready, 1)

            def ln_out(t, b, n, rows, uses, first):
                dve.wait_ge(S["x1_ready"], t + 1)
                if not first:
                    dve.wait_ge(S[f"u2_st{b}"], 16 * (uses - 1))
                    dve.wait_ge(S["u2T_mm"], 2 * t - 2)
                o.step(dve.tensor_tensor(u2[b][0:n, :], x1[b][0:n, :], rows[1][0:n, :], ALU.mult))
                dve.tensor_tensor(u2[b][0:n, :], u2[b][0:n, :], rows[2][0:n, :], ALU.add).then_inc(S["u2_ready"], 1)

            def router_out(t, n=P):
                dve.wait_ge(S["rt_mm"], t + 1)
                dve.tensor_tensor(logits[0:n, ds(t, 1), :].rearrange("p a r -> p (a r)"), bank[6][0:n, 0:NR], b_rt[0:n, :],
                                  ALU.add).then_inc(S["rt_ok"], 1)

            o.did(dve.memset(logits[:], 0.0))
            prompt_rows = (row_tiles[:, 0, :], row_tiles[:, 3, :], row_tiles[:, 4, :])
            sample_rows = (row_tiles_s[:, 0, :], row_tiles_s[:, 1, :], row_tiles_s[:, 2, :])
            ln_in(0, 0, P, prompt_rows, 1, True)
            ln_in(1, 1, P, prompt_rows, 1, True)
            dve.wait_ge(S["tiles_in"], 64)
            ln_out(0, 0, P, prompt_rows, 1, True)
            ln_in(2, 0, P, prompt_rows, 2, False)
            ln_out(1, 1, P, prompt_rows, 1, True)
            dve.wait_ge(S["rt_in"], 64)
            router_out(0)
            ln_in(3, 1, P, prompt_rows, 2, False)
            ln_out(2, 0, P, prompt_rows, 2, False)
            router_out(1)
            with dve.Fori(2, NT // 2) as j:
                o.enter(j, 2, LN_STEPS)
                for b in range(2):
                    ln_in(2 * j + b, b, P, prompt_rows, j + 1, False)
                    ln_out(2 * j + b - 1, 1 - b, P, prompt_rows, j + b, False)
                    router_out(2 * j + b - 2)
            o.leave(NT // 2 - 2)
            dve.wait_ge(S["tiles_s_in"], 16 * 3 * DEC_B)
            ln_in(NT - 1, 0, NS, sample_rows, NT // 2 + 1, False)
            ln_out(NT - 2, 1, P, prompt_rows, NT // 2, False)
            router_out(NT - 3)
            ln_out(NT - 1, 0, NS, sample_rows, NT // 2 + 1, False)
            router_out(NT - 2)
            router_out(NT - 1, NS)
            dve.wait_ge(S["rt_ok"], NT)

            bc = lambda v, n: v.unsqueeze(2).to_broadcast([P, v.shape[1], n])
            gl, el = logits[:, :, 0:NGR], logits[:, :, NGR:NR]
            hot_g, hot_1, hot_2, esel, f4 = rt_f[0], rt_f[1], rt_f[2], rt_f[3], rt_f[4]
            gm, m1, m2, mx = r17[0], r17[1], r17[2], r17[3]

            def first_max(v, top, hot):
                o.step(dve.tensor_reduce(top, v, axis=AX, op=ALU.max))
                o.step(dve.tensor_tensor(f4, v, bc(top, EPG), ALU.is_equal))
                o.step(dve.tensor_tensor(f4, f4, prio[:].unsqueeze(1).to_broadcast([P, NT, EPG]), ALU.mult))
                o.step(dve.tensor_reduce(mx, f4, axis=AX, op=ALU.max))
                o.step(dve.tensor_tensor(hot, f4, bc(mx, EPG), ALU.is_equal))

            dve.wait_ge(S["consts"], 4)
            first_max(gl, gm, hot_g)
            prod, e1, e2, both, rank, base = rt[0], rt[1], rt[2], rt[3], rt[4], rt[5]
            g4 = lambda v: v.rearrange("p t (g e) -> p t g e", g=NGR)
            over_e = hot_g.unsqueeze(3).to_broadcast([P, NT, NGR, EPG])
            o.step(dve.tensor_tensor(g4(prod), g4(el), over_e, ALU.mult))
            o.step(dve.tensor_reduce(esel, prod.rearrange("p t (g e) -> p t e g", g=NGR), axis=AX, op=ALU.add))
            first_max(esel, m1, hot_1)
            o.step(dve.scalar_tensor_tensor(esel, hot_1, -BIG, esel, ALU.mult, ALU.add))
            first_max(esel, m2, hot_2)
            o.step(dve.tensor_tensor(hot_g, hot_g, bc(valid[:], NGR), ALU.mult))
            for e_hot, hot in ((e1, hot_1), (e2, hot_2)):
                o.step(dve.tensor_tensor(g4(e_hot), over_e, hot.unsqueeze(2).to_broadcast([P, NT, NGR, EPG]), ALU.mult))
            dve.tensor_tensor(both, e1, e2, ALU.add).then_inc(S["m_ready"], 1)
            o.did(dve.tensor_tensor(rt_f[8], gl, bc(gm, NGR), ALU.subtract))
            dve.tensor_tensor(r17[4], m2, m1, ALU.subtract).then_inc(S["w_exp"], 1)
            dve.wait_ge(S["cnt_mm"], 2)
            tot = bank[1][:, 0:NT * NE].rearrange("p (t e) -> p t e", e=NE)
            o.step(dve.memset(base[:, 0, :], 0.0))
            n_e, slots_n, start_e, end_e = e16[0], e16[1], e16[2], e16[3]
            for t in range(NT):
                dst = base[:, t + 1, :] if t + 1 < NT else n_e
                o.step(dve.tensor_tensor(dst, base[:, t, :], tot[:, t, :], ALU.add))
            o.step(dve.tensor_tensor(rank, bank[0][:, 0:NT * NE].rearrange("p (t e) -> p t e", e=NE), base, ALU.add))
            o.step(dve.tensor_tensor(big_t, bc(n_e, NT), iota17[:].unsqueeze(1).to_broadcast([P, NE, NT]), ALU.is_gt))
            o.step(dve.tensor_reduce(slots_n, big_t, axis=AX, op=ALU.add))
            o.step(dve.tensor_scalar(slots_n, slots_n, 1.0, None, ALU.max))
            o.step(dve.tensor_tensor(lt_prod, lt16[:], slots_n.unsqueeze(1).to_broadcast([P, NE, NE]), ALU.mult))
            o.step(dve.tensor_reduce(start_e, lt_prod, axis=AX, op=ALU.add))
            o.step(dve.tensor_tensor(end_e, start_e, slots_n, ALU.add))
            o.step(dve.tensor_tensor(slot_ge, bc(iota_s[:], NE), end_e.unsqueeze(1).to_broadcast([P, SLOTS, NE]), ALU.is_ge))
            o.step(dve.tensor_reduce(slot_e[:], slot_ge, axis=AX, op=ALU.add))
            o.step(dve.tensor_scalar(slot_ei[:, 0, :], slot_e[:], float(NE - 1), None, ALU.min))
            nxt = e48[0]
            o.did(dve.memset(nxt[:, 0:1], 1.0))
            o.step(dve.tensor_tensor(nxt[:, 1:SLOTS], slot_e[:, 1:SLOTS], slot_e[:, 0:SLOTS - 1], ALU.is_gt))
            o.did(dve.tensor_scalar(e48[1], slot_e[:], float(NE - 1), None, ALU.is_lt))
            o.step(dve.scalar_tensor_tensor(nxt, slot_e[:], 1.0, nxt, ALU.add, ALU.mult))
            o.step(dve.tensor_tensor(slot_ei[:, 1, :], nxt, e48[1], ALU.mult))
            o.step(dve.tensor_scalar(e16[4], start_e, float(P), None, ALU.mult))
            o.step(dve.tensor_tensor(rank, rank, e16[4].unsqueeze(1).to_broadcast([P, NT, NE]), ALU.add))
            o.step(dve.tensor_scalar(r17[5], valid[:], -8192.0, 8192.0, ALU.mult, ALU.add))
            for k, e_hot in enumerate((e1, e2)):
                o.step(dve.tensor_tensor(prod, e_hot, rank, ALU.mult))
                o.step(dve.tensor_reduce(r17[6], prod, axis=AX, op=ALU.add))
                o.step(dve.tensor_tensor(pos_a[:, k, :], r17[6], r17[5], ALU.add))
            o.step(dve.tensor_scalar(pos_b[:], pos_a[:], 7, None, ALU.arith_shift_right))
            o.did(dve.tensor_scalar(pos_a[:], pos_a[:], P - 1, None, ALU.bitwise_and))
            o.step(dve.tensor_copy(pos_f[:, 2:4, :], pos_b[:]))
            o.step(dve.tensor_copy(pos_f[:, 0:2, :], pos_a[:]))
            o.did(dve.scalar_tensor_tensor(pos_i[:], pos_f[:, 0:2, :], float(SLOTS), pos_f[:, 2:4, :], ALU.mult, ALU.add))
            o.step(dve.tensor_scalar(r17[7], iota17[:], 1.0 / P, None, ALU.mult))
            for b, n in ((0, NT // 2 + 1), (1, NT // 2)):
                dve.wait_ge(S[f"x1_st{b}"], 16 * n)
                dve.wait_ge(S[f"u2_st{b}"], 16 * n)
            over_k = lambda v, n: v.unsqueeze(1).unsqueeze(1).to_broadcast([P, 2, NT, n])
            by_tok = lambda v, n: v.unsqueeze(3).to_broadcast([P, 2, NT, n])
            o.step(dve.tensor_tensor(hot_b[:, :, :, 0, :], over_k(iota_s[:], SLOTS), by_tok(pos_f[:, 2:4, :], SLOTS), ALU.is_equal))
            o.did(dve.tensor_scalar(hot_b[:, :, :, 1, :], hot_b[:, :, :, 0, :], part_i[:, 0:1], None, ALU.mult))
            tile_no = r17[7].unsqueeze(1).unsqueeze(3).to_broadcast([P, 2, NT, SLOTS])
            o.wait()
            o.did(dve.tensor_tensor(hot_b[:, :, :, 0, :], hot_b[:, :, :, 0, :], tile_no, ALU.mult))
            dve.tensor_tensor(hot_a, over_k(iota_r[:], P), by_tok(pos_f[:, 0:2, :], P), ALU.is_equal).then_inc(S["hot_ready"], 1)
            dve.wait_ge(S["idx_mm"], 1)
            o.step(dve.tensor_copy(slot_ge[:, 0:6, :].rearrange("p a b -> p (a b)"), bank[2][:, 0:2 * SLOTS]))
            lo_hi = slot_ge[:, 0:6, :].rearrange("p a b -> p (a b)")
            dve.scalar_tensor_tensor(tok_i[:], lo_hi[:, 0:SLOTS], float(P), lo_hi[:, SLOTS:2 * SLOTS], ALU.mult, ALU.add).then_inc(S["idx_ready"], 1)
            dve.wait_ge(S["w_expd"], 2)
            o.step(dve.tensor_reduce(r17[8], rt_f[8], axis=AX, op=ALU.add))
            o.did(dve.tensor_scalar(r17[9], r17[4], 1.0, None, ALU.add))
            o.wait()
            o.step(dve.tensor_tensor(r17[8], r17[8], r17[9], ALU.mult))
            o.step(dve.reciprocal(wgt[:, 0, :], r17[8]))
            dve.tensor_tensor(wgt[:, 1, :], wgt[:, 0, :], r17[4], ALU.mult).then_inc(S["wgt_ok"], 1)

            def next_expert(s):
                return dve.value_load(slot_ei[0:1, 1, ds(s, 1)], min_val=0, max_val=NE - 1)

            def split_next(e, parts):
                with dve.If(e > 0):
                    for n in parts:
                        dve.wait_ge(S["w_hi"], e * E_PARTS + n + 1)
                        dve.tensor_tensor(part(w_lo, e & 1, n), raw_part(e & 1, n), part(w_hi, e & 1, n).bitcast(F32),
                                          ALU.subtract).then_inc(S["w_lo"], 1)

            def x_evac(s):
                for h in range(2):
                    k = slice(4 * h, 4 * h + 4)
                    dve.wait_ge(S["xT_hi_ok"], 2 * s + h + 1)
                    dve.tensor_tensor(xT_lo[:, k, :], bank[h][:, :].rearrange("p (k n) -> p k n", n=P),
                                      xT_hi[:, k, :].bitcast(F32), ALU.subtract).then_inc(S["xT_lo_ok"], 1)

            def hidden(s, b):
                dve.wait_ge(S["sil_ok"], s + 1)
                dve.tensor_tensor(hid, sil, bank[2 + b][:, F:2 * F], ALU.mult).then_inc(S["hid_ok"], 1)

            def hT_evac(s):
                dve.wait_ge(S["hT_hi_ok"], s + 1)
                dve.tensor_tensor(hT_lo[:, :, :], bank[4][:, 0:F].rearrange("p (k n) -> p k n", n=P),
                                  hT_hi[:, :, :].bitcast(F32), ALU.subtract).then_inc(S["hT_lo_ok"], 1)

            def y_evac(s, b, before=None):
                dve.wait_ge(S["dn_mm"], s + 1)
                if before is not None:
                    dve.wait_ge(S[f"ys{b}"], 16 * before)
                dve.tensor_copy(y_sb[b][:, 512:1024], bank[6][:, :]).then_inc(S["y_dve"], 1)

            dve.wait_ge(S["w0_lo"], E_PARTS)
            dve.memset(spare[0:1, 0:1], 0.0).then_inc(S["w_lo"], E_PARTS)
            slots = [next_expert(s) for s in range(3)]
            x_evac(0)
            hidden(0, 0)
            x_evac(1)
            hT_evac(0)
            split_next(slots[0], range(GU_PARTS))
            for s in (1, 2):
                hidden(s, s % 2)
                x_evac(s + 1)
                split_next(slots[s - 1], range(GU_PARTS, E_PARTS))
                y_evac(s - 1, (s - 1) % 2)
                hT_evac(s)
                split_next(slots[s], range(GU_PARTS))
            with dve.Fori(1, SLOTS // 2 - 1) as j:
                for b in range(2):
                    s = 2 * j + 1 + b
                    slots = [next_expert(s - 1), next_expert(s)]
                    hidden(s, 1 - b)
                    x_evac(s + 1)
                    split_next(slots[0], range(GU_PARTS, E_PARTS))
                    y_evac(s - 1, b, j)
                    hT_evac(s)
                    split_next(slots[1], range(GU_PARTS))
            s = SLOTS - 1
            hidden(s, 1)
            split_next(next_expert(s - 1), range(GU_PARTS, E_PARTS))
            y_evac(s - 1, 0, SLOTS // 2 - 1)
            hT_evac(s)
            y_evac(s, 1, SLOTS // 2 - 1)

            dve.wait_ge(S["fin_in"], 48)

            def fin_in(t, b, n, gate2, uses):
                dve.wait_ge(S["comb_mm"], t + 1)
                for h in range(2):
                    o.did(dve.tensor_tensor(z2[b][0:n, 512 * h:512 * h + 512], bank[2 * b + h][0:n, :],
                                            gate2[0:n, 512 * h:512 * h + 512], ALU.mult))
                o.wait()
                dve.wait_ge(S[f"xo{b}"], 16 * uses)
                dve.scalar_tensor_tensor(z2[b][0:n, :], xo[b][0:n, :], ALPHA, z2[b][0:n, :], ALU.mult, ALU.add).then_inc(S["comb_used"], 1)
                dve.wait_ge(S["comb_used"], t + 1)
                stats(b, n, z2[b], S["fvar_ready"], S["fsd_ready"], t)

            def fin_out(t, b, n, before):
                dve.wait_ge(S["fg_ok"], t + 1)
                if before is not None:
                    dve.wait_ge(S[f"os{b}"], 16 * before)
                dve.tensor_tensor(oo[b][0:n, :], z2[b][0:n, :], fin_tiles[0:n, 2, :], ALU.add).then_inc(S["fo_ok"], 1)
                dve.wait_ge(S["fo_ok"], t + 1)

            g2 = fin_tiles[:, 0, :]
            fin_in(0, 0, P, g2, 1)
            fin_in(1, 1, P, g2, 1)
            fin_out(0, 0, P, None)
            fin_in(2, 0, P, g2, 2)
            fin_out(1, 1, P, None)
            fin_in(3, 1, P, g2, 2)
            fin_out(2, 0, P, 1)
            with dve.Fori(2, NT // 2) as j:
                o.enter(j, 2, FIN_STEPS)
                for b in range(2):
                    fin_in(2 * j + b, b, P, g2, j + 1)
                    fin_out(2 * j + b - 1, 1 - b, P, j + b - 1)
            o.leave(NT // 2 - 2)
            dve.wait_ge(S["fin_s_in"], 16 * DEC_B)
            fin_in(NT - 1, 0, NS, fin_tile_s, NT // 2 + 1)
            fin_out(NT - 2, 1, P, NT // 2 - 1)
            fin_out(NT - 1, 0, NS, NT // 2)

        @block.tensor
        def _(pe):
            def turn(out, in_, rows):
                return pe.transpose(out, in_, ident[0:rows, 0:rows])

            pe.wait_ge(S["consts"], 1)
            pe.wait_ge(S["c_in"], 32)
            for k in range(KD):
                last = turn(bank[6][:, k * NM:(k + 1) * NM], c_rows[0:NM, k * P:(k + 1) * P], NM)
            last.then_inc(S["cT_mm"], 1)
            pe.wait_ge(S["vec_in"], 96)
            for g in range(NG):
                last = turn(bank[7][:, g * NV:(g + 1) * NV], row_v[0:NV, g * P:(g + 1) * P], NV)
            last.then_inc(S["vec_mm"], 1)
            pe.wait_ge(S["cT_ok"], 1)

            def ada(j, first=False):
                for n in range(3):
                    pe.wait_ge(S[f"ada{n}"], 16 * (j + 1))
                    if not first:
                        pe.wait_ge(S["ada_ok"], 3 * j + n - 2)
                    for k in range(KD):
                        last = pe.matmul(bank[n][0:NM, :], cT[:, k, :], w_ada[n][:, k, :], start=k == 0, stop=k == KD - 1)
                    last.then_inc(S["ada_mm"], 1)

            ada(0, first=True)
            with pe.Fori(1, 4) as j:
                ada(j)
            pe.wait_ge(S["mod_ok"], 1)
            for k in range(2 * KD):
                last = turn(bank[6][:, k * NM:(k + 1) * NM], mod[0:NM, k * P:(k + 1) * P], NM)
            last.then_inc(S["modT_mm"], 1)
            pe.wait_ge(S["st_in"], 48)
            for g in range(NG):
                turn(bank[4][:, g * 120:(g + 1) * 120], row_a[0:120, g * P:(g + 1) * P], 120)
                turn(bank[5][:, g * 24:(g + 1) * 24], row_b[0:24, g * P:(g + 1) * P], 24)
                last = turn(bank[5][:, 128 + g * DEC_B:128 + (g + 1) * DEC_B], row_c[0:DEC_B, g * P:(g + 1) * P], DEC_B)
            last.then_inc(S["st_mm"], 1)
            pe.wait_ge(S["xs_loaded"], 16)
            for k in range(KD):
                last = turn(bank[7][:, k * NS:(k + 1) * NS], xs[0:NS, k * P:(k + 1) * P], NS)
            last.then_inc(S["xsT_mm"], 1)
            pe.wait_ge(S["w_in_in"], 16)
            pe.wait_ge(S["gates_in"], 64)
            pe.wait_ge(S["wpool_in"], 16)

            def split_product(out, x_hi, x_lo, w_hi, w_lo, start, stop):
                pe.matmul(out, x_hi, w_hi, start=start, stop=False)
                pe.matmul(out, x_hi, w_lo, start=False, stop=False)
                return pe.matmul(out, x_lo, w_hi, start=False, stop=stop)

            def project(i, m, order, n, wait_k=None):
                cols = slice(m * P, (m + 1) * P)
                for k in range(KD):
                    if wait_k is not None:
                        pe.wait_ge(S["uT_lo_ok"], wait_k + k + 1)
                    last = split_product(bank[2 + order % 2][:, 0:n], w_in_hi[:, k, cols], w_in_lo[:, k, cols],
                                         uT_hi[:, k, 0:n], uT_lo[:, k, 0:n], k == 0, k == KD - 1)
                last.then_inc(S["proj_ready"], 1)

            def gates(i, n, first=False):
                for j in range(NG):
                    pe.wait_ge(S["xc_ready"], NG * i + j + 1)
                    for q, w in ((0, wa), (1, wx)):
                        if not (first and j == 0):
                            pe.wait_ge(S["gates_evac"], 2 * NG * i + 2 * j + q - 1)
                        pe.matmul(bank[4 + q][:, 0:n], w[:, j, :], xc[:, j, 0:n], start=True, stop=True).then_inc(S["gates_mm"], 1)

            def pool_group(i, g, n, first=False):
                pe.wait_ge(S["d_ready"], NG * i + g + 1)
                if not (first and g < 2):
                    pe.wait_ge(S["pool_evac"], NG * i + g - 1)
                pe.matmul(bank[6 + g % 2][:, 0:n], wp[:, g, :], dif[:, g % 2, 0:n], start=True, stop=True).then_inc(S["pool_mm"], 1)

            def column(order):
                return NG + order if order < NG else order - NG if order < 2 * NG else order

            def mixers(i, turn_next):
                for order in range(3 * NG):
                    if order == 2 * NG:
                        gates(i, C)
                    pe.wait_ge(S["proj_evac"], 12 * i + order - 1)
                    project(i, column(order), order, C, KD * (i - 1) if order == 0 else None)
                    if order > 2 * NG:
                        pool_group(i, order - 2 * NG - 1, C)
                pool_group(i, NG - 1, C)
                if turn_next is not None:
                    turn_next()

            def turn_chunk(i, first=False):
                pe.wait_ge(S["x_loaded"], 16 * i)
                for k in range(KD):
                    if not (first and k < 4):
                        pe.wait_ge(S["uT_lo_ok"], KD * (i - 1) + k - 3)
                    if k == 2:
                        pe.wait_ge(S["pool_evac"], NG * i)
                    for t in range(TPC):
                        last = turn(bank[turn_bank(k)][:, t * P:(t + 1) * P], xin[:, t, k * P:(k + 1) * P], P)
                    last.then_inc(S["xT_ready"], 1)

            pe.wait_ge(S["uTs_ready"], 1)
            for n in range(3):
                cols = slice(DH, 2 * DH) if n == 0 else slice(0, DH) if n == 1 else slice(2 * DH, 3 * DH)
                for k in range(KD):
                    last = pe.matmul(bank[2 + n][0:NS + 1, :], uTs[:, k, :], w_in[:, k, cols], start=k == 0, stop=k == KD - 1)
                last.then_inc(S["rows_mm"], 1)
            for n in range(3):
                pe.wait_ge(S["rows_ok"], n + 1)
                for g in range(NG):
                    last = turn(bank[2 + n][:, g * (NS + 1):(g + 1) * (NS + 1)], rows_s[0:NS + 1, n, g * P:(g + 1) * P], NS + 1)
                last.then_inc(S["proj_ready"], NG)
            pe.wait_ge(S["proj_evac"], 3 * NG)
            gates(0, NS, first=True)
            for g in range(NG):
                pool_group(0, g, NS, first=True)
            turn_chunk(1, first=True)
            pe.wait_ge(S["win_lo_pool"], KD // 2)
            pe.wait_ge(S["win_lo_dve"], KD // 2)
            with pe.Fori(1, NCH) as i:
                mixers(i, lambda: turn_chunk(i + 1))

            def state_rows(n, src, rows):
                if n:
                    pe.wait_ge(S["out_evac"], n)
                for g in range(NG):
                    last = pe.transpose(bank[7][0:rows, g * P:(g + 1) * P], src(g), ident[:])
                last.then_inc(S["out_mm"], 1)

            pe.wait_ge(S["prj_copied"], 1)
            pe.wait_ge(S["uT_lo_ok"], KD * NCH)
            state_rows(0, lambda g: prj_s[:, g, :], NS)
            state_rows(1, lambda g: prj_s[:, NG + g, :], NS)
            state_rows(2, lambda g: h0_s[:, g, :], DEC_B)
            pe.wait_ge(S["out_evac"], 3)
            mixers(NCH, None)

            def out_proj(t, b, n=P, first=False, turn_before=None):
                pe.wait_ge(S["yT_lo_ok"], t + 1)
                if not first:
                    pe.wait_ge(S["mix_used"], t - 1)
                for h in range(2):
                    for k in range(KD):
                        if turn_before is not None and h == 1 and k == 3:
                            turn_before()
                        if first:
                            pe.wait_ge(S["wout_lo_pool" if k < KD // 2 else "wout_lo_dve"], k % (KD // 2) + 1)
                        cols = slice(512 * h, 512 * h + 512)
                        last = split_product(bank[2 * b + h][0:n, :], yT_hi[b][:, k, 0:n], yT_lo[b][:, k, 0:n],
                                             w_out_hi[:, k, cols], w_out_lo[:, k, cols], k == 0, k == KD - 1)
                last.then_inc(S["mix_ready"], 1)

            def turn_u2(t, b, n=P, first=False):
                pe.wait_ge(S["u2_ready"], t + 1)
                for h in range(2):
                    if not first:
                        pe.wait_ge(S["u2T_ok"], 2 * t + h - 1)
                    for k in range(4):
                        last = turn(bank[4 + h][:, k * P:k * P + n], u2[b][0:n, (4 * h + k) * P:(4 * h + k + 1) * P], n)
                    last.then_inc(S["u2T_mm"], 1)

            def router(t, n=P, first=False):
                pe.wait_ge(S["u2T_ok"], 2 * t + 2)
                if not first:
                    pe.wait_ge(S["rt_ok"], t)
                for k in range(KD):
                    last = pe.matmul(bank[6][0:n, 0:NR], u2T[:, k, 0:n], w_rt[:, k, :], start=k == 0, stop=k == KD - 1)
                last.then_inc(S["rt_mm"], 1)

            out_proj(0, 0, first=True)
            out_proj(1, 1, first=True)
            pe.wait_ge(S["ylru_ready"], NG * NCH + NG)
            pe.wait_ge(S["pool_evac"], NG * NCH + NG)
            state_rows(3, lambda g: p_buf[:, g, 0:PB], PB)
            state_rows(4, lambda g: xr_buf[:, g, 0:CB], CB)
            pe.wait_ge(S["out_evac"], 5)
            pe.transpose(bank[7][0:NG, 0:P], h_last[:], ident[:]).then_inc(S["out_mm"], 1)
            pe.wait_ge(S["rt_in"], 64)
            out_proj(2, 0, turn_before=lambda: turn_u2(0, 0, first=True))
            router(0, first=True)
            out_proj(3, 1, turn_before=lambda: turn_u2(1, 1))
            router(1)
            with pe.Fori(2, NT // 2) as j:
                for b in range(2):
                    out_proj(2 * j + b, b, turn_before=lambda: turn_u2(2 * j + b - 2, b))
                    router(2 * j + b - 2)
            out_proj(NT - 1, 0, NS, turn_before=lambda: turn_u2(NT - 3, 0))
            router(NT - 3)
            turn_u2(NT - 2, 1)
            router(NT - 2)
            turn_u2(NT - 1, 0, NS)
            router(NT - 1, NS)
            pe.wait_ge(S["m_ready"], 1)
            m_all = rt[3].rearrange("p t e -> p (t e)")
            pe.matmul(bank[0][:, 0:NT * NE], tri[:], m_all, start=True, stop=True).then_inc(S["cnt_mm"], 1)
            pe.matmul(bank[1][:, 0:NT * NE], ones[:], m_all, start=True, stop=True).then_inc(S["cnt_mm"], 1)

            pe.wait_ge(S["hot_ready"], 1)
            for k in range(2):
                for t in range(NT):
                    last = pe.matmul(bank[2][:, 0:2 * SLOTS], hot_a[:, k, t, :], hot_b[:, k, t, :, :].rearrange("p v s -> p (v s)"),
                                     start=k == 0 and t == 0, stop=k == 1 and t == NT - 1)
            last.then_inc(S["idx_mm"], 1)

            pe.wait_ge(S["idx_ready"], 1)

            def turn_x(s, b, uses, first=False):
                pe.wait_ge(S[f"xg{b}"], 16 * uses)
                for h in range(2):
                    if not first:
                        pe.wait_ge(S["xT_lo_ok"], 2 * s + h - 1)
                    for k in range(4):
                        last = turn(bank[h][:, k * P:(k + 1) * P], xg[b][:, (4 * h + k) * P:(4 * h + k + 1) * P], P)
                    last.then_inc(S["xgT_mm"], 1)

            def product(out, x_hi, x_lo, buf, off, start, stop):
                hi, lo = (w[:, ds(buf, 1), off:off + 512].rearrange("p a n -> p (a n)") for w in (w_hi, w_lo))
                return split_product(out, x_hi, x_lo, hi, lo, start, stop)

            def gate_up(s, b):
                e = pe.value_load(slot_ei[0:1, 0, ds(s, 1)], min_val=0, max_val=NE - 1)
                pe.wait_ge(S["xT_lo_ok"], 2 * s + 2)
                pe.wait_ge(S["w_lo"], e * E_PARTS + GU_PARTS)
                for k in range(KD):
                    last = product(bank[2 + b][:, :], xT_hi[:, k, :], xT_lo[:, k, :], e & 1, k * 2 * F, k == 0, k == KD - 1)
                last.then_inc(S["gu_mm"], 1)

            def turn_h(s):
                pe.wait_ge(S["hid_ok"], s + 1)
                for k in range(F // P):
                    last = turn(bank[4][:, k * P:(k + 1) * P], hid[:, k * P:(k + 1) * P], P)
                last.then_inc(S["hT_mm"], 1)

            def down(s, first=False):
                e = pe.value_load(slot_ei[0:1, 0, ds(s, 1)], min_val=0, max_val=NE - 1)
                pe.wait_ge(S["hT_lo_ok"], s + 1)
                pe.wait_ge(S["w_lo"], e * E_PARTS + E_PARTS)
                if not first:
                    pe.wait_ge(S["y_act"], s)
                    pe.wait_ge(S["y_dve"], s)
                for h in range(2):
                    for k in range(F // P):
                        last = product(bank[5 + h][:, :], hT_hi[:, k, :], hT_lo[:, k, :], e & 1, GU + k * D + 512 * h,
                                       k == 0, k == F // P - 1)
                last.then_inc(S["dn_mm"], 1)

            turn_x(0, 0, 1, first=True)
            gate_up(0, 0)
            turn_x(1, 1, 1)
            turn_h(0)
            for s in (1, 2):
                gate_up(s, s % 2)
                turn_x(s + 1, (s + 1) % 2, (s + 1) // 2 + 1)
                down(s - 1, first=s == 1)
                turn_h(s)
            with pe.Fori(1, SLOTS // 2 - 1) as j:
                for b in range(2):
                    s = 2 * j + 1 + b
                    gate_up(s, 1 - b)
                    turn_x(s + 1, b, j + 2 if b else j + 2)
                    down(s - 1)
                    turn_h(s)
            s = SLOTS - 1
            gate_up(s, 1)
            down(s - 1)
            turn_h(s)
            down(s)

            def combine(t, b, rows_b, uses, n=P, first=False):
                pe.wait_ge(S["diag_ok"], 2 * t + 2)
                pe.wait_ge(S[f"ya{rows_b}"], 16 * uses)
                pe.wait_ge(S[f"yb{rows_b}"], 16 * uses)
                if not first:
                    pe.wait_ge(S["comb_used"], t - 1)
                for h in range(2):
                    for k, rows in enumerate((ya[rows_b], yb[rows_b])):
                        last = pe.matmul(bank[2 * b + h][0:n, :], dg[b][0:n, k, 0:n], rows[0:n, 512 * h:512 * h + 512],
                                         start=k == 0, stop=k == 1)
                last.then_inc(S["comb_mm"], 1)

            pe.wait_ge(S["y_dve"], SLOTS)
            for t in range(4):
                combine(t, t % 2, t, 1, first=t < 2)
            with pe.Fori(1, NT // 4) as j:
                for b in range(4):
                    combine(4 * j + b, b % 2, b, j + 1)
            combine(NT - 1, 0, 0, NT // 4 + 1, NS)


CHUNK_STEPS = 58
LN_STEPS = 14
FIN_STEPS = 12

_INS = ['x_prompt', 'x_sample', 'c_prompt', 'c_sample', 'state_pool', 'state_conv', 'state_lru', 'w_ada', 'b_ada', 'w_in',
        'w_pool', 'pool_scale', 'w_conv', 'b_conv', 'w_a', 'b_a', 'w_x', 'b_x', 'lru_lambda', 'w_out', 'ln1_g', 'ln1_b',
        'w_group', 'b_group', 'w_route', 'b_route', 'w_gate', 'w_up', 'w_down', 'ln2_g', 'ln2_b']
_OUTS = [(1, SEQ, D), (DEC_B, DEC_T, D), (1, 1, PB, DH), (1, 1, CB, DH), (1, 1, DH),
         (1, DEC_B, PB, DH), (1, DEC_B, CB, DH), (1, DEC_B, DH)]


def kernel(**inputs):
    import numpy as _np
    import concourse.bacc as _bacc
    from concourse.bass_utils import run_bass_kernel_spmd as _run

    nc = _bacc.Bacc("TRN2", target_bir_lowering=False, num_devices=1)
    arrays, aps = {}, {}
    for name in _INS:
        a = _np.ascontiguousarray(inputs[name])
        arrays[f"in_{name}"] = a
        aps[name] = nc.dram_tensor(f"in_{name}", a.shape, mybir.dt.from_np(a.dtype), kind="ExternalInput").ap()
    for i, shape in enumerate(_OUTS):
        aps[f"out_{i}"] = nc.dram_tensor(f"result_{i}", shape, F32, kind="ExternalOutput").ap()
    build(nc, aps)
    r = _run(nc, [arrays], core_ids=[0])
    return tuple(r.results[0][f"result_{i}"] for i in range(len(_OUTS)))
```
